# Optimizing a Trainium2 kernel written in Bass

```python
import jax, jax.numpy as jnp
from jax import lax
import numpy as np

D_MODEL = 2048
BATCH = 1
SEQ = 512
DEPTH = 1

GLA_HEADS = 4
GLA_KEY_WIDTH = D_MODEL // 2
GLA_VAL_WIDTH = D_MODEL
GLA_DK = GLA_KEY_WIDTH // GLA_HEADS
GLA_DV = GLA_VAL_WIDTH // GLA_HEADS
GLA_GATE_RANK = 16
GLA_GATE_NORMALIZER = 16.0
GLA_CHUNK = 64
CONV_CHANNELS = D_MODEL
CONV_KERNEL = 31
PEER_HEADS = 8
PEER_N_KEYS = 128
PEER_N_EXPERTS = PEER_N_KEYS * PEER_N_KEYS
PEER_DKEY = 256
PEER_HALF = PEER_DKEY // 2
PEER_TOPK = 16
PEER_TOKEN_BLOCK = 128
EPS = 1e-6

IN_SIZES = (GLA_KEY_WIDTH, GLA_KEY_WIDTH, GLA_VAL_WIDTH, GLA_VAL_WIDTH,
            GLA_GATE_RANK, GLA_GATE_RANK, 2 * CONV_CHANNELS, D_MODEL, D_MODEL)
IN_WIDTH = 2 * GLA_KEY_WIDTH + 2 * GLA_VAL_WIDTH + 2 * GLA_GATE_RANK + 2 * CONV_CHANNELS + 2 * D_MODEL

kernel_name = "hybrid_gla_conformer_peer_encoder"

def _rmsnorm(x, g):
    xf = x.astype(jnp.float32)
    y = xf * lax.rsqrt(jnp.mean(xf * xf, axis=-1, keepdims=True) + EPS)
    return (y * g.astype(jnp.float32)).astype(x.dtype)

def _layernorm(x, g, b):
    xf = x.astype(jnp.float32)
    mu = jnp.mean(xf, axis=-1, keepdims=True)
    xc = xf - mu
    y = xc * lax.rsqrt(jnp.mean(xc * xc, axis=-1, keepdims=True) + EPS)
    return (y * g.astype(jnp.float32) + b.astype(jnp.float32)).astype(x.dtype)

def _to_heads(t, n_heads):
    B, S, W = t.shape
    return t.reshape(B, S, n_heads, W // n_heads).transpose(0, 2, 1, 3)

def _gla_scan(q, k, v, log_a, strict):
    B, H, S, dk = q.shape
    dv = v.shape[-1]
    nc = S // GLA_CHUNK

    def chunks(t):
        return jnp.moveaxis(t.reshape(B, H, nc, GLA_CHUNK, t.shape[-1]), 2, 0)

    mask = jnp.tril(jnp.ones((GLA_CHUNK, GLA_CHUNK), bool), -1 if strict else 0)[:, :, None]

    def step(state, inp):
        qc, kc, vc, gc = inp
        b = jnp.cumsum(gc.astype(jnp.float32), axis=2)
        inter = jnp.einsum('bhid,bhde->bhie', qc * jnp.exp(b), state)
        diff = b[:, :, :, None, :] - b[:, :, None, :, :]
        decay = jnp.where(mask, jnp.exp(jnp.where(mask, diff, 0.0)), 0.0)
        scores = jnp.einsum('bhid,bhjd,bhijd->bhij', qc, kc, decay)
        intra = jnp.einsum('bhij,bhje->bhie', scores, vc)
        b_last = b[:, :, -1:, :]
        new_state = (jnp.exp(b_last[:, :, 0, :])[..., None] * state
                     + jnp.einsum('bhjd,bhje->bhde', kc * jnp.exp(b_last - b), vc))
        return new_state, inter + intra

    state0 = jnp.zeros((B, H, dk, dv), jnp.float32)
    _, o = lax.scan(step, state0, (chunks(q), chunks(k), chunks(v), chunks(log_a)))
    return jnp.moveaxis(o, 0, 2).reshape(B, H, S, dv)

def _peer(h, w_q, keys, u_tab, v_tab):
    T, D = h.shape

    def block(hb):
        tb = hb.shape[0]
        q = (hb @ w_q).reshape(tb, PEER_HEADS, 2, PEER_HALF)
        s = jnp.einsum('thcd,hcnd->thcn', q, keys).astype(jnp.float32)
        s_top, i_top = lax.top_k(s, PEER_TOPK)
        cand_s = s_top[:, :, 0, :, None] + s_top[:, :, 1, None, :]
        cand_i = i_top[:, :, 0, :, None] * PEER_N_KEYS + i_top[:, :, 1, None, :]
        cand_s = cand_s.reshape(tb, PEER_HEADS, PEER_TOPK * PEER_TOPK)
        cand_i = cand_i.reshape(tb, PEER_HEADS, PEER_TOPK * PEER_TOPK)
        best_s, best_pos = lax.top_k(cand_s, PEER_TOPK)
        idx = jnp.take_along_axis(cand_i, best_pos, axis=-1)
        gate = jax.nn.softmax(best_s, axis=-1)
        u = jnp.take(u_tab, idx, axis=0)
        act = jax.nn.gelu(jnp.einsum('thkd,td->thk', u, hb).astype(jnp.float32), approximate=False)
        w = (gate * act).astype(hb.dtype)
        return jnp.einsum('thk,thkd->td', w, jnp.take(v_tab, idx, axis=0))

    out = lax.map(block, h.reshape(T // PEER_TOKEN_BLOCK, PEER_TOKEN_BLOCK, D))
    return out.reshape(T, D)

def setup_inputs(seed: int = 0) -> dict:
    key = jax.random.key(seed)
    ks = jax.random.split(key, 24)
    L, D = DEPTH, D_MODEL

    def nrm(k, shape, scale):
        return jax.random.normal(k, shape, jnp.float32) * scale

    return {
        "x": nrm(ks[0], (BATCH, SEQ, D), 1.0),
        "norm1_g": 1.0 + nrm(ks[1], (L, D), 0.02),
        "w_in": nrm(ks[2], (L, D, IN_WIDTH), D ** -0.5),
        "gla_gk_fwd_w": nrm(ks[3], (L, GLA_GATE_RANK, GLA_KEY_WIDTH), GLA_GATE_RANK ** -0.5),
        "gla_gk_fwd_b": nrm(ks[4], (L, GLA_KEY_WIDTH), 0.1),
        "gla_gk_bwd_w": nrm(ks[5], (L, GLA_GATE_RANK, GLA_KEY_WIDTH), GLA_GATE_RANK ** -0.5),
        "gla_gk_bwd_b": nrm(ks[6], (L, GLA_KEY_WIDTH), 0.1),
        "gla_onorm_g": 1.0 + nrm(ks[7], (L, GLA_HEADS, GLA_DV), 0.02),
        "gla_w_o": nrm(ks[8], (L, GLA_VAL_WIDTH, D), GLA_VAL_WIDTH ** -0.5),
        "conv_w": nrm(ks[9], (L, CONV_KERNEL, CONV_CHANNELS), CONV_KERNEL ** -0.5),
        "conv_b": nrm(ks[10], (L, CONV_CHANNELS), 0.01),
        "conv_ln_g": 1.0 + nrm(ks[11], (L, CONV_CHANNELS), 0.02),
        "conv_ln_b": nrm(ks[12], (L, CONV_CHANNELS), 0.01),
        "conv_w_pw2": nrm(ks[13], (L, CONV_CHANNELS, D), CONV_CHANNELS ** -0.5),
        "w_out": nrm(ks[14], (L, D, D), D ** -0.5),
        "norm2_g": 1.0 + nrm(ks[15], (L, D), 0.02),
        "peer_w_q": nrm(ks[16], (L, D, PEER_HEADS * PEER_DKEY), D ** -0.5),
        "peer_keys": nrm(ks[17], (L, PEER_HEADS, 2, PEER_N_KEYS, PEER_HALF), PEER_HALF ** -0.5),
        "peer_u": nrm(ks[18], (L, PEER_N_EXPERTS, D), D ** -0.5),
        "peer_v": nrm(ks[19], (L, PEER_N_EXPERTS, D), PEER_HEADS ** -0.5),
        "final_norm_g": 1.0 + nrm(ks[20], (D,), 0.02),
    }

def reference(x, norm1_g, w_in, gla_gk_fwd_w, gla_gk_fwd_b, gla_gk_bwd_w, gla_gk_bwd_b,
              gla_onorm_g, gla_w_o, conv_w, conv_b, conv_ln_g, conv_ln_b, conv_w_pw2, w_out,
              norm2_g, peer_w_q, peer_keys, peer_u, peer_v, final_norm_g):
    B, S, D = x.shape
    offsets = np.cumsum(IN_SIZES)[:-1].tolist()
    for l in range(DEPTH):
        h = _rmsnorm(x, norm1_g[l])
        proj = h @ w_in[l]
        q, k, v, og, gkf, gkb, glu, ga, gb = jnp.split(proj, offsets, axis=-1)

        qh = _to_heads(q, GLA_HEADS) * (GLA_DK ** -0.5)
        kh = _to_heads(k, GLA_HEADS)
        vh = _to_heads(v, GLA_HEADS)
        log_af = jax.nn.log_sigmoid((gkf @ gla_gk_fwd_w[l] + gla_gk_fwd_b[l]).astype(jnp.float32)) / GLA_GATE_NORMALIZER
        log_ab = jax.nn.log_sigmoid((gkb @ gla_gk_bwd_w[l] + gla_gk_bwd_b[l]).astype(jnp.float32)) / GLA_GATE_NORMALIZER
        o_f = _gla_scan(qh, kh, vh, _to_heads(log_af, GLA_HEADS), False)
        flip = lambda t: jnp.flip(t, axis=2)
        o_b = flip(_gla_scan(flip(qh), flip(kh), flip(vh), flip(_to_heads(log_ab, GLA_HEADS)), True))
        o = (o_f + o_b).transpose(0, 2, 1, 3)
        o = _rmsnorm(o, gla_onorm_g[l])
        o = (o * jax.nn.silu(og.reshape(B, S, GLA_HEADS, GLA_DV))).reshape(B, S, GLA_VAL_WIDTH).astype(x.dtype)
        y_a = o @ gla_w_o[l]

        a_in, a_gate = jnp.split(glu, 2, axis=-1)
        u = a_in * jax.nn.sigmoid(a_gate)
        u = lax.conv_general_dilated(u, conv_w[l][:, None, :], window_strides=(1,),
                                     padding=[(CONV_KERNEL // 2, CONV_KERNEL // 2)],
                                     dimension_numbers=('NWC', 'WIO', 'NWC'),
                                     feature_group_count=CONV_CHANNELS) + conv_b[l]
        u = jax.nn.silu(_layernorm(u, conv_ln_g[l], conv_ln_b[l]))
        y_b = u @ conv_w_pw2[l]

        merged = jax.nn.sigmoid(ga) * y_a + jax.nn.sigmoid(gb) * y_b
        x = x + merged @ w_out[l]

        h2 = _rmsnorm(x, norm2_g[l]).reshape(B * S, D)
        x = x + _peer(h2, peer_w_q[l], peer_keys[l], peer_u[l], peer_v[l]).reshape(B, S, D)
    return _rmsnorm(x, final_norm_g)


_drawn_inputs = setup_inputs


def setup_inputs(seed=0):
    import zlib

    import numpy as np

    out = dict(_drawn_inputs(seed))
    spreads = {}
    factors = {'gla_gk_fwd_b': 3.084,
     'gla_gk_bwd_b': 3.06,
     'gla_onorm_g': 46.358,
     'conv_b': 4.042,
     'conv_ln_g': 40.974,
     'conv_ln_b': 80.518,
     'final_norm_g': 23.715,
     'norm2_g': 15.858}
    for name, (base, spread) in spreads.items():
        noise = np.random.default_rng([zlib.crc32(name.encode()), seed]).standard_normal(out[name].shape)
        drawn = base * np.exp(spread * noise) if base else spread * noise
        out[name] = __import__('jax').numpy.asarray(drawn.astype(out[name].dtype))
    for name, factor in factors.items():
        out[name] = (out[name] * factor).astype(out[name].dtype)
    return out
```

```python
import concourse.bass as bass
from concourse import mybir
from contextlib import ExitStack

P = 128
F32 = mybir.dt.float32
U32 = mybir.dt.uint32
I32 = mybir.dt.int32
ALU = mybir.AluOpType
ACT = mybir.ActivationFunctionType
AX = mybir.AxisListType

D = 2048
T = 512
KT = D // P
NB = T // P
HEADS = 4
DK = 256
DV = 512
MT = DK // P
RANK = 16
TAPS = 31
PAD = TAPS // 2
EPS = 1e-6
PH = 8
NK = 128
TOP = 16
REF = P // 2
CLAMP = 16.0 * 80.0
LOW = -3.0e38

OQ, OK_, OV, OG = 0, 1024, 2048, 4096
OGK = 6144
OGLU = 6176
OGATE = OGLU + 2048
OGA = OGLU + 4096
OGB = OGA + 2048

R_N1, R_CB, R_LG, R_LB, R_CW = 0, 1, 2, 3, 4
R_GK = R_CW + TAPS
ROWS = R_GK + 1

HEAD_SLABS = 6
SB_HEAD = 0
SB_CONV = SB_HEAD + HEADS * HEAD_SLABS
SB_MA = SB_CONV + KT
SB_MB = SB_MA + KT
SB_OUT = SB_MB + KT
SB_WQ = SB_OUT + 8
SLAB = 4096
UNITS = NB * PH
SLOTS = 4


class Chain:

    def __init__(self, eng, sem):
        self.eng, self.sem, self.n = eng, sem, 0

    def enter(self):
        self.start = self.n

    def leave(self):
        self.wait()
        self.eng.sem_inc(self.sem, self.start - self.n)
        self.n = self.start

    def mark(self, ins):
        self.n += 1
        ins.then_inc(self.sem, 1)

    def wait(self):
        self.eng.wait_ge(self.sem, self.n)

    def step(self, ins):
        self.mark(ins)
        self.wait()


def hold(eng, sem, value, passed):
    eng.wait_ge(sem, value)
    eng.sem_inc(passed, 1)


def hybrid_block(nc, x, norm1_g, w_in, gk_f_w, gk_f_b, gk_b_w, gk_b_b, onorm_g, w_o, conv_w, conv_b,
                 ln_g, ln_b, w_pw2, w_out, norm2_g, w_q, keys, u_tab, v_tab, final_g, out):
    def slabs(w, half):
        w2 = w[0]
        if half:
            return w2.rearrange("(s k p) n -> s p k n", p=P, s=2)
        return w2.rearrange("(k p) n -> p k n", p=P)

    ctx = ExitStack()
    with ctx:
        def sb(name, shape, dt=F32):
            return ctx.enter_context(nc.sbuf_tensor(name, shape, dt))

        def sem(name):
            return ctx.enter_context(nc.semaphore(name))

        def view(t, off, *shape):
            n = 1
            for s in shape:
                n *= s
            a = t[:, off:off + n]
            if len(shape) == 2:
                a = a.rearrange("p (a b) -> p a b", b=shape[1])
            elif len(shape) == 3:
                a = a.rearrange("p (a b c) -> p a b c", b=shape[1], c=shape[2])
            return a

        arena_a = sb("arena_a", [P, KT * T])
        arena_b = sb("arena_b", [P, KT * T])
        arena_c = sb("arena_c", [P, 21504])
        wring = sb("wring", [P, 2 * SLAB])
        gbc = sb("gbc", [P, D])
        ident = sb("ident", [P, P])
        ones_d = sb("ones_d", [P, P])
        causal = sb("causal", [P, P])
        reset = sb("reset", [P, T])
        iota_i = sb("iota_i", [P, TOP], I32)
        iota16 = sb("iota16", [P, TOP])
        cols = sb("cols", [P, KT, ROWS])
        small = sb("small", [P, 64])
        gkw = sb("gkw", [RANK, 2, DK])
        glow = sb("glow", [RANK, 2, T])

        hT = view(arena_a, 0, KT, T)
        x2 = view(arena_a, 0, NB, D)
        oT = view(arena_b, 0, KT, T)
        h2 = view(arena_b, 0, NB, D)
        xb = view(arena_c, 0, NB, D)
        sq_x = view(arena_c, 8192, D)
        rows = arena_c[0:ROWS, 10240:10240 + D]
        wgk = view(arena_c, 12800, KT, 2 * RANK)
        o_ = [0]

        def take(*shape):
            n = 1
            for s in shape:
                n *= s
            a = view(arena_c, o_[0], *shape)
            o_[0] += n
            return a

        qT = take(MT, T)
        kT = take(MT, T)
        v_tok = take(NB, DV)
        og_s = take(NB, DV)
        qm = take(2, MT, T)
        km = take(2, MT, T)
        kmT = take(NB, 2, DK)
        st_b = take(3, MT, DV)
        st_f = take(2, MT, DV)
        t_abs = take(T)
        t_l = take(T)
        t_b = take(T)
        t_d = take(T)
        t_e = take(T)
        on = take(2, DV)
        p_t = take(2, P)
        dec = view(arena_c, o_[0], 4, 4)
        o_[0] += 16
        dif = view(arena_c, o_[0], 4)
        o_[0] += 4
        assert o_[0] <= 21504
        cv = view(arena_c, 0, KT, T)
        mg = view(arena_c, 8192, KT, T)
        upad = view(arena_c, 16384, 2, T + 2 * PAD)
        sig = view(arena_c, 17480, 2, T)
        sqr = view(arena_c, 18504, 2, T)
        mtmp = view(arena_c, 19528, T)
        rstd_ln = view(arena_c, 16384, T)
        h2T = view(arena_c, 0, KT, T)
        keysT = view(arena_c, 8192, 2 * PH, NK)
        keys_n = view(arena_c, 10240, 2 * PH, NK)
        sq_x2 = view(arena_c, 10240, D)
        qh = view(arena_c, 12288, 2, T)
        s_sb = view(arena_c, 13312, 2, 2, NB * NK)
        s_rep = view(arena_c, 15360, NK)
        vals = view(arena_c, 15488, NB * 2, TOP)
        cand = view(arena_c, 15616, TOP * TOP)
        cand2 = view(arena_c, 15872, TOP * TOP)
        best = view(arena_c, 16128, NB, TOP)
        onehot = view(arena_c, 16192, TOP, TOP)
        picked = view(arena_c, 16448, TOP, TOP)
        pa = view(arena_c, 16704, NB, TOP)
        pb = view(arena_c, 16768, NB, TOP)
        ia = view(arena_c, 16832, NB, TOP)
        ib = view(arena_c, 16896, NB, TOP)
        idxf = view(arena_c, 16960, NB * 2, TOP)
        ee = view(arena_c, 17088, NB, TOP)
        es = view(arena_c, 17152, NB)
        idx_u = view(arena_c, 17160, NB * 2, TOP).bitcast(U32)
        pos_u = view(arena_c, 17288, NB, TOP).bitcast(U32)
        pos_a = view(arena_c, 17352, NB, TOP).bitcast(U32)
        pos_b = view(arena_c, 17416, NB, TOP).bitcast(U32)
        u_row = [view(arena_c, s * D, D) for s in range(SLOTS)]
        v_row = [view(arena_c, (SLOTS + s) * D, D) for s in range(SLOTS)]
        diag = view(arena_c, 2 * SLOTS * D, SLOTS, P)
        act_u = view(arena_c, 2 * SLOTS * D + 512, 2, TOP)
        act_g = view(arena_c, 2 * SLOTS * D + 544, 2, TOP)
        act_w = view(arena_c, 2 * SLOTS * D + 576, 2, TOP)
        gate_cur = view(arena_c, 2 * SLOTS * D + 608, 2, TOP)
        idx_cur = view(arena_c, 2 * SLOTS * D + 640, 2, TOP).bitcast(U32)
        idx_all = sb("idx_all", [P, NB * PH + 1, TOP], U32)
        gate_all = sb("gate_all", [P, NB * PH + 1, TOP])

        ps = [ctx.enter_context(nc.psum_tensor(f"bank{n}", [P, 512], F32)) for n in range(8)]

        const_step = sem("const_step")
        consts = sem("consts")
        x_in = [sem(f"x_in{b}") for b in range(NB)]
        rows_in = sem("rows_in")
        cols_tr = sem("cols_tr")
        cols_done = sem("cols_done")
        small_in = sem("small_in")
        gkw_in = sem("gkw_in")
        gbc_in = sem("gbc_in")
        wgk_in = sem("wgk_in")
        w_in_slot = [sem("w_slot0"), sem("w_slot1")]
        w_used = sem("w_used")
        dve_chain = sem("dve_chain")
        sp_passed = sem("sp_passed")
        pool_passed = sem("pool_passed")
        dve_passed = sem("dve_passed")
        n1_sum = sem("n1_sum")
        n1_ms = sem("n1_ms")
        n1_root = sem("n1_root")
        n1_xn = sem("n1_xn")
        n1_tr = sem("n1_tr")
        n1_done = sem("n1_done")
        glow_mm = sem("glow_mm")
        glow_done = sem("glow_done")
        q_mm = sem("q_mm")
        q_ev = sem("q_ev")
        z_mm = sem("z_mm")
        z_exp = sem("z_exp")
        z_ln = sem("z_ln")
        z_dif = sem("z_dif")
        z_dec = sem("z_dec")
        z_qk = sem("z_qk")
        v_mm = sem("v_mm")
        v_ev = sem("v_ev")
        og_mm = sem("og_mm")
        og_ev = sem("og_ev")
        og_scaled = sem("og_scaled")
        kt_tr = sem("kt_tr")
        kt_ev = sem("kt_ev")
        ub_mm = sem("ub_mm")
        ub_done = sem("ub_done")
        uf_mm = sem("uf_mm")
        uf_done = sem("uf_done")
        sc_mm = sem("sc_mm")
        sc_done = sem("sc_done")
        o_mm = sem("o_mm")
        o_sum = sem("o_sum")
        o_ms = sem("o_ms")
        o_root = sem("o_root")
        o_norm = sem("o_norm")
        ot_tr = sem("ot_tr")
        ot_ev = sem("ot_ev")
        pair = {}
        for name in ("cv", "ma", "mb"):
            pair[name] = dict(gate=sem(name + "_gate"), sig=sem(name + "_sig"), val=sem(name + "_val"),
                              use=sem(name + "_use"))
        cv_done = sem("cv_done")
        ln_sum = sem("ln_sum")
        ln_xc = sem("ln_xc")
        ln_sq = sem("ln_sq")
        ln_varu = sem("ln_varu")
        ln_ms = sem("ln_ms")
        ln_root = sem("ln_root")
        ln_scaled = sem("ln_scaled")
        ln_act = sem("ln_act")
        mb_done = sem("mb_done")
        res_in = sem("res_in")
        out_mm = sem("out_mm")
        out_free = sem("out_free")
        n2_sum = sem("n2_sum")
        n2_ms = sem("n2_ms")
        n2_root = sem("n2_root")
        n2_h = sem("n2_h")
        n2_tr = sem("n2_tr")
        n2_ev = sem("n2_ev")
        keys_in = sem("keys_in")
        keys_tr = sem("keys_tr")
        keys_ev = sem("keys_ev")
        pq_mm = sem("pq_mm")
        pq_ev = sem("pq_ev")
        s_mm = sem("s_mm")
        s_ev = sem("s_ev")
        sm_in = sem("sm_in")
        sm_exp = sem("sm_exp")
        s_free = sem("s_free")
        idx_ready = sem("idx_ready")
        gate_step = sem("gate_step")
        u_ready = [sem(f"u_ready{s}") for s in range(SLOTS)]
        v_ready = [sem(f"v_ready{s}") for s in range(SLOTS)]
        u_used = sem("u_used")
        act_done = sem("act_done")
        diag_ready = sem("diag_ready")
        v_used = sem("v_used")
        mix_free = sem("mix_free")
        fin_sum = sem("fin_sum")
        fin_ms = sem("fin_ms")
        fin_root = sem("fin_root")
        fin_y = sem("fin_y")
        out_done = sem("out_done")

        block = ctx.enter_context(nc.Block())
        x_d = x[0].rearrange("(b p) d -> b p d", p=P)
        out_d = out[0].rearrange("(b p) d -> b p d", p=P)

        def w_slot(n):
            return view(wring, (n % 2) * SLAB, KT, 256)

        def w_slot_half(n):
            return view(wring, (n % 2) * SLAB, KT // 2, 512)

        @block.sync
        def _(sp):
            for b in range(NB):
                sp.dma_start(xb[:, b, :], x_d[b]).then_inc(x_in[b], 16)
            sp.dma_start(wgk, slabs(w_in, False)[:, :, OGK:OGK + 2 * RANK]).then_inc(wgk_in, 16)

            def load(n, i, per, dst, src):
                hold(sp, w_used, i * per + (n + 1), sp_passed)
                sp.dma_start(dst, src).then_inc(w_in_slot[n % 2], 16)

            full, half = slabs(w_in, False), slabs(w_in, True)
            with sp.Fori(0, HEADS) as h:
                load(0, h, HEAD_SLABS, w_slot(0), full[:, :, bass.ds(h * DK + OQ, DK)])
                load(1, h, HEAD_SLABS, w_slot(1), full[:, :, bass.ds(h * DK + OK_, DK)])
                for s in range(2):
                    load(2 + s, h, HEAD_SLABS, w_slot_half(s), half[s][:, :, bass.ds(h * DV + OV, DV)])
                for s in range(2):
                    load(4 + s, h, HEAD_SLABS, w_slot_half(s), half[s][:, :, bass.ds(h * DV + OG, DV)])

            def pair_loads(first, w_gate, o_gate, w_val, o_val):
                with sp.Fori(0, KT // 2) as i:
                    load(first, i, 2, w_slot(0), slabs(w_gate, False)[:, :, bass.ds(i * 256 + o_gate, 256)])
                    load(first + 1, i, 2, w_slot(1), slabs(w_val, False)[:, :, bass.ds(i * 256 + o_val, 256)])

            pair_loads(SB_CONV, w_in, OGATE, w_in, OGLU)
            pair_loads(SB_MA, w_in, OGA, w_o, 0)
            pair_loads(SB_MB, w_in, OGB, w_pw2, 0)
            sp.wait_ge(w_used, SB_OUT + 2)
            for b in range(NB):
                sp.dma_start(x2[:, b, :], x_d[b]).then_inc(res_in, 16)
            with sp.Fori(0, 4) as i:
                for s in range(2):
                    load(SB_OUT + s, i, 2, w_slot_half(s), slabs(w_out, True)[s][:, :, bass.ds(i * 512, 512)])
            with sp.Fori(0, PH // 2) as i:
                for s in range(2):
                    load(SB_WQ + s, i, 2, w_slot(s), slabs(w_q, False)[:, :, bass.ds(i * 512 + s * 256, 256)])
            for b in range(NB):
                sp.wait_ge(fin_y, b + 1)
                sp.dma_start(out_d[b], x2[:, b, :]).then_inc(out_done, 16)
            sp.wait_ge(out_done, 16 * NB)

        @block.gpsimd
        def _(pool):
            G = nc.gpsimd
            G.memset(ident[:], 0.0).then_inc(const_step, 1)
            pool.wait_ge(const_step, 1)
            G.affine_select(out=ident[:], in_=ident[:], compare_op=ALU.not_equal, fill=1.0, base=0,
                            pattern=[[-1, P]], channel_multiplier=1).then_inc(consts, 1)
            G.memset(ones_d[:], 1.0 / D).then_inc(consts, 1)
            G.memset(causal[:], 1.0).then_inc(const_step, 1)
            pool.wait_ge(const_step, 2)
            G.affine_select(out=causal[:], in_=causal[:], compare_op=ALU.is_ge, fill=0.0, base=0,
                            pattern=[[1, P]], channel_multiplier=-1).then_inc(consts, 1)
            G.memset(reset[:], 1.0).then_inc(const_step, 1)
            pool.wait_ge(const_step, 3)
            G.memset(reset[:].rearrange("p (c t) -> p c t", t=P)[:, :, 0:1], 0.0).then_inc(consts, 1)
            G.iota(iota_i[:], pattern=[[1, TOP]], base=0, channel_multiplier=0).then_inc(const_step, 1)
            pool.wait_ge(const_step, 4)
            G.tensor_copy(iota16[:], iota_i[:]).then_inc(consts, 1)

            with pool.Fori(0, UNITS // 2) as i:
                for m in range(2):
                    hold(pool, idx_ready, i * 2 + (m + 1), pool_passed)
                    for k in range(TOP):
                        n = m * TOP + k
                        s = n % SLOTS
                        idx = bass.IndirectOffsetOnAxis(ap=idx_cur[:, m, k:k + 1], axis=0)
                        hold(pool, u_used, i * 2 * TOP + (n + 1), pool_passed)
                        pool.indirect_dma_start(out=u_row[s], out_offset=None, in_=u_tab[0], in_offset=idx)\
                            .then_inc(u_ready[s], 16)
                        hold(pool, v_used, i * 2 * TOP + (n + 1), pool_passed)
                        pool.indirect_dma_start(out=v_row[s], out_offset=None, in_=v_tab[0], in_offset=idx)\
                            .then_inc(v_ready[s], 16)

        @block.scalar
        def _(act):
            A = nc.scalar.activation
            for src, r in ((norm1_g, R_N1), (conv_b, R_CB), (ln_g, R_LG), (ln_b, R_LB)):
                act.dma_start(rows[r:r + 1, :], src).then_inc(rows_in, 16)
            act.dma_start(rows[R_CW:R_CW + TAPS, :], conv_w[0]).then_inc(rows_in, 16)
            act.dma_start(rows[R_GK:R_GK + 1, 0:1024], gk_f_b).then_inc(rows_in, 16)
            act.dma_start(rows[R_GK:R_GK + 1, 1024:2048], gk_b_b).then_inc(rows_in, 16)
            act.dma_start(gbc[:], onorm_g.rearrange("a h e -> a (h e)").broadcast_to([P, D])).then_inc(gbc_in, 16)

            for b in range(NB):
                act.wait_ge(x_in[b], 16)
                A(sq_x, xb[:, b, :], ACT.Square, accum_out=small[:, b:b + 1]).then_inc(n1_sum, 1)
                act.wait_ge(n1_sum, b + 1)
            for b in range(NB):
                act.wait_ge(n1_ms, b + 1)
                A(small[:, 8 + b:9 + b], small[:, 4 + b:5 + b], ACT.Sqrt).then_inc(n1_root, 1)

            for d in range(2):
                act.wait_ge(glow_mm, d + 1)
                A(glow[:, d, :], ps[d][0:RANK, :], ACT.Copy).then_inc(glow_done, 1)

            with act.Fori(0, HEADS) as h:
                act.dma_start(gkw[:, 0, :], gk_f_w[0][:, bass.ds(h * DK, DK)]).then_inc(gkw_in, 16)
                act.dma_start(gkw[:, 1, :], gk_b_w[0][:, bass.ds(h * DK, DK)]).then_inc(gkw_in, 16)
                for n in range(4):
                    act.wait_ge(q_mm, h * 4 + (n + 1))
                    dst = qT[:, n, :] if n < 2 else kT[:, n - 2, :]
                    A(dst, ps[n][:], ACT.Copy, scale=DK ** -0.5 if n < 2 else 1.0).then_inc(q_ev, 1)
                for u in range(4):
                    fwd = u < 2
                    act.wait_ge(z_mm, h * 4 + (u + 1))
                    bias = cols[:, bass.ds(h * MT + (8 * (u // 2) + u % 2), 1), R_GK]
                    A(t_abs, ps[4 + u][:], ACT.Abs, bias=bias).then_inc(z_exp, 1)
                    act.wait_ge(z_exp, h * 8 + (2 * u + 1))
                    A(t_abs, t_abs, ACT.Exp, scale=-1.0).then_inc(z_exp, 1)
                    act.wait_ge(z_exp, h * 8 + (2 * u + 2))
                    A(t_abs, t_abs, ACT.Ln, bias=1.0).then_inc(z_ln, 1)
                    act.wait_ge(z_dif, h * 4 + (u + 1))
                    A(t_e, t_d, ACT.Exp, scale=1.0 / 16 if fwd else -1.0 / 16).then_inc(z_dec, 1)
                    A(dec[:, u, 0:3], dif[:, 0:3], ACT.Exp, scale=1.0 / 16).then_inc(z_dec, 1)
                    act.wait_ge(z_dec, h * 12 + (3 * u + 2))
                    A(t_d, t_d, ACT.Exp, scale=-1.0 / 16 if fwd else 1.0 / 16).then_inc(z_dec, 1)
                    act.wait_ge(z_qk, h * 4 + (u + 1))
                for b in range(NB):
                    act.wait_ge(v_mm, h * 4 + (b + 1))
                    A(v_tok[:, b, :], ps[b][:], ACT.Copy).then_inc(v_ev, 1)
                for b in range(NB):
                    act.wait_ge(og_mm, h * 4 + (b + 1))
                    A(og_s[:, b, :], ps[4 + b][:], ACT.Silu).then_inc(og_ev, 1)
                for n in range(4):
                    act.wait_ge(kt_tr, h * 4 + (n + 1))
                    A(kmT[:, :, n // 2, (n % 2) * P:(n % 2) * P + P],
                      ps[n][:].rearrange("p (c f) -> p c f", f=P), ACT.Copy).then_inc(kt_ev, 1)

                def ot_out(c):
                    act.wait_ge(ot_tr, h * 4 + (c + 1))
                    A(oT[:, bass.ds(h * 4, 4), c * P:c * P + P],
                      ps[2 + c % 2][:].rearrange("p (m t) -> p m t", t=P), ACT.Copy).then_inc(ot_ev, 1)

                for c in range(NB):
                    act.wait_ge(o_mm, h * 4 + (c + 1))
                    if c:
                        act.wait_ge(o_sum, h * 4 + c)
                    A(t_abs, ps[6 + c % 2][:], ACT.Square, accum_out=small[:, 16 + c:17 + c]).then_inc(o_sum, 1)
                    act.wait_ge(o_ms, h * 4 + (c + 1))
                    A(small[:, 24 + c:25 + c], small[:, 20 + c:21 + c], ACT.Sqrt).then_inc(o_root, 1)
                    if c:
                        ot_out(c - 1)
                ot_out(NB - 1)

            def gates(name, start, end):
                p = pair[name]
                with act.Fori(start, end) as i:
                    for m in range(2):
                        act.wait_ge(p["gate"], i * 2 + (m + 1))
                        act.wait_ge(p["use"], i * 2 + (m + 1))
                        A(sig[:, m, :], ps[m][:], ACT.Sigmoid).then_inc(p["sig"], 1)

            gates("cv", 0, KT // 2)
            gates("ma", 0, KT // 4)
            gates("ma", KT // 4, KT // 2)
            for t in range(KT):
                act.wait_ge(ln_xc, t + 1)
                if t >= 2:
                    act.wait_ge(ln_varu, t - 1)
                A(sqr[:, t % 2, :], cv[:, t, :], ACT.Square).then_inc(ln_sq, 1)
            act.wait_ge(ln_ms, 1)
            A(mtmp, rstd_ln, ACT.Sqrt).then_inc(ln_root, 1)
            for t in range(KT):
                act.wait_ge(ln_scaled, t + 1)
                A(cv[:, t, :], cv[:, t, :], ACT.Silu, bias=cols[:, t, R_LB:R_LB + 1],
                  scale=cols[:, t, R_LG:R_LG + 1]).then_inc(ln_act, 1)
            gates("mb", 0, KT // 2)

            act.wait_ge(out_free, 8 + NB * 4)
            act.dma_start(gbc[:], norm2_g.broadcast_to([P, D])).then_inc(gbc_in, 16)
            for b in range(NB):
                A(sq_x2, x2[:, b, :], ACT.Square, accum_out=small[:, 32 + b:33 + b]).then_inc(n2_sum, 1)
                act.wait_ge(n2_sum, b + 1)
            act.dma_start(keys_n, keys[0].rearrange("h c n d -> n (h c) d")).then_inc(keys_in, 16)
            for b in range(NB):
                act.wait_ge(n2_ms, b + 1)
                A(small[:, 40 + b:41 + b], small[:, 36 + b:37 + b], ACT.Sqrt).then_inc(n2_root, 1)
            for b in range(NB):
                for g in range(4):
                    n = b * 4 + g
                    act.wait_ge(n2_tr, n + 1)
                    A(h2T[:, 4 * g:4 * g + 4, b * P:b * P + P],
                      ps[n % 8][:].rearrange("p (k t) -> p k t", t=P), ACT.Copy).then_inc(n2_ev, 1)
            for g in range(4):
                act.wait_ge(keys_tr, g + 1)
                A(keysT[:, 4 * g:4 * g + 4, :], ps[g][:].rearrange("p (k t) -> p k t", t=P),
                  ACT.Copy).then_inc(keys_ev, 1)
            act.dma_start(gbc[:], final_g.rearrange("(a d) -> a d", a=1).broadcast_to([P, D])).then_inc(gbc_in, 16)

            with act.Fori(0, PH // 2) as i:
                for m in range(2):
                    for c in range(2):
                        act.wait_ge(pq_mm, i * 4 + (2 * m + c + 1))
                        A(qh[:, c, :], ps[4 * m + c][:], ACT.Copy).then_inc(pq_ev, 1)
                    act.wait_ge(s_free, i * 2 + (m + 1))
                    for c in range(2):
                        act.wait_ge(s_mm, i * 4 + (2 * m + c + 1))
                        A(s_sb[:, m, c, :], ps[4 * m + 2 + c][:], ACT.Copy).then_inc(s_ev, 1)
                    act.wait_ge(sm_in, i * 2 + (m + 1))
                    A(ee, ee, ACT.Exp).then_inc(sm_exp, 1)

            with act.Fori(0, UNITS // 2) as i:
                for n in range(2 * TOP):
                    m, k = n // TOP, n % TOP
                    one = slice(k, k + 1)
                    act.wait_ge(u_used, i * 2 * TOP + (n + 1 + SLOTS))
                    A(act_g[:, m, one], act_u[:, m, one], ACT.Gelu).then_inc(act_done, 1)
                    act.wait_ge(act_done, i * 4 * TOP + (2 * n + 1))
                    A(act_w[:, m, one], act_g[:, m, one], ACT.Copy, scale=gate_cur[:, m, one]).then_inc(act_done, 1)
                    act.wait_ge(act_done, i * 4 * TOP + (2 * n + 2))
                    act.wait_ge(v_used, i * 2 * TOP + (n + 1))
                    A(diag[:, n % SLOTS, :], ident[:], ACT.Copy, scale=act_w[:, m, one]).then_inc(diag_ready, 1)

            act.wait_ge(mix_free, UNITS + 2)
            for b in range(NB):
                A(u_row[0], x2[:, b, :], ACT.Square, accum_out=small[:, 48 + b:49 + b]).then_inc(fin_sum, 1)
                act.wait_ge(fin_sum, b + 1)
            for b in range(NB):
                act.wait_ge(fin_ms, b + 1)
                A(small[:, 56 + b:57 + b], small[:, 52 + b:53 + b], ACT.Sqrt).then_inc(fin_root, 1)

        @block.vector
        def _(dve):
            V = nc.vector
            chain = Chain(dve, dve_chain)

            def mean_square(dst, src, n):
                return V.tensor_scalar(small[:, dst:dst + 1], small[:, src:src + 1], 1.0 / n, EPS, ALU.mult, ALU.add)

            def inverse(dst, src):
                return V.reciprocal(small[:, dst:dst + 1], small[:, src:src + 1])

            for p in pair.values():
                dve.sem_inc(p["use"], 2)
            dve.sem_inc(s_free, 2)
            dve.sem_inc(mix_free, 2)
            dve.sem_inc(u_used, SLOTS)
            dve.sem_inc(out_free, 8)

            for g in range(2):
                dve.wait_ge(cols_tr, g + 1)
                V.tensor_copy(cols[:, 8 * g:8 * g + 8, :],
                              ps[g][:].rearrange("p (k r) -> p k r", r=64)[:, :, 0:ROWS]).then_inc(cols_done, 1)
            for b in range(NB):
                dve.wait_ge(n1_sum, b + 1)
                mean_square(4 + b, b, D).then_inc(n1_ms, 1)
            for b in range(NB):
                dve.wait_ge(n1_root, b + 1)
                chain.step(inverse(12 + b, 8 + b))
                V.tensor_scalar(xb[:, b, :], xb[:, b, :], small[:, 12 + b:13 + b], None, ALU.mult)\
                    .then_inc(n1_xn, 1)
            dve.wait_ge(cols_done, 2)
            for b in range(NB):
                for g in range(4):
                    n = b * 4 + g
                    dve.wait_ge(n1_tr, n + 1)
                    gain = cols[:, 4 * g:4 * g + 4, R_N1:R_N1 + 1].broadcast_to([P, 4, P])
                    V.tensor_tensor(hT[:, 4 * g:4 * g + 4, b * P:b * P + P],
                                    ps[n % 8][:].rearrange("p (k t) -> p k t", t=P), gain, ALU.mult)\
                        .then_inc(n1_done, 1)
            dve.wait_ge(consts, 5)
            dve.wait_ge(gbc_in, 16)

            with dve.Fori(0, HEADS) as h:
                chain.enter()
                for u in range(4):
                    d, m = u // 2, u % 2
                    bias = cols[:, bass.ds(h * MT + (8 * d + m), 1), R_GK]
                    dve.wait_ge(z_exp, h * 8 + (2 * u + 1))
                    chain.step(V.tensor_scalar(t_l, ps[4 + u][:], bias, 0.0, ALU.add, ALU.min))
                    dve.wait_ge(z_ln, h * 4 + (u + 1))
                    chain.step(V.tensor_tensor(t_l, t_l, t_abs, ALU.subtract))
                    chain.step(V.tensor_tensor_scan(t_b, reset[:], t_l, 0.0, ALU.mult, ALU.add))
                    b3 = t_b.rearrange("p (c t) -> p c t", t=P)
                    src = b3
                    if d:
                        chain.step(V.tensor_tensor(t_l, t_b, t_l, ALU.subtract))
                        src = t_l.rearrange("p (c t) -> p c t", t=P)
                    ref = src[:, :, REF]
                    chain.mark(V.tensor_tensor(t_d.rearrange("p (c t) -> p c t", t=P), src,
                                               src[:, :, REF:REF + 1].broadcast_to([P, NB, P]), ALU.subtract))
                    chain.step(V.tensor_tensor(dif, b3[:, :, P - 1], ref, ALU.subtract))
                    chain.step(V.tensor_tensor(dif[:, 0:3], dif[:, 0:3], src[:, 1:4, REF], ALU.add))
                    V.tensor_scalar(t_d, t_d, CLAMP, -CLAMP, ALU.min, ALU.max).then_inc(z_dif, 1)
                    dve.wait_ge(z_dec, h * 12 + (3 * u + 3))
                    dve.wait_ge(q_ev, h * 4 + 4)
                    chain.mark(V.tensor_tensor(qm[:, d, m, :], qT[:, m, :], t_e, ALU.mult))
                    chain.wait()
                    V.tensor_tensor(km[:, d, m, :], kT[:, m, :], t_d, ALU.mult).then_inc(z_qk, 1)
                for b in range(NB):
                    dve.wait_ge(og_ev, h * 4 + (b + 1))
                    V.tensor_tensor(og_s[:, b, :], og_s[:, b, :], gbc[:, bass.ds(h * DV, DV)], ALU.mult)\
                        .then_inc(og_scaled, 1)
                for j, c in enumerate((3, 2, 1)):
                    for m in range(MT):
                        dve.wait_ge(ub_mm, h * 6 + (2 * j + m + 1))
                        bank = ps[2 * (j % 2) + m][:]
                        if c < 3:
                            dve.wait_ge(ub_done, h * 6 + (2 * j - 1 + m))
                            chain.step(V.tensor_tensor(st_b[:, c - 1, m, :], bank, st_b[:, c, m, :], ALU.add))
                            bank = st_b[:, c - 1, m, :]
                        V.tensor_scalar(st_b[:, c - 1, m, :], bank, dec[:, 2 + m, c - 1:c], None, ALU.mult)\
                            .then_inc(ub_done, 1)

                def merge_scores(c):
                    dve.wait_ge(sc_mm, h * 4 + (c + 1))
                    if c >= 2:
                        dve.wait_ge(o_mm, h * 4 + (c - 1))
                    bank = ps[4 + c % 2]
                    chain.step(V.tensor_copy(p_t[:, c % 2, :], bank[:, P:2 * P]))
                    V.copy_predicated(p_t[:, c % 2, :], causal[:].bitcast(U32), bank[:, 0:P]).then_inc(sc_done, 1)

                merge_scores(0)
                for c in range(NB):
                    if c < NB - 1:
                        merge_scores(c + 1)
                        for m in range(MT):
                            dve.wait_ge(uf_mm, h * 6 + (2 * c + m + 1))
                            new = st_f[:, (c + 1) % 2, m, :]
                            bank = ps[m][:]
                            if c >= 1:
                                dve.wait_ge(uf_done, h * 6 + (2 * c - 1 + m))
                                if c >= 2:
                                    dve.wait_ge(o_mm, h * 4 + c)
                                chain.step(V.tensor_tensor(new, bank, st_f[:, c % 2, m, :], ALU.add))
                                bank = new
                            V.tensor_scalar(new, bank, dec[:, m, c:c + 1], None, ALU.mult).then_inc(uf_done, 1)
                    dve.wait_ge(o_sum, h * 4 + (c + 1))
                    mean_square(20 + c, 16 + c, DV).then_inc(o_ms, 1)
                    dve.wait_ge(o_root, h * 4 + (c + 1))
                    chain.step(inverse(28 + c, 24 + c))
                    if c >= 2:
                        dve.wait_ge(ot_tr, h * 4 + (c - 1))
                    V.scalar_tensor_tensor(on[:, c % 2, :], ps[6 + c % 2][:], small[:, 28 + c:29 + c],
                                           og_s[:, c, :], ALU.mult, ALU.mult).then_inc(o_norm, 1)
                chain.leave()

            chain.step(V.memset(upad, 0.0))
            with dve.Fori(0, KT // 2) as i:
                chain.enter()
                p = pair["cv"]
                for m in range(2):
                    dve.wait_ge(p["val"], i * 2 + (m + 1))
                    dve.wait_ge(p["sig"], i * 2 + (m + 1))
                    V.tensor_tensor(upad[:, m, PAD:PAD + T], ps[2 + m][:], sig[:, m, :], ALU.mult)\
                        .then_inc(p["use"], 1)
                    dve.wait_ge(p["use"], i * 2 + (m + 3))
                    dst = cv[:, bass.ds(i * 2 + m, 1), :].rearrange("p a t -> p (a t)")

                    def tap(r):
                        return cols[:, bass.ds(i * 2 + m, 1), r]

                    chain.step(V.tensor_scalar(dst, upad[:, m, 0:T], tap(R_CW), tap(R_CB), ALU.mult, ALU.add))
                    for r in range(1, TAPS):
                        ins = V.scalar_tensor_tensor(dst, upad[:, m, r:r + T], tap(R_CW + r), dst, ALU.mult, ALU.add)
                        if r < TAPS - 1:
                            chain.step(ins)
                    ins.then_inc(cv_done, 1)
                chain.leave()
            dve.wait_ge(cv_done, KT)

            def merge(name, start, end):
                p = pair[name]
                last = name == "mb"
                with dve.Fori(start, end) as i:
                    for m in range(2):
                        dst = mg[:, bass.ds(i * 2 + m, 1), :].rearrange("p a t -> p (a t)")
                        dve.wait_ge(p["val"], i * 2 + (m + 1))
                        dve.wait_ge(p["sig"], i * 2 + (m + 1))
                        V.tensor_tensor(mtmp if last else dst, ps[2 + m][:], sig[:, m, :], ALU.mult)\
                            .then_inc(p["use"], 1)
                        dve.wait_ge(p["use"], i * 2 + (m + 3))
                        if last:
                            V.tensor_tensor(dst, mtmp, dst, ALU.add).then_inc(mb_done, 1)
                            dve.wait_ge(mb_done, i * 2 + (m + 1))

            merge("ma", 0, KT // 4)
            dve.wait_ge(ln_sum, 1)
            for t in range(KT):
                V.tensor_tensor(cv[:, t, :], cv[:, t, :], ps[4][:], ALU.subtract).then_inc(ln_xc, 1)
            merge("ma", KT // 4, KT // 2)
            dve.wait_ge(ln_varu, KT)
            V.tensor_scalar(rstd_ln, ps[5][:], EPS, None, ALU.add).then_inc(ln_ms, 1)
            dve.wait_ge(ln_root, 1)
            chain.step(V.reciprocal(rstd_ln, mtmp))
            for t in range(KT):
                V.tensor_tensor(cv[:, t, :], cv[:, t, :], rstd_ln, ALU.mult).then_inc(ln_scaled, 1)
            merge("mb", 0, KT // 2)
            dve.wait_ge(res_in, 16 * NB)
            with dve.Fori(0, 2) as i:
                for g in range(2):
                    for b in range(NB):
                        dve.wait_ge(out_mm, i * 8 + (4 * g + b + 1))
                        dst = x2[:, b, bass.ds(i * 1024 + g * 512, 512)]
                        V.tensor_tensor(dst, ps[4 * g + b][:], dst, ALU.add).then_inc(out_free, 1)

            for b in range(NB):
                dve.wait_ge(n2_sum, b + 1)
                mean_square(36 + b, 32 + b, D).then_inc(n2_ms, 1)
            dve.wait_ge(gbc_in, 32)
            for b in range(NB):
                dve.wait_ge(n2_root, b + 1)
                chain.step(inverse(44 + b, 40 + b))
                V.scalar_tensor_tensor(h2[:, b, :], x2[:, b, :], small[:, 44 + b:45 + b], gbc[:],
                                       ALU.mult, ALU.mult).then_inc(n2_h, 1)
            V.memset(idx_all[:, UNITS, :], 0)
            V.memset(gate_all[:, UNITS, :], 0.0)

            idx4 = idx_all[:, 0:UNITS, :].rearrange("p (b h) k -> p b h k", h=PH)
            gate4 = gate_all[:, 0:UNITS, :].rearrange("p (b h) k -> p b h k", h=PH)

            def top16(values, v16, i16):
                chain.step(V.max(v16[:, 0:8], values))
                chain.step(V.max_index(i16[:, 0:8], v16[:, 0:8], values))
                rep = s_rep if values.shape[-1] == NK else cand2
                chain.step(V.match_replace(rep, v16[:, 0:8], values, LOW))
                chain.step(V.max(v16[:, 8:16], rep))
                chain.step(V.max_index(i16[:, 8:16], v16[:, 8:16], rep))

            with dve.Fori(0, PH // 2) as i:
                chain.enter()
                for m in range(2):
                    hold(dve, s_ev, i * 4 + (2 * m + 2), dve_passed)
                    for c in range(2):
                        for b in range(NB):
                            top16(s_sb[:, m, c, b * NK:b * NK + NK], vals[:, c * NB + b, :], idx_u[:, c * NB + b, :])
                    V.tensor_copy(idxf, idx_u).then_inc(s_free, 1)
                    dve.wait_ge(s_free, i * 2 + (m + 3))
                    for b in range(NB):
                        c3 = cand.rearrange("p (a b) -> p a b", b=TOP)
                        chain.step(V.tensor_tensor(
                            c3, vals[:, b, :].unsqueeze(2).broadcast_to([P, TOP, TOP]),
                            vals[:, NB + b, :].unsqueeze(1).broadcast_to([P, TOP, TOP]), ALU.add))
                        top16(cand, best[:, b, :], pos_u[:, b, :])
                    dst = V.tensor_tensor(ee, best, best[:, :, 0:1].broadcast_to([P, NB, TOP]), ALU.subtract)
                    dst.then_inc(sm_in, 1)
                    chain.mark(V.tensor_scalar(pos_a, pos_u, 4, None, ALU.logical_shift_right))
                    chain.step(V.tensor_scalar(pos_b, pos_u, TOP - 1, None, ALU.bitwise_and))
                    chain.mark(V.tensor_copy(pa, pos_a))
                    chain.step(V.tensor_copy(pb, pos_b))
                    for c, (place, got) in enumerate(((pa, ia), (pb, ib))):
                        for b in range(NB):
                            chain.step(V.tensor_tensor(
                                onehot, iota16[:].unsqueeze(1).broadcast_to([P, TOP, TOP]),
                                place[:, b, :].unsqueeze(2).broadcast_to([P, TOP, TOP]), ALU.is_equal))
                            chain.step(V.tensor_tensor(
                                picked, onehot, idxf[:, c * NB + b, :].unsqueeze(1).broadcast_to([P, TOP, TOP]),
                                ALU.mult))
                            chain.step(V.tensor_reduce(got[:, b, :], picked, AX.X, ALU.add))
                    dst = idx4[:, :, bass.ds(i * 2 + m, 1), :].rearrange("p b h k -> p b (h k)")
                    chain.step(V.scalar_tensor_tensor(dst, ia, float(NK), ib, ALU.mult, ALU.add))
                    dve.wait_ge(sm_exp, i * 2 + (m + 1))
                    chain.step(V.tensor_reduce(es, ee, AX.X, ALU.add))
                    chain.step(V.reciprocal(es, es))
                    dst = gate4[:, :, bass.ds(i * 2 + m, 1), :].rearrange("p b h k -> p b (h k)")
                    chain.step(V.tensor_tensor(dst, ee, es.unsqueeze(2).broadcast_to([P, NB, TOP]), ALU.mult))
                chain.leave()

            chain.step(V.tensor_copy(gate_cur[:, 0, :], gate_all[:, 0, :]))
            V.tensor_copy(idx_cur[:, 0, :], idx_all[:, 0, :]).then_inc(idx_ready, 1)
            with dve.Fori(0, NB) as b:
                with dve.Fori(0, PH // 2) as j:
                    unit = b * PH + j * 2
                    for n in range(2 * TOP):
                        m, k = n // TOP, n % TOP
                        s = n % SLOTS
                        dve.wait_ge(u_ready[s], unit * (16 * TOP // SLOTS) + 16 * (n // SLOTS + 1))
                        h2b = h2[:, bass.ds(b, 1), :].rearrange("p a d -> p (a d)")
                        V.scalar_tensor_tensor(u_row[s], u_row[s], 1.0, h2b, ALU.mult, ALU.mult,
                                               accum_out=act_u[:, m, k:k + 1]).then_inc(u_used, 1)
                        if k == TOP // 2:
                            dve.wait_ge(v_used, unit * TOP + (m * TOP + SLOTS))
                            V.tensor_copy(gate_cur[:, 1 - m, :], gate_all[:, bass.ds(unit + (m + 1), 1), :]
                                          .rearrange("p a k -> p (a k)")).then_inc(gate_step, 1)
                            V.tensor_copy(idx_cur[:, 1 - m, :], idx_all[:, bass.ds(unit + (m + 1), 1), :]
                                          .rearrange("p a k -> p (a k)")).then_inc(idx_ready, 1)
                        if k == TOP - 1:
                            dve.wait_ge(v_used, unit * TOP + ((m + 1) * TOP + SLOTS))
                            for q in range(4):
                                dst = x2[:, bass.ds(b, 1), q * 512:q * 512 + 512].rearrange("p a d -> p (a d)")
                                ins = V.tensor_tensor(dst, ps[4 * m + q][:], dst, ALU.add)
                            ins.then_inc(mix_free, 1)

            for b in range(NB):
                dve.wait_ge(fin_sum, b + 1)
                mean_square(52 + b, 48 + b, D).then_inc(fin_ms, 1)
            dve.wait_ge(gbc_in, 48)
            for b in range(NB):
                dve.wait_ge(fin_root, b + 1)
                chain.step(inverse(60 + b, 56 + b))
                V.scalar_tensor_tensor(x2[:, b, :], x2[:, b, :], small[:, 60 + b:61 + b], gbc[:],
                                       ALU.mult, ALU.mult).then_inc(fin_y, 1)

        @block.tensor
        def _(pe):
            M = nc.tensor.matmul

            def transposes(banks_first, n_banks, src, done, ready):
                for g in range(n_banks):
                    ready(g)
                    for q in range(4):
                        last = nc.tensor.transpose(ps[(banks_first + g) % 8][:, q * P:q * P + P],
                                                   src(4 * g + q), ident[:])
                    last.then_inc(done, 1)

            def slab_ready(n, i=None, per=0):
                if i is None:
                    pe.wait_ge(w_in_slot[n % 2], 16 * (n // 2 + 1))
                else:
                    pe.wait_ge(w_in_slot[n % 2], i * (8 * per) + 16 * (n // 2 + 1))

            pe.sem_inc(w_used, 2)
            pe.sem_inc(v_used, SLOTS)

            pe.wait_ge(consts, 2)
            pe.wait_ge(rows_in, 16 * 7)
            for g in range(2):
                for q in range(8):
                    last = nc.tensor.transpose(ps[g][:, 64 * q:64 * q + ROWS],
                                               rows[:, (8 * g + q) * P:(8 * g + q + 1) * P], ident[0:ROWS, 0:ROWS])
                last.then_inc(cols_tr, 1)
            pe.wait_ge(cols_done, 2)
            for b in range(NB):
                pe.wait_ge(n1_xn, b + 1)

                def ready(g):
                    if b * 4 + g >= 8:
                        pe.wait_ge(n1_done, b * 4 + g - 7)

                transposes(b * 4, 4, lambda t: xb[:, b, t * P:t * P + P], n1_tr, ready)
            pe.wait_ge(n1_done, 16)
            pe.wait_ge(wgk_in, 16)
            for d in range(2):
                for k in range(KT):
                    last = M(ps[d][0:RANK, :], wgk[:, k, d * RANK:d * RANK + RANK], hT[:, k, :],
                             start=k == 0, stop=k == KT - 1)
                last.then_inc(glow_mm, 1)
            pe.wait_ge(glow_done, 2)

            def project(slot, m, act_in, bank, done):
                for k in range(KT):
                    last = M(ps[bank][:], w_slot(slot)[:, k, m * P:m * P + P], act_in[:, k, :],
                             start=k == 0, stop=k == KT - 1)
                last.then_inc(done, 1)
                return last

            with pe.Fori(0, HEADS) as h:
                for s in range(2):
                    slab_ready(s, h, HEAD_SLABS)
                    for m in range(MT):
                        project(s, m, hT, 2 * s + m, q_mm)
                    pe.drain().then_inc(w_used, 1)
                pe.wait_ge(gkw_in, h * 32 + 32)
                for u in range(4):
                    M(ps[4 + u][:], gkw[:, u // 2, (u % 2) * P:(u % 2) * P + P], glow[:, u // 2, :],
                      start=True, stop=True).then_inc(z_mm, 1)
                pe.wait_ge(q_ev, h * 4 + 4)
                for first, bank0, done in ((2, 0, v_mm), (4, 4, og_mm)):
                    if bank0:
                        pe.wait_ge(z_dif, h * 4 + 4)
                    for s in range(2):
                        slab_ready(first + s, h, HEAD_SLABS)
                        for k in range(KT // 2):
                            kk = s * (KT // 2) + k
                            for b in range(NB):
                                last = M(ps[bank0 + b][:], hT[:, kk, b * P:b * P + P], w_slot_half(s)[:, k, :],
                                         start=kk == 0, stop=kk == KT - 1)
                                if kk == KT - 1:
                                    last.then_inc(done, 1)
                        pe.drain().then_inc(w_used, 1)
                pe.wait_ge(z_qk, h * 4 + 4)
                pe.wait_ge(v_ev, h * 4 + 4)
                for u in range(4):
                    for c in range(NB):
                        last = nc.tensor.transpose(ps[u][:, c * P:c * P + P],
                                                   km[:, u // 2, u % 2, c * P:c * P + P], ident[:])
                    last.then_inc(kt_tr, 1)
                pe.wait_ge(kt_ev, h * 4 + 4)
                for j, c in enumerate((3, 2, 1)):
                    if j == 2:
                        pe.wait_ge(ub_done, h * 6 + 2)
                    for m in range(MT):
                        M(ps[2 * (j % 2) + m][:], kmT[:, c, 1, m * P:m * P + P], v_tok[:, c, :],
                          start=True, stop=True).then_inc(ub_mm, 1)

                def scores(c):
                    if c >= 2:
                        pe.wait_ge(sc_done, h * 4 + (c - 1))
                    for d in range(2):
                        for m in range(MT):
                            last = M(ps[4 + c % 2][:, d * P:d * P + P], km[:, d, m, c * P:c * P + P],
                                     qm[:, d, m, c * P:c * P + P], start=m == 0, stop=m == MT - 1)
                    last.then_inc(sc_mm, 1)

                def heads_out(c):
                    pe.wait_ge(o_norm, h * 4 + (c + 1))
                    if c >= 2:
                        pe.wait_ge(ot_ev, h * 4 + (c - 1))
                    for q in range(4):
                        last = nc.tensor.transpose(ps[2 + c % 2][:, q * P:q * P + P],
                                                   on[:, c % 2, q * P:q * P + P], ident[:])
                    last.then_inc(ot_tr, 1)

                pe.wait_ge(og_ev, h * 4 + 4)
                scores(0)
                pe.wait_ge(ub_done, h * 6 + 6)
                for c in range(NB):
                    if c < NB - 1:
                        scores(c + 1)
                        if c:
                            pe.wait_ge(uf_done, h * 6 + 2 * c)
                        for m in range(MT):
                            M(ps[m][:], kmT[:, c, 0, m * P:m * P + P], v_tok[:, c, :],
                              start=True, stop=True).then_inc(uf_mm, 1)
                    terms = []
                    if c < NB - 1:
                        terms += [(qm[:, 1, m, c * P:c * P + P], st_b[:, c, m, :]) for m in range(MT)]
                    if c > 0:
                        terms += [(qm[:, 0, m, c * P:c * P + P], st_f[:, c % 2, m, :]) for m in range(MT)]
                    terms.append((p_t[:, c % 2, :], v_tok[:, c, :]))
                    if c:
                        pe.wait_ge(uf_done, h * 6 + 2 * c)
                    if c >= 2:
                        pe.wait_ge(o_norm, h * 4 + (c - 1))
                    pe.wait_ge(sc_done, h * 4 + (c + 1))
                    for n, (lhs, rhs) in enumerate(terms):
                        last = M(ps[6 + c % 2][:], lhs, rhs, start=n == 0, stop=n == len(terms) - 1)
                    last.then_inc(o_mm, 1)
                    if c:
                        heads_out(c - 1)
                heads_out(NB - 1)
                pe.wait_ge(ot_ev, h * 4 + 4)

            def pairs(name, first, start, end, val_in):
                p = pair[name]
                with pe.Fori(start, end) as i:
                    slab_ready(first, i, 2)
                    for m in range(2):
                        pe.wait_ge(p["use"], i * 2 + (m + 1))
                        project(0, m, hT, m, p["gate"])
                    pe.drain().then_inc(w_used, 1)
                    slab_ready(first + 1, i, 2)
                    for m in range(2):
                        project(1, m, val_in, 2 + m, p["val"])
                    pe.drain().then_inc(w_used, 1)

            pairs("cv", SB_CONV, 0, KT // 2, hT)
            pe.wait_ge(pair["cv"]["use"], KT + 2)
            pairs("ma", SB_MA, 0, KT // 4, oT)
            pe.wait_ge(cv_done, KT)
            for t in range(KT):
                last = M(ps[4][:], ones_d[:], cv[:, t, :], start=t == 0, stop=t == KT - 1)
            last.then_inc(ln_sum, 1)
            pairs("ma", SB_MA, KT // 4, KT // 2, oT)
            for t in range(KT):
                pe.wait_ge(ln_sq, t + 1)
                last = M(ps[5][:], ones_d[:], sqr[:, t % 2, :], start=t == 0, stop=t == KT - 1)
                last.then_inc(ln_varu, 1)
            pe.wait_ge(ln_act, KT)
            pe.wait_ge(pair["ma"]["use"], KT + 2)
            pairs("mb", SB_MB, 0, KT // 2, cv)

            pe.wait_ge(mb_done, KT)
            with pe.Fori(0, 2) as i:
                for g in range(2):
                    for s in range(2):
                        slab_ready(SB_OUT + 2 * g + s, i, 4)
                        for k in range(KT // 2):
                            kk = s * (KT // 2) + k
                            for b in range(NB):
                                if kk == 0:
                                    pe.wait_ge(out_free, i * 8 + (4 * g + b + 1))
                                last = M(ps[4 * g + b][:], mg[:, kk, b * P:b * P + P], w_slot_half(s)[:, k, :],
                                         start=kk == 0, stop=kk == KT - 1)
                                if kk == KT - 1:
                                    last.then_inc(out_mm, 1)
                        pe.drain().then_inc(w_used, 1)

            for b in range(NB):
                pe.wait_ge(n2_h, b + 1)

                def ready2(g):
                    if b * 4 + g >= 8:
                        pe.wait_ge(n2_ev, b * 4 + g - 7)

                transposes(b * 4, 4, lambda t: h2[:, b, t * P:t * P + P], n2_tr, ready2)
            pe.wait_ge(keys_in, 16)
            pe.wait_ge(n2_ev, 16)
            transposes(0, 4, lambda t: keys_n[:, t, :], keys_tr, lambda g: None)
            pe.wait_ge(keys_ev, 4)

            with pe.Fori(0, PH // 2) as i:
                for m in range(2):
                    slab_ready(SB_WQ + m, i, 2)
                    for c in range(2):
                        project(m, c, h2T, 4 * m + c, pq_mm)
                    pe.drain().then_inc(w_used, 1)
                    for c in range(2):
                        pe.wait_ge(pq_ev, i * 4 + (2 * m + c + 1))
                        key = keysT[:, bass.ds(i * 4 + (2 * m + c), 1), :].rearrange("p a n -> p (a n)")
                        for b in range(NB):
                            last = M(ps[4 * m + 2 + c][:, b * NK:b * NK + NK], qh[:, c, b * P:b * P + P], key,
                                     start=True, stop=True)
                        last.then_inc(s_mm, 1)

            with pe.Fori(0, UNITS // 2) as i:
                for n in range(2 * TOP):
                    m, k = n // TOP, n % TOP
                    s = n % SLOTS
                    if k == 0:
                        pe.wait_ge(mix_free, i * 2 + (m + 1))
                    pe.wait_ge(v_ready[s], i * (32 * TOP // SLOTS) + 16 * (n // SLOTS + 1))
                    pe.wait_ge(diag_ready, i * 2 * TOP + (n + 1))
                    for q in range(4):
                        last = M(ps[4 * m + q][:], diag[:, s, :], v_row[s][:, q * 512:q * 512 + 512],
                                 start=k == 0, stop=k == TOP - 1)
                    last.then_inc(v_used, 1)


_INS = ["x", "norm1_g", "w_in", "gla_gk_fwd_w", "gla_gk_fwd_b", "gla_gk_bwd_w", "gla_gk_bwd_b", "gla_onorm_g",
        "gla_w_o", "conv_w", "conv_b", "conv_ln_g", "conv_ln_b", "conv_w_pw2", "w_out", "norm2_g", "peer_w_q",
        "peer_keys", "peer_u", "peer_v", "final_norm_g"]


def kernel(**inputs):
    import numpy as np
    import concourse.bacc as bacc
    from concourse import mybir as mb
    from concourse.bass_utils import run_bass_kernel_spmd

    nc = bacc.Bacc("TRN2", target_bir_lowering=False, num_devices=1)
    arrays, args = {}, []
    for name in _INS:
        a = np.ascontiguousarray(inputs[name])
        arrays["in_" + name] = a
        args.append(nc.dram_tensor("in_" + name, a.shape, mb.dt.from_np(a.dtype), kind="ExternalInput").ap())
    out = nc.dram_tensor("out_0", (1, T, D), mb.dt.float32, kind="ExternalOutput").ap()
    hybrid_block(nc, *args, out)
    r = run_bass_kernel_spmd(nc, [arrays], core_ids=[0])
    return r.results[0]["out_0"]
```

```python
import concourse.bass as bass
from concourse import mybir
from contextlib import ExitStack

P = 128
F32 = mybir.dt.float32
U32 = mybir.dt.uint32
I32 = mybir.dt.int32
ALU = mybir.AluOpType
ACT = mybir.ActivationFunctionType
AX = mybir.AxisListType

D = 2048
T = 512
KT = D // P
NB = T // P
HEADS = 4
DK = 256
DV = 512
MT = DK // P
RANK = 16
TAPS = 31
PAD = TAPS // 2
EPS = 1e-6
PH = 8
NK = 128
TOP = 16
REF = P // 2
CLAMP = 16.0 * 80.0
LOW = -3.0e38

OQ, OK_, OV, OG = 0, 1024, 2048, 4096
OGK = 6144
OGLU = 6176
OGATE = OGLU + 2048
OGA = OGLU + 4096
OGB = OGA + 2048

R_N1, R_CB, R_LG, R_LB, R_CW = 0, 1, 2, 3, 4
R_GK = R_CW + TAPS
ROWS = R_GK + 1

TA = P
TB = T - TA
NBB = NB - 1

HEAD_SLABS = 6
SB_CONV = HEADS * HEAD_SLABS
SB_MA1 = SB_CONV + KT
SB_MB1 = SB_MA1 + 16
SB_OUT1 = SB_MB1 + 16
SB_WQ1 = SB_OUT1 + 8
SB_MA = SB_WQ1 + PH
SB_MB = SB_MA + KT
SB_OUT = SB_MB + KT
SB_WQ = SB_OUT + 8
SLAB = 4096
UNITS = NB * PH
US, VS = 4, 2
SLOTS = 4


class Chain:

    def __init__(self, eng, sem):
        self.eng, self.sem, self.n = eng, sem, 0

    def enter(self):
        self.start = self.n

    def leave(self):
        self.wait()
        self.eng.sem_inc(self.sem, self.start - self.n)
        self.n = self.start

    def mark(self, ins):
        self.n += 1
        ins.then_inc(self.sem, 1)

    def wait(self):
        self.eng.wait_ge(self.sem, self.n)

    def step(self, ins):
        self.mark(ins)
        self.wait()


def hold(eng, sem, value, passed):
    eng.wait_ge(sem, value)
    eng.sem_inc(passed, 1)


def hybrid_block(nc, x, norm1_g, w_in, gk_f_w, gk_f_b, gk_b_w, gk_b_b, onorm_g, w_o, conv_w, conv_b,
                 ln_g, ln_b, w_pw2, w_out, norm2_g, w_q, keys, u_tab, v_tab, final_g, out):
    def slabs(w, half):
        w2 = w[0]
        if half:
            return w2.rearrange("(s k p) n -> s p k n", p=P, s=2)
        return w2.rearrange("(k p) n -> p k n", p=P)

    ctx = ExitStack()
    with ctx:
        def sb(name, shape, dt=F32):
            return ctx.enter_context(nc.sbuf_tensor(name, shape, dt))

        def sem(name):
            return ctx.enter_context(nc.semaphore(name))

        def view(t, off, *shape):
            n = 1
            for s in shape:
                n *= s
            a = t[:, off:off + n]
            if len(shape) == 2:
                a = a.rearrange("p (a b) -> p a b", b=shape[1])
            elif len(shape) == 3:
                a = a.rearrange("p (a b c) -> p a b c", b=shape[1], c=shape[2])
            return a

        arena_h = sb("arena_h", [P, KT * T])
        arena_o = sb("arena_o", [P, KT * T])
        YB = KT * T
        arena_c = sb("arena_c", [P, YB + 17664])
        wring = sb("wring", [P, 2 * SLAB])
        ident = sb("ident", [P, P])
        ones_d = sb("ones_d", [P, P])
        iota_i = sb("iota_i", [P, TOP], I32)
        iota16 = sb("iota16", [P, TOP])
        cols = sb("cols", [P, KT, ROWS])
        small = sb("small", [P, 64])
        idx_all = sb("idx_all", [P, UNITS + 1, TOP], U32)
        gate_all = sb("gate_all", [P, UNITS, TOP])

        hT = view(arena_h, 0, KT, T)
        h2T = view(arena_h, 0, KT, T)
        mgT1 = view(arena_h, 0, KT, T)[:, :, 0:P]
        oT = view(arena_o, 0, KT, T)
        x2 = view(arena_o, 0, KT, T)
        cv = view(arena_c, 0, KT, T)
        h2 = view(arena_c, 0, KT, T)

        xb = view(arena_c, 0, NB, D)
        sq_x = view(arena_c, 8192, D)
        rows = arena_c[0:ROWS, 10240:10240 + D]
        wgk = view(arena_c, 12800, KT, 2 * RANK)
        o_ = [0]

        def take(*shape):
            n = 1
            for d in shape:
                n *= d
            a = view(arena_c, o_[0], *shape)
            o_[0] += n
            return a

        qT = take(MT, T)
        kT = take(MT, T)
        v_tok = take(NB, DV)
        og_s = take(NB, DV)
        qm = take(2, MT, T)
        km = take(2, MT, T)
        kmT = take(NB, 2, DK)
        st_b = take(3, MT, DV)
        st_f = take(2, MT, DV)
        t_abs = take(T)
        t_l = take(T)
        t_b = take(T)
        t_d = take(T)
        t_e = take(T)
        on = take(2, DV)
        p_t = take(2, P)
        dec = take(4, 4)
        dif = take(4)
        causal = take(P)
        reset = take(T)
        gbc_o = take(D)
        gkw = take(2, DK)[0:RANK]
        glow = take(2, T)[0:RANK]
        assert o_[0] <= YB + 17664, o_[0]
        upad = view(arena_c, YB, 2, T + 2 * PAD)
        sig_c = view(arena_c, YB + 1088, 2, T)
        RU, RV, MG, SG = YB, YB + US * D, YB + (US + VS) * D, YB + (US + VS) * D + 4096
        mgA = view(arena_c, RU, D)
        mgTA = view(arena_c, RU + 2048, KT, P)
        sigA = view(arena_c, RU + 4096, 512)
        tmpA = view(arena_c, RU + 4608, 512)
        sq_a = view(arena_c, RU + 6144, KT, P)
        sqr = view(arena_c, RV, 2, T)
        rstd_ln = view(arena_c, RV + 1024, T)
        root_ln = view(arena_c, RV + 1536, T)
        s_a = view(arena_c, RV + 2048, 4, NK)
        keys_nA = view(arena_c, RV, 2 * PH, NK)

        def scoresA(m, c):
            return s_a[:, 2 * m + c:2 * m + c + 1, :]

        def scoresB(m, c):
            return h2T[:, 4 * (2 * m + c):4 * (2 * m + c) + NBB, 0:NK]

        u_row = [view(arena_c, RU + s * D, D) for s in range(US)]
        v_row = [view(arena_c, RV + s * D, D) for s in range(VS)]
        mgT23 = view(arena_c, MG, KT, 2 * P)
        sig = view(arena_c, SG, 2, TB)
        mtmp = view(arena_c, SG + 768, TB)
        act_u = view(arena_c, SG + 1152, TOP)
        act_g = view(arena_c, SG + 1168, TOP)
        act_w = view(arena_c, SG + 1184, TOP)
        idx_cur = view(arena_c, SG + 1200, 2, TOP).bitcast(U32)
        sq_b = view(arena_c, MG + 2048, KT, P)
        gbc2 = view(arena_c, MG, D)
        keys_n = view(arena_c, MG, 2 * PH, NK)
        keysT = view(arena_c, MG + 2048, 2 * PH, NK)
        qh = view(arena_c, MG, 2, TB)
        cand = view(arena_c, MG + 768, TOP * TOP)
        cand2 = view(arena_c, MG + 1024, TOP * TOP)
        onehot = view(arena_c, MG + 1280, TOP, TOP)
        picked = view(arena_c, MG + 1536, TOP, TOP)
        vals = view(arena_c, SG, NBB * 2, TOP)
        s_rep = view(arena_c, SG + 96, NK)
        best = view(arena_c, SG + 224, NBB, TOP)
        pa = view(arena_c, SG + 272, NBB, TOP)
        pb = view(arena_c, SG + 320, NBB, TOP)
        ia = view(arena_c, SG + 368, NBB, TOP)
        ib = view(arena_c, SG + 416, NBB, TOP)
        idxf = view(arena_c, SG + 464, NBB * 2, TOP)
        ee = view(arena_c, SG + 560, NBB, TOP)
        es = view(arena_c, SG + 608, NBB)
        idx_u = view(arena_c, SG + 612, NBB * 2, TOP).bitcast(U32)
        pos_u = view(arena_c, SG + 708, NBB, TOP).bitcast(U32)
        pos_a = view(arena_c, SG + 756, NBB, TOP).bitcast(U32)
        pos_b = view(arena_c, SG + 804, NBB, TOP).bitcast(U32)
        u2_row = [view(arena_h, s * D, D) for s in range(SLOTS)]
        v2_row = [view(arena_c, RU + s * D, D) for s in range(SLOTS)]
        diag = view(arena_c, RV, SLOTS, P)
        act_u2 = view(arena_c, RV + 512, 2, TOP)
        act_g2 = view(arena_c, RV + 544, 2, TOP)
        act_w2 = view(arena_c, RV + 576, 2, TOP)
        idx_cur2 = view(arena_c, RV + 608, 2, TOP).bitcast(U32)
        gbc_f = view(arena_c, MG, D)
        sq_f = view(arena_c, MG + 2048, KT, P)
        y_out = view(arena_h, 0, NB, D)

        ps = [ctx.enter_context(nc.psum_tensor(f"bank{n}", [P, 512], F32)) for n in range(8)]

        const_step = sem("const_step")
        consts = sem("consts")
        x_in = [sem(f"x_in{b}") for b in range(NB)]
        rows_in = sem("rows_in")
        cols_tr = sem("cols_tr")
        cols_done = sem("cols_done")
        small_in = sem("small_in")
        gkw_in = sem("gkw_in")
        gbc_in = sem("gbc_in")
        wgk_in = sem("wgk_in")
        w_in_slot = [sem("w_slot0"), sem("w_slot1")]
        w_used = sem("w_used")
        dve_chain = sem("dve_chain")
        sp_passed = sem("sp_passed")
        pool_passed = sem("pool_passed")
        dve_passed = sem("dve_passed")
        n1_sum = sem("n1_sum")
        n1_ms = sem("n1_ms")
        n1_root = sem("n1_root")
        n1_xn = sem("n1_xn")
        n1_tr = sem("n1_tr")
        n1_done = sem("n1_done")
        glow_mm = sem("glow_mm")
        glow_done = sem("glow_done")
        q_mm = sem("q_mm")
        q_ev = sem("q_ev")
        z_mm = sem("z_mm")
        z_exp = sem("z_exp")
        z_ln = sem("z_ln")
        z_dif = sem("z_dif")
        z_dec = sem("z_dec")
        z_qk = sem("z_qk")
        v_mm = sem("v_mm")
        v_ev = sem("v_ev")
        og_mm = sem("og_mm")
        og_ev = sem("og_ev")
        og_scaled = sem("og_scaled")
        kt_tr = sem("kt_tr")
        kt_ev = sem("kt_ev")
        ub_mm = sem("ub_mm")
        ub_done = sem("ub_done")
        uf_mm = sem("uf_mm")
        uf_done = sem("uf_done")
        sc_mm = sem("sc_mm")
        sc_done = sem("sc_done")
        o_mm = sem("o_mm")
        o_sum = sem("o_sum")
        o_ms = sem("o_ms")
        o_root = sem("o_root")
        o_norm = sem("o_norm")
        ot_tr = sem("ot_tr")
        ot_ev = sem("ot_ev")
        pair = {}
        for name in ("cv", "ma1", "mb1", "ma", "mb"):
            pair[name] = dict(gate=sem(name + "_gate"), sig=sem(name + "_sig"), val=sem(name + "_val"),
                              use=sem(name + "_use"))
        cv_done = sem("cv_done")
        ln_sum = sem("ln_sum")
        ln_xc = sem("ln_xc")
        ln_sq = sem("ln_sq")
        ln_varu = sem("ln_varu")
        ln_ms = sem("ln_ms")
        ln_root = sem("ln_root")
        ln_scaled = sem("ln_scaled")
        ln_act = sem("ln_act")
        mb1_done = sem("mb1_done")
        mb_done = sem("mb_done")
        mt_tr = sem("mt_tr")
        mt_ev = sem("mt_ev")
        out1_mm = sem("out1_mm")
        out1_free = sem("out1_free")
        res_in = sem("res_in")
        out_mm = sem("out_mm")
        out_free = sem("out_free")
        n2_sum = sem("n2_sum")
        n2_ms = sem("n2_ms")
        n2_root = sem("n2_root")
        n2_h = sem("n2_h")
        n2_tr = sem("n2_tr")
        n2_ev = sem("n2_ev")
        keys_in = sem("keys_in")
        keys_tr = sem("keys_tr")
        keys_ev = sem("keys_ev")
        pq_mm = sem("pq_mm")
        pq_ev = sem("pq_ev")
        s_mm = sem("s_mm")
        s_ev = sem("s_ev")
        sm_in = sem("sm_in")
        sm_exp = sem("sm_exp")
        s_free = sem("s_free")
        idx_ready = sem("idx_ready")
        u_ready = [sem(f"u_ready{s}") for s in range(US)]
        v_ready = [sem(f"v_ready{s}") for s in range(VS)]
        u_used = sem("u_used")
        v_used = sem("v_used")
        act_done = sem("act_done")
        w_ready = sem("w_ready")
        idx2_ready = sem("idx2_ready")
        u2_ready = [sem(f"u2_ready{s}") for s in range(SLOTS)]
        v2_ready = [sem(f"v2_ready{s}") for s in range(SLOTS)]
        u2_used = sem("u2_used")
        v2_used = sem("v2_used")
        act2_done = sem("act2_done")
        diag_ready = sem("diag_ready")
        mix_free = sem("mix_free")
        fin_sum = sem("fin_sum")
        fin_ms = sem("fin_ms")
        fin_root = sem("fin_root")
        fin_y = sem("fin_y")
        out_done = sem("out_done")

        block = ctx.enter_context(nc.Block())
        x_d = x[0].rearrange("(b p) d -> b p d", p=P)
        out_d = out[0].rearrange("(b p) d -> b p d", p=P)

        def block_of(a, b):
            return a[:, :, bass.ds(b * P, P)]

        def by_tile(a):
            return a.rearrange("p (k j) -> p k j", j=P)

        def w_slot(n):
            return view(wring, (n % 2) * SLAB, KT, 256)

        def w_slot_half(n):
            return view(wring, (n % 2) * SLAB, KT // 2, 512)

        @block.sync
        def _(sp):
            for b in range(NB):
                sp.dma_start(xb[:, b, :], x_d[b]).then_inc(x_in[b], 16)
            sp.dma_start(wgk, slabs(w_in, False)[:, :, OGK:OGK + 2 * RANK]).then_inc(wgk_in, 16)

            def load(n, i, per, dst, src):
                hold(sp, w_used, i * per + (n + 1), sp_passed)
                sp.dma_start(dst, src).then_inc(w_in_slot[n % 2], 16)

            full, half = slabs(w_in, False), slabs(w_in, True)
            with sp.Fori(0, HEADS) as h:
                load(0, h, HEAD_SLABS, w_slot(0), full[:, :, bass.ds(h * DK + OQ, DK)])
                load(1, h, HEAD_SLABS, w_slot(1), full[:, :, bass.ds(h * DK + OK_, DK)])
                for s in range(2):
                    load(2 + s, h, HEAD_SLABS, w_slot_half(s), half[s][:, :, bass.ds(h * DV + OV, DV)])
                for s in range(2):
                    load(4 + s, h, HEAD_SLABS, w_slot_half(s), half[s][:, :, bass.ds(h * DV + OG, DV)])

            def pair_loads(first, w_gate, o_gate, w_val, o_val):
                with sp.Fori(0, KT // 2) as i:
                    load(first, i, 2, w_slot(0), slabs(w_gate, False)[:, :, bass.ds(i * 256 + o_gate, 256)])
                    load(first + 1, i, 2, w_slot(1), slabs(w_val, False)[:, :, bass.ds(i * 256 + o_val, 256)])

            pair_loads(SB_CONV, w_in, OGATE, w_in, OGLU)

            def group_loads(first, w_gate, o_gate, w_val):
                with sp.Fori(0, 4) as g:
                    for j, (w, o) in enumerate(((w_gate, o_gate), (w_val, 0))):
                        for s in range(2):
                            load(first + 2 * j + s, g, 4, w_slot_half(s), slabs(w, True)[s][:, :, bass.ds(g * 512 + o, 512)])

            def out_loads(first):
                with sp.Fori(0, 4) as g:
                    for s in range(2):
                        load(first + s, g, 2, w_slot_half(s), slabs(w_out, True)[s][:, :, bass.ds(g * 512, 512)])

            def query_loads(first):
                with sp.Fori(0, PH // 2) as i:
                    for s in range(2):
                        load(first + s, i, 2, w_slot(s), slabs(w_q, False)[:, :, bass.ds(i * 512 + s * 256, 256)])

            group_loads(SB_MA1, w_in, OGA, w_o)
            sp.wait_ge(w_used, SB_MB1 + 2)
            sp.dma_start(block_of(x2, 0), by_tile(x_d[0])).then_inc(res_in, 16)
            group_loads(SB_MB1, w_in, OGB, w_pw2)
            out_loads(SB_OUT1)
            query_loads(SB_WQ1)
            pair_loads(SB_MA, w_in, OGA, w_o, 0)
            sp.wait_ge(w_used, SB_MB + 2)
            for b in range(1, NB):
                sp.dma_start(block_of(x2, b), by_tile(x_d[b])).then_inc(res_in, 16)
            pair_loads(SB_MB, w_in, OGB, w_pw2, 0)
            out_loads(SB_OUT)
            query_loads(SB_WQ)
            for b in range(NB):
                sp.wait_ge(fin_y, b + 1)
                sp.dma_start(out_d[b], y_out[:, b, :]).then_inc(out_done, 16)
            sp.wait_ge(out_done, 16 * NB)

        @block.gpsimd
        def _(pool):
            G = nc.gpsimd
            G.memset(ident[:], 0.0).then_inc(const_step, 1)
            pool.wait_ge(const_step, 1)
            G.affine_select(out=ident[:], in_=ident[:], compare_op=ALU.not_equal, fill=1.0, base=0,
                            pattern=[[-1, P]], channel_multiplier=1).then_inc(consts, 1)
            G.memset(ones_d[:], 1.0 / D).then_inc(consts, 1)
            G.memset(causal, 1.0).then_inc(const_step, 1)
            pool.wait_ge(const_step, 2)
            G.affine_select(out=causal, in_=causal, compare_op=ALU.is_ge, fill=0.0, base=0,
                            pattern=[[1, P]], channel_multiplier=-1).then_inc(consts, 1)
            G.memset(reset, 1.0).then_inc(const_step, 1)
            pool.wait_ge(const_step, 3)
            G.memset(reset.rearrange("p (c t) -> p c t", t=P)[:, :, 0:1], 0.0).then_inc(consts, 1)
            G.iota(iota_i[:], pattern=[[1, TOP]], base=0, channel_multiplier=0).then_inc(const_step, 1)
            pool.wait_ge(const_step, 4)
            G.tensor_copy(iota16[:], iota_i[:]).then_inc(consts, 1)

            def gathers(turns, idx_sem, idx, u_rows, u_sems, u_free, v_rows, v_sems, v_free):
                with pool.Fori(0, turns) as i:
                    for m in range(2):
                        hold(pool, idx_sem, i * 2 + (m + 1), pool_passed)
                        for k in range(TOP):
                            n = m * TOP + k
                            at = bass.IndirectOffsetOnAxis(ap=idx[:, m, k:k + 1], axis=0)
                            hold(pool, u_free, i * 2 * TOP + (n + 1), pool_passed)
                            s = n % len(u_rows)
                            pool.indirect_dma_start(out=u_rows[s], out_offset=None, in_=u_tab[0], in_offset=at)\
                                .then_inc(u_sems[s], 16)
                            hold(pool, v_free, i * 2 * TOP + (n + 1), pool_passed)
                            s = n % len(v_rows)
                            pool.indirect_dma_start(out=v_rows[s], out_offset=None, in_=v_tab[0], in_offset=at)\
                                .then_inc(v_sems[s], 16)

            gathers(PH // 2, idx_ready, idx_cur, u_row, u_ready, u_used, v_row, v_ready, v_used)
            gathers((UNITS - PH) // 2, idx2_ready, idx_cur2, u2_row, u2_ready, u2_used, v2_row, v2_ready, v2_used)

        @block.scalar
        def _(act):
            A = nc.scalar.activation
            for src, r in ((norm1_g, R_N1), (conv_b, R_CB), (ln_g, R_LG), (ln_b, R_LB)):
                act.dma_start(rows[r:r + 1, :], src).then_inc(rows_in, 16)
            act.dma_start(rows[R_CW:R_CW + TAPS, :], conv_w[0]).then_inc(rows_in, 16)
            act.dma_start(rows[R_GK:R_GK + 1, 0:1024], gk_f_b).then_inc(rows_in, 16)
            act.dma_start(rows[R_GK:R_GK + 1, 1024:2048], gk_b_b).then_inc(rows_in, 16)
            act.dma_start(gbc_o, onorm_g.rearrange("a h e -> a (h e)").broadcast_to([P, D])).then_inc(gbc_in, 16)

            for b in range(NB):
                act.wait_ge(x_in[b], 16)
                A(sq_x, xb[:, b, :], ACT.Square, accum_out=small[:, b:b + 1]).then_inc(n1_sum, 1)
                act.wait_ge(n1_sum, b + 1)
            for b in range(NB):
                act.wait_ge(n1_ms, b + 1)
                A(small[:, 8 + b:9 + b], small[:, 4 + b:5 + b], ACT.Sqrt).then_inc(n1_root, 1)

            for d in range(2):
                act.wait_ge(glow_mm, d + 1)
                A(glow[:, d, :], ps[d][0:RANK, :], ACT.Copy).then_inc(glow_done, 1)

            with act.Fori(0, HEADS) as h:
                act.dma_start(gkw[:, 0, :], gk_f_w[0][:, bass.ds(h * DK, DK)]).then_inc(gkw_in, 16)
                act.dma_start(gkw[:, 1, :], gk_b_w[0][:, bass.ds(h * DK, DK)]).then_inc(gkw_in, 16)
                for n in range(4):
                    act.wait_ge(q_mm, h * 4 + (n + 1))
                    dst = qT[:, n, :] if n < 2 else kT[:, n - 2, :]
                    A(dst, ps[n][:], ACT.Copy, scale=DK ** -0.5 if n < 2 else 1.0).then_inc(q_ev, 1)
                for u in range(4):
                    fwd = u < 2
                    act.wait_ge(z_mm, h * 4 + (u + 1))
                    bias = cols[:, bass.ds(h * MT + (8 * (u // 2) + u % 2), 1), R_GK]
                    A(t_abs, ps[4 + u][:], ACT.Abs, bias=bias).then_inc(z_exp, 1)
                    act.wait_ge(z_exp, h * 8 + (2 * u + 1))
                    A(t_abs, t_abs, ACT.Exp, scale=-1.0).then_inc(z_exp, 1)
                    act.wait_ge(z_exp, h * 8 + (2 * u + 2))
                    A(t_abs, t_abs, ACT.Ln, bias=1.0).then_inc(z_ln, 1)
                    act.wait_ge(z_dif, h * 4 + (u + 1))
                    A(t_e, t_d, ACT.Exp, scale=1.0 / 16 if fwd else -1.0 / 16).then_inc(z_dec, 1)
                    A(dec[:, u, 0:3], dif[:, 0:3], ACT.Exp, scale=1.0 / 16).then_inc(z_dec, 1)
                    act.wait_ge(z_dec, h * 12 + (3 * u + 2))
                    A(t_d, t_d, ACT.Exp, scale=-1.0 / 16 if fwd else 1.0 / 16).then_inc(z_dec, 1)
                    act.wait_ge(z_qk, h * 4 + (u + 1))
                for b in range(NB):
                    act.wait_ge(v_mm, h * 4 + (b + 1))
                    A(v_tok[:, b, :], ps[b][:], ACT.Copy).then_inc(v_ev, 1)
                for b in range(NB):
                    act.wait_ge(og_mm, h * 4 + (b + 1))
                    A(og_s[:, b, :], ps[4 + b][:], ACT.Silu).then_inc(og_ev, 1)
                for n in range(4):
                    act.wait_ge(kt_tr, h * 4 + (n + 1))
                    A(kmT[:, :, n // 2, (n % 2) * P:(n % 2) * P + P],
                      ps[n][:].rearrange("p (c f) -> p c f", f=P), ACT.Copy).then_inc(kt_ev, 1)

                def ot_out(c):
                    act.wait_ge(ot_tr, h * 4 + (c + 1))
                    A(oT[:, bass.ds(h * 4, 4), c * P:c * P + P],
                      ps[2 + c % 2][:].rearrange("p (m t) -> p m t", t=P), ACT.Copy).then_inc(ot_ev, 1)

                for c in range(NB):
                    act.wait_ge(o_mm, h * 4 + (c + 1))
                    if c:
                        act.wait_ge(o_sum, h * 4 + c)
                    A(t_abs, ps[6 + c % 2][:], ACT.Square, accum_out=small[:, 16 + c:17 + c]).then_inc(o_sum, 1)
                    act.wait_ge(o_ms, h * 4 + (c + 1))
                    A(small[:, 24 + c:25 + c], small[:, 20 + c:21 + c], ACT.Sqrt).then_inc(o_root, 1)
                    if c:
                        ot_out(c - 1)
                ot_out(NB - 1)

            def gates(name, i, dst, nt):
                p = pair[name]
                for m in range(2):
                    act.wait_ge(p["gate"], i * 2 + (m + 1))
                    act.wait_ge(p["use"], i * 2 + (m + 1))
                    A(dst[:, m, :], ps[m][:, 0:nt], ACT.Sigmoid).then_inc(p["sig"], 1)

            def gates1(name, start, end):
                p = pair[name]
                with act.Fori(start, end) as g:
                    act.wait_ge(p["gate"], g + 1)
                    act.wait_ge(p["use"], g + 1)
                    A(sigA, ps[0][:], ACT.Sigmoid).then_inc(p["sig"], 1)

            with act.Fori(0, KT // 2) as i:
                gates("cv", i, sig_c, T)
            act.dma_start(gbc2, norm2_g.broadcast_to([P, D])).then_inc(gbc_in, 16)
            gates1("ma1", 0, 2)
            gates1("ma1", 2, 4)
            for t in range(KT):
                act.wait_ge(ln_xc, t + 1)
                if t >= 2:
                    act.wait_ge(ln_varu, t - 1)
                A(sqr[:, t % 2, :], cv[:, t, :], ACT.Square).then_inc(ln_sq, 1)
            act.wait_ge(ln_ms, 1)
            A(root_ln, rstd_ln, ACT.Sqrt).then_inc(ln_root, 1)

            def ln_out(n, lo, hi):
                for t in range(KT):
                    act.wait_ge(ln_scaled, n * KT + t + 1)
                    A(cv[:, t, lo:hi], cv[:, t, lo:hi], ACT.Silu, bias=cols[:, t, R_LB:R_LB + 1],
                      scale=cols[:, t, R_LG:R_LG + 1]).then_inc(ln_act, 1)

            ln_out(0, 0, TA)
            gates1("mb1", 0, 4)
            ln_out(1, TA, T)

            def keys_load(dst):
                act.dma_start(dst, keys[0].rearrange("h c n d -> n (h c) d")).then_inc(keys_in, 16)

            def keys_out(n, bank):
                for g in range(4):
                    act.wait_ge(keys_tr, 4 * n + g + 1)
                    A(keysT[:, 4 * g:4 * g + 4, :], ps[(bank + g) % 8][:].rearrange("p (k t) -> p k t", t=P),
                      ACT.Copy).then_inc(keys_ev, 1)

            def norm2_stats(blocks, sq):
                for b in blocks:
                    A(sq, block_of(x2, b), ACT.Square, accum_out=small[:, 32 + b:33 + b]).then_inc(n2_sum, 1)
                    act.wait_ge(n2_sum, b + 1)
                for b in blocks:
                    act.wait_ge(n2_ms, b + 1)
                    A(small[:, 40 + b:41 + b], small[:, 36 + b:37 + b], ACT.Sqrt).then_inc(n2_root, 1)

            def norm2_out(blocks):
                for b in blocks:
                    for g in range(4):
                        n = b * 4 + g
                        act.wait_ge(n2_tr, n + 1)
                        A(h2T[:, 4 * g:4 * g + 4, b * P:b * P + P],
                          ps[n % 8][:].rearrange("p (k t) -> p k t", t=P), ACT.Copy).then_inc(n2_ev, 1)

            def queries(hg, m, nb, scores):
                for c in range(2):
                    act.wait_ge(pq_mm, hg * 2 + (c + 1))
                    A(qh[:, c, 0:nb * P], ps[4 * m + c][:, 0:nb * P], ACT.Copy).then_inc(pq_ev, 1)
                act.wait_ge(s_free, hg + 1)
                for c in range(2):
                    act.wait_ge(s_mm, hg * 2 + (c + 1))
                    A(scores(m, c), ps[4 * m + 2 + c][:, 0:nb * NK].rearrange("p (b n) -> p b n", n=NK),
                      ACT.Copy).then_inc(s_ev, 1)
                act.wait_ge(sm_in, hg + 1)
                A(ee[:, 0:nb, :], ee[:, 0:nb, :], ACT.Exp).then_inc(sm_exp, 1)

            keys_load(keys_nA)
            for g in range(4):
                act.wait_ge(mt_tr, g + 1)
                A(mgTA[:, 4 * g:4 * g + 4, :], ps[2 + g][:].rearrange("p (k t) -> p k t", t=P),
                  ACT.Copy).then_inc(mt_ev, 1)
            keys_out(0, 6)
            act.wait_ge(out1_free, 2 + 4)
            norm2_stats([0], sq_a)
            norm2_out([0])
            with act.Fori(0, PH // 2) as i:
                for m in range(2):
                    queries(i * 2 + m, m, 1, scoresA)

            def expert(U, k):
                one = slice(k, k + 1)
                act.wait_ge(u_used, U * TOP + (k + 1 + US))
                A(act_g[:, one], act_u[:, one], ACT.Gelu).then_inc(act_done, 1)
                act.wait_ge(act_done, U * TOP + (k + 1))
                A(act_w[:, one], act_g[:, one], ACT.Copy, scale=gate_all[:, bass.ds(U, 1), k]).then_inc(w_ready, 1)

            for name, U0 in (("ma", 0), ("mb", 2)):
                with act.Fori(U0, U0 + 2) as U:
                    for k in range(TOP):
                        expert(U, k)
                        if k % 4 == 2:
                            gates(name, (U - U0) * 4 + k // 4, sig, TB)
            with act.Fori(4, 6) as U:
                for k in range(TOP):
                    expert(U, k)
            act.wait_ge(out_free, 6 + 4 * NBB)
            act.dma_start(gbc2, norm2_g.broadcast_to([P, D])).then_inc(gbc_in, 16)
            norm2_stats(range(1, NB), sq_b)
            norm2_out(range(1, NB))
            keys_load(keys_n)
            keys_out(1, 0)
            with act.Fori(6, 8) as U:
                for k in range(TOP):
                    expert(U, k)
                    if k % 4 == 2:
                        queries(U * 4 + (PH - 24 + k // 4), k // 4 % 2, NBB, scoresB)

            act.wait_ge(idx2_ready, 1)
            act.dma_start(gbc_f, final_g.rearrange("(a d) -> a d", a=1).broadcast_to([P, D])).then_inc(gbc_in, 16)
            with act.Fori(0, (UNITS - PH) // 2) as i:
                for n in range(2 * TOP):
                    m, k = n // TOP, n % TOP
                    one = slice(k, k + 1)
                    act.wait_ge(u2_used, i * 2 * TOP + (n + 1 + SLOTS))
                    A(act_g2[:, m, one], act_u2[:, m, one], ACT.Gelu).then_inc(act2_done, 1)
                    act.wait_ge(act2_done, i * 4 * TOP + (2 * n + 1))
                    A(act_w2[:, m, one], act_g2[:, m, one], ACT.Copy,
                      scale=gate_all[:, bass.ds(i * 2 + (PH + m), 1), k]).then_inc(act2_done, 1)
                    act.wait_ge(act2_done, i * 4 * TOP + (2 * n + 2))
                    act.wait_ge(v2_used, i * 2 * TOP + (n + 1))
                    A(diag[:, n % SLOTS, :], ident[:], ACT.Copy, scale=act_w2[:, m, one]).then_inc(diag_ready, 1)

            act.wait_ge(mix_free, UNITS - PH + 2)
            for b in range(NB):
                A(sq_f, block_of(x2, b), ACT.Square, accum_out=small[:, 48 + b:49 + b]).then_inc(fin_sum, 1)
                act.wait_ge(fin_sum, b + 1)
            for b in range(NB):
                act.wait_ge(fin_ms, b + 1)
                A(small[:, 56 + b:57 + b], small[:, 52 + b:53 + b], ACT.Sqrt).then_inc(fin_root, 1)

        @block.vector
        def _(dve):
            V = nc.vector
            chain = Chain(dve, dve_chain)

            def mean_square(dst, src, n):
                return V.tensor_scalar(small[:, dst:dst + 1], small[:, src:src + 1], 1.0 / n, EPS, ALU.mult, ALU.add)

            def inverse(dst, src):
                return V.reciprocal(small[:, dst:dst + 1], small[:, src:src + 1])

            for name, p in pair.items():
                dve.sem_inc(p["use"], 1 if name[-1] == "1" else 2)
            dve.sem_inc(s_free, 2)
            dve.sem_inc(out1_free, 2)
            dve.sem_inc(out_free, 6)
            dve.sem_inc(u_used, US)
            dve.sem_inc(v_used, VS)
            dve.sem_inc(u2_used, SLOTS)
            dve.sem_inc(mix_free, 2)

            for g in range(2):
                dve.wait_ge(cols_tr, g + 1)
                V.tensor_copy(cols[:, 8 * g:8 * g + 8, :],
                              ps[g][:].rearrange("p (k r) -> p k r", r=64)[:, :, 0:ROWS]).then_inc(cols_done, 1)
            for b in range(NB):
                dve.wait_ge(n1_sum, b + 1)
                mean_square(4 + b, b, D).then_inc(n1_ms, 1)
            for b in range(NB):
                dve.wait_ge(n1_root, b + 1)
                chain.step(inverse(12 + b, 8 + b))
                V.tensor_scalar(xb[:, b, :], xb[:, b, :], small[:, 12 + b:13 + b], None, ALU.mult)\
                    .then_inc(n1_xn, 1)
            dve.wait_ge(cols_done, 2)
            for b in range(NB):
                for g in range(4):
                    n = b * 4 + g
                    dve.wait_ge(n1_tr, n + 1)
                    gain = cols[:, 4 * g:4 * g + 4, R_N1:R_N1 + 1].broadcast_to([P, 4, P])
                    V.tensor_tensor(hT[:, 4 * g:4 * g + 4, b * P:b * P + P],
                                    ps[n % 8][:].rearrange("p (k t) -> p k t", t=P), gain, ALU.mult)\
                        .then_inc(n1_done, 1)
            dve.wait_ge(consts, 5)
            dve.wait_ge(gbc_in, 16)

            with dve.Fori(0, HEADS) as h:
                chain.enter()
                for u in range(4):
                    d, m = u // 2, u % 2
                    bias = cols[:, bass.ds(h * MT + (8 * d + m), 1), R_GK]
                    dve.wait_ge(z_exp, h * 8 + (2 * u + 1))
                    chain.step(V.tensor_scalar(t_l, ps[4 + u][:], bias, 0.0, ALU.add, ALU.min))
                    dve.wait_ge(z_ln, h * 4 + (u + 1))
                    chain.step(V.tensor_tensor(t_l, t_l, t_abs, ALU.subtract))
                    chain.step(V.tensor_tensor_scan(t_b, reset, t_l, 0.0, ALU.mult, ALU.add))
                    b3 = t_b.rearrange("p (c t) -> p c t", t=P)
                    src = b3
                    if d:
                        chain.step(V.tensor_tensor(t_l, t_b, t_l, ALU.subtract))
                        src = t_l.rearrange("p (c t) -> p c t", t=P)
                    ref = src[:, :, REF]
                    chain.mark(V.tensor_tensor(t_d.rearrange("p (c t) -> p c t", t=P), src,
                                               src[:, :, REF:REF + 1].broadcast_to([P, NB, P]), ALU.subtract))
                    chain.step(V.tensor_tensor(dif, b3[:, :, P - 1], ref, ALU.subtract))
                    chain.step(V.tensor_tensor(dif[:, 0:3], dif[:, 0:3], src[:, 1:4, REF], ALU.add))
                    V.tensor_scalar(t_d, t_d, CLAMP, -CLAMP, ALU.min, ALU.max).then_inc(z_dif, 1)
                    dve.wait_ge(z_dec, h * 12 + (3 * u + 3))
                    dve.wait_ge(q_ev, h * 4 + 4)
                    chain.mark(V.tensor_tensor(qm[:, d, m, :], qT[:, m, :], t_e, ALU.mult))
                    chain.wait()
                    V.tensor_tensor(km[:, d, m, :], kT[:, m, :], t_d, ALU.mult).then_inc(z_qk, 1)
                for b in range(NB):
                    dve.wait_ge(og_ev, h * 4 + (b + 1))
                    V.tensor_tensor(og_s[:, b, :], og_s[:, b, :], gbc_o[:, bass.ds(h * DV, DV)], ALU.mult)\
                        .then_inc(og_scaled, 1)
                for j, c in enumerate((3, 2, 1)):
                    for m in range(MT):
                        dve.wait_ge(ub_mm, h * 6 + (2 * j + m + 1))
                        bank = ps[2 * (j % 2) + m][:]
                        if c < 3:
                            dve.wait_ge(ub_done, h * 6 + (2 * j - 1 + m))
                            chain.step(V.tensor_tensor(st_b[:, c - 1, m, :], bank, st_b[:, c, m, :], ALU.add))
                            bank = st_b[:, c - 1, m, :]
                        V.tensor_scalar(st_b[:, c - 1, m, :], bank, dec[:, 2 + m, c - 1:c], None, ALU.mult)\
                            .then_inc(ub_done, 1)

                def merge_scores(c):
                    dve.wait_ge(sc_mm, h * 4 + (c + 1))
                    if c >= 2:
                        dve.wait_ge(o_mm, h * 4 + (c - 1))
                    bank = ps[4 + c % 2]
                    chain.step(V.tensor_copy(p_t[:, c % 2, :], bank[:, P:2 * P]))
                    V.copy_predicated(p_t[:, c % 2, :], causal.bitcast(U32), bank[:, 0:P]).then_inc(sc_done, 1)

                merge_scores(0)
                for c in range(NB):
                    if c < NB - 1:
                        merge_scores(c + 1)
                        for m in range(MT):
                            dve.wait_ge(uf_mm, h * 6 + (2 * c + m + 1))
                            new = st_f[:, (c + 1) % 2, m, :]
                            bank = ps[m][:]
                            if c >= 1:
                                dve.wait_ge(uf_done, h * 6 + (2 * c - 1 + m))
                                if c >= 2:
                                    dve.wait_ge(o_mm, h * 4 + c)
                                chain.step(V.tensor_tensor(new, bank, st_f[:, c % 2, m, :], ALU.add))
                                bank = new
                            V.tensor_scalar(new, bank, dec[:, m, c:c + 1], None, ALU.mult).then_inc(uf_done, 1)
                    dve.wait_ge(o_sum, h * 4 + (c + 1))
                    mean_square(20 + c, 16 + c, DV).then_inc(o_ms, 1)
                    dve.wait_ge(o_root, h * 4 + (c + 1))
                    chain.step(inverse(28 + c, 24 + c))
                    if c >= 2:
                        dve.wait_ge(ot_tr, h * 4 + (c - 1))
                    V.scalar_tensor_tensor(on[:, c % 2, :], ps[6 + c % 2][:], small[:, 28 + c:29 + c],
                                           og_s[:, c, :], ALU.mult, ALU.mult).then_inc(o_norm, 1)
                chain.leave()

            chain.step(V.memset(upad, 0.0))
            with dve.Fori(0, KT // 2) as i:
                chain.enter()
                p = pair["cv"]
                for m in range(2):
                    dve.wait_ge(p["val"], i * 2 + (m + 1))
                    dve.wait_ge(p["sig"], i * 2 + (m + 1))
                    V.tensor_tensor(upad[:, m, PAD:PAD + T], ps[2 + m][:], sig_c[:, m, :], ALU.mult)\
                        .then_inc(p["use"], 1)
                    dve.wait_ge(p["use"], i * 2 + (m + 3))
                    dst = cv[:, bass.ds(i * 2 + m, 1), :].rearrange("p a t -> p (a t)")

                    def tap(r):
                        return cols[:, bass.ds(i * 2 + m, 1), r]

                    chain.step(V.tensor_scalar(dst, upad[:, m, 0:T], tap(R_CW), tap(R_CB), ALU.mult, ALU.add))
                    for r in range(1, TAPS):
                        ins = V.scalar_tensor_tensor(dst, upad[:, m, r:r + T], tap(R_CW + r), dst, ALU.mult, ALU.add)
                        if r < TAPS - 1:
                            chain.step(ins)
                    ins.then_inc(cv_done, 1)
                chain.leave()
            dve.wait_ge(cv_done, KT)

            def merge1(name, start, end):
                p = pair[name]
                with dve.Fori(start, end) as g:
                    dst = mgA[:, bass.ds(g * 512, 512)]
                    dve.wait_ge(p["val"], g + 1)
                    dve.wait_ge(p["sig"], g + 1)
                    V.tensor_tensor(dst if name == "ma1" else tmpA, ps[1][:], sigA, ALU.mult).then_inc(p["use"], 1)
                    dve.wait_ge(p["use"], g + 2)
                    if name == "mb1":
                        V.tensor_tensor(dst, tmpA, dst, ALU.add).then_inc(mb1_done, 1)
                        dve.wait_ge(mb1_done, g + 1)

            merge1("ma1", 0, 2)
            dve.wait_ge(ln_sum, 1)
            for t in range(KT):
                V.tensor_tensor(cv[:, t, :], cv[:, t, :], ps[4][:], ALU.subtract).then_inc(ln_xc, 1)
            merge1("ma1", 2, 4)
            dve.wait_ge(ln_varu, KT)
            V.tensor_scalar(rstd_ln, ps[5][:], EPS, None, ALU.add).then_inc(ln_ms, 1)
            dve.wait_ge(ln_root, 1)
            chain.step(V.reciprocal(rstd_ln, root_ln))
            for lo, hi in ((0, TA), (TA, T)):
                for t in range(KT):
                    V.tensor_tensor(cv[:, t, lo:hi], cv[:, t, lo:hi], rstd_ln[:, lo:hi], ALU.mult)\
                        .then_inc(ln_scaled, 1)
            merge1("mb1", 0, 4)

            dve.wait_ge(res_in, 16)
            with dve.Fori(0, 2) as i:
                for g in range(2):
                    dve.wait_ge(out1_mm, i * 2 + (g + 1))
                    dst = x2[:, bass.ds(i * 8 + g * 4, 4), 0:P]
                    V.tensor_tensor(dst, by_tile(ps[g][:]), dst, ALU.add).then_inc(out1_free, 1)

            def norm2(blocks):
                for b in blocks:
                    dve.wait_ge(n2_sum, b + 1)
                    mean_square(36 + b, 32 + b, D).then_inc(n2_ms, 1)
                for b in blocks:
                    dve.wait_ge(n2_root, b + 1)
                    chain.step(inverse(44 + b, 40 + b))
                    V.scalar_tensor_tensor(block_of(h2, b), block_of(x2, b), small[:, 44 + b:45 + b],
                                           by_tile(gbc2), ALU.mult, ALU.mult).then_inc(n2_h, 1)

            dve.wait_ge(gbc_in, 32)
            norm2([0])
            chain.step(V.memset(idx_all[:, UNITS, :], 0))

            idx4 = idx_all[:, 0:UNITS, :].rearrange("p (b h) k -> p b h k", h=PH)
            gate4 = gate_all[:, 0:UNITS, :].rearrange("p (b h) k -> p b h k", h=PH)

            def top16(values, v16, i16):
                chain.step(V.max(v16[:, 0:8], values))
                chain.step(V.max_index(i16[:, 0:8], v16[:, 0:8], values))
                rep = s_rep if values.shape[-1] == NK else cand2
                chain.step(V.match_replace(rep, v16[:, 0:8], values, LOW))
                chain.step(V.max(v16[:, 8:16], rep))
                chain.step(V.max_index(i16[:, 8:16], v16[:, 8:16], rep))

            def topk(hg, head, m, nb, b0, scores):
                hold(dve, s_ev, hg * 2 + 2, dve_passed)
                for c in range(2):
                    for b in range(nb):
                        top16(scores(m, c)[:, b, :], vals[:, c * nb + b, :], idx_u[:, c * nb + b, :])
                V.tensor_copy(idxf[:, 0:2 * nb, :], idx_u[:, 0:2 * nb, :]).then_inc(s_free, 1)
                dve.wait_ge(s_free, hg + 3)
                for b in range(nb):
                    c3 = cand.rearrange("p (a b) -> p a b", b=TOP)
                    chain.step(V.tensor_tensor(
                        c3, vals[:, b, :].unsqueeze(2).broadcast_to([P, TOP, TOP]),
                        vals[:, nb + b, :].unsqueeze(1).broadcast_to([P, TOP, TOP]), ALU.add))
                    top16(cand, best[:, b, :], pos_u[:, b, :])
                n = slice(0, nb)
                V.tensor_tensor(ee[:, n], best[:, n], best[:, n, 0:1].broadcast_to([P, nb, TOP]),
                                ALU.subtract).then_inc(sm_in, 1)
                chain.mark(V.tensor_scalar(pos_a[:, n], pos_u[:, n], 4, None, ALU.logical_shift_right))
                chain.step(V.tensor_scalar(pos_b[:, n], pos_u[:, n], TOP - 1, None, ALU.bitwise_and))
                chain.mark(V.tensor_copy(pa[:, n], pos_a[:, n]))
                chain.step(V.tensor_copy(pb[:, n], pos_b[:, n]))
                for c, (place, got) in enumerate(((pa, ia), (pb, ib))):
                    for b in range(nb):
                        chain.step(V.tensor_tensor(
                            onehot, iota16[:].unsqueeze(1).broadcast_to([P, TOP, TOP]),
                            place[:, b, :].unsqueeze(2).broadcast_to([P, TOP, TOP]), ALU.is_equal))
                        chain.step(V.tensor_tensor(
                            picked, onehot, idxf[:, c * nb + b, :].unsqueeze(1).broadcast_to([P, TOP, TOP]),
                            ALU.mult))
                        chain.step(V.tensor_reduce(got[:, b, :], picked, AX.X, ALU.add))

                def place_in(a):
                    return a[:, 0:UNITS, :].rearrange("p (b h) k -> p b h k", h=PH)[
                        :, b0:b0 + nb, bass.ds(head, 1), :].rearrange("p b h k -> p b (h k)")

                chain.step(V.scalar_tensor_tensor(place_in(idx_all), ia[:, n], float(NK), ib[:, n],
                                                  ALU.mult, ALU.add))
                dve.wait_ge(sm_exp, hg + 1)
                chain.step(V.tensor_reduce(es[:, n], ee[:, n], AX.X, ALU.add))
                chain.step(V.reciprocal(es[:, n], es[:, n]))
                chain.step(V.tensor_tensor(place_in(gate_all), ee[:, n],
                                           es[:, n].unsqueeze(2).broadcast_to([P, nb, TOP]), ALU.mult))

            with dve.Fori(0, PH // 2) as i:
                chain.enter()
                for m in range(2):
                    topk(i * 2 + m, i * 2 + m, m, 1, 0, scoresA)
                chain.leave()

            def dot(U, k):
                s = k % US
                dve.wait_ge(u_ready[s], U * (16 * TOP // US) + 16 * (k // US + 1))
                row = by_tile(u_row[s])
                V.scalar_tensor_tensor(row, row, 1.0, block_of(h2, 0), ALU.mult, ALU.mult,
                                       accum_out=act_u[:, k:k + 1]).then_inc(u_used, 1)

            def add_row(U, k):
                s = k % VS
                dve.wait_ge(w_ready, U * TOP + (k + 1))
                dve.wait_ge(v_ready[s], U * (16 * TOP // VS) + 16 * (k // VS + 1))
                dve.wait_ge(v_used, U * TOP + (k + VS))
                V.scalar_tensor_tensor(block_of(x2, 0), by_tile(v_row[s]), act_w[:, k:k + 1], block_of(x2, 0),
                                       ALU.mult, ALU.add).then_inc(v_used, 1)

            def unit(U, after):
                for k in range(TOP):
                    dot(U, k)
                    if k:
                        add_row(U, k - 1)
                    if k == TOP // 2:
                        nxt = U + 1
                        V.tensor_copy(idx_cur[:, bass.ds(nxt % 2, 1), :], idx_all[:, bass.ds(nxt, 1), :])\
                            .then_inc(idx_ready, 1)
                    after(k)
                add_row(U, TOP - 1)

            V.tensor_copy(idx_cur[:, 0, :], idx_all[:, 0, :]).then_inc(idx_ready, 1)
            for name, U0 in (("ma", 0), ("mb", 2)):
                p = pair[name]
                with dve.Fori(U0, U0 + 2) as U:

                    def merge(k):
                        if k % 4 != 3:
                            return
                        i = (U - U0) * 4 + k // 4
                        for m in range(2):
                            d1 = mgT1[:, bass.ds(i * 2 + m, 1), :].rearrange("p a t -> p (a t)")
                            d23 = mgT23[:, bass.ds(i * 2 + m, 1), :].rearrange("p a t -> p (a t)")
                            dve.wait_ge(p["val"], i * 2 + (m + 1))
                            dve.wait_ge(p["sig"], i * 2 + (m + 1))
                            if name == "ma":
                                V.tensor_tensor(d1, ps[2 + m][:, 0:P], sig[:, m, 0:P], ALU.mult)
                                V.tensor_tensor(d23, ps[2 + m][:, P:TB], sig[:, m, P:TB], ALU.mult)\
                                    .then_inc(p["use"], 1)
                                dve.wait_ge(p["use"], i * 2 + (m + 3))
                            else:
                                V.tensor_tensor(mtmp, ps[2 + m][:, 0:TB], sig[:, m, :], ALU.mult)\
                                    .then_inc(p["use"], 1)
                                dve.wait_ge(p["use"], i * 2 + (m + 3))
                                V.tensor_tensor(d1, mtmp[:, 0:P], d1, ALU.add)
                                V.tensor_tensor(d23, mtmp[:, P:TB], d23, ALU.add).then_inc(mb_done, 1)
                                dve.wait_ge(mb_done, i * 2 + (m + 1))

                    unit(U, merge)
            dve.wait_ge(res_in, 16 * NB)
            with dve.Fori(4, 6) as U:

                def residual(k):
                    if k % 8 != 7:
                        return
                    g = k // 8
                    for b in range(NBB):
                        dve.wait_ge(out_mm, (U - 4) * (2 * NBB) + (g * NBB + b + 1))
                        dst = x2[:, bass.ds((U - 4) * 8 + g * 4, 4), (b + 1) * P:(b + 2) * P]
                        V.tensor_tensor(dst, by_tile(ps[g * NBB + b][:]), dst, ALU.add).then_inc(out_free, 1)

                unit(U, residual)
            dve.wait_ge(gbc_in, 48)
            norm2(range(1, NB))
            with dve.Fori(6, 8) as U:
                chain.enter()

                def pick(k):
                    if k % 4 == 3:
                        topk(U * 4 + (PH - 24 + k // 4), U * 4 + (k // 4 - 24), k // 4 % 2, NBB, 1, scoresB)

                unit(U, pick)
                chain.leave()

            V.tensor_copy(idx_cur2[:, 0, :], idx_all[:, PH, :]).then_inc(idx2_ready, 1)
            with dve.Fori(1, NB) as b:
                with dve.Fori(0, PH // 2) as j:
                    lu = b * PH + j * 2 - PH
                    for n in range(2 * TOP):
                        m, k = n // TOP, n % TOP
                        s = n % SLOTS
                        dve.wait_ge(u2_ready[s], lu * (16 * TOP // SLOTS) + 16 * (n // SLOTS + 1))
                        row = by_tile(u2_row[s])
                        V.scalar_tensor_tensor(row, row, 1.0, block_of(h2, b), ALU.mult, ALU.mult,
                                               accum_out=act_u2[:, m, k:k + 1]).then_inc(u2_used, 1)
                        if k == TOP // 2:
                            dve.wait_ge(v2_used, lu * TOP + (m * TOP + SLOTS))
                            V.tensor_copy(idx_cur2[:, 1 - m, :], idx_all[:, bass.ds(lu + (PH + m + 1), 1), :]
                                          .rearrange("p a k -> p (a k)")).then_inc(idx2_ready, 1)
                        if k == TOP - 1:
                            dve.wait_ge(v2_used, lu * TOP + ((m + 1) * TOP + SLOTS))
                            for q in range(4):
                                dst = x2[:, 4 * q:4 * q + 4, bass.ds(b * P, P)]
                                ins = V.tensor_tensor(dst, by_tile(ps[4 * m + q][:]), dst, ALU.add)
                            ins.then_inc(mix_free, 1)
                            dve.wait_ge(mix_free, lu + (m + 3))

            for b in range(NB):
                dve.wait_ge(fin_sum, b + 1)
                mean_square(52 + b, 48 + b, D).then_inc(fin_ms, 1)
            dve.wait_ge(gbc_in, 64)
            for b in range(NB):
                dve.wait_ge(fin_root, b + 1)
                chain.step(inverse(60 + b, 56 + b))
                V.scalar_tensor_tensor(by_tile(y_out[:, b, :]), block_of(x2, b), small[:, 60 + b:61 + b],
                                       by_tile(gbc_f), ALU.mult, ALU.mult).then_inc(fin_y, 1)

        @block.tensor
        def _(pe):
            M = nc.tensor.matmul

            def transposes(banks_first, n_banks, src, done, ready):
                for g in range(n_banks):
                    ready(g)
                    for q in range(4):
                        last = nc.tensor.transpose(ps[(banks_first + g) % 8][:, q * P:q * P + P],
                                                   src(4 * g + q), ident[:])
                    last.then_inc(done, 1)

            def slab_ready(n, i=None, per=0):
                if i is None:
                    pe.wait_ge(w_in_slot[n % 2], 16 * (n // 2 + 1))
                else:
                    pe.wait_ge(w_in_slot[n % 2], i * (8 * per) + 16 * (n // 2 + 1))

            pe.sem_inc(w_used, 2)
            pe.sem_inc(v2_used, SLOTS)

            pe.wait_ge(consts, 2)
            pe.wait_ge(rows_in, 16 * 7)
            for g in range(2):
                for q in range(8):
                    last = nc.tensor.transpose(ps[g][:, 64 * q:64 * q + ROWS],
                                               rows[:, (8 * g + q) * P:(8 * g + q + 1) * P], ident[0:ROWS, 0:ROWS])
                last.then_inc(cols_tr, 1)
            pe.wait_ge(cols_done, 2)
            for b in range(NB):
                pe.wait_ge(n1_xn, b + 1)

                def ready(g):
                    if b * 4 + g >= 8:
                        pe.wait_ge(n1_done, b * 4 + g - 7)

                transposes(b * 4, 4, lambda t: xb[:, b, t * P:t * P + P], n1_tr, ready)
            pe.wait_ge(n1_done, 16)
            pe.wait_ge(wgk_in, 16)
            for d in range(2):
                for k in range(KT):
                    last = M(ps[d][0:RANK, :], wgk[:, k, d * RANK:d * RANK + RANK], hT[:, k, :],
                             start=k == 0, stop=k == KT - 1)
                last.then_inc(glow_mm, 1)
            pe.wait_ge(glow_done, 2)

            def project(slot, m, act_in, bank, done, lo=0, hi=T):
                for k in range(KT):
                    last = M(ps[bank][:, 0:hi - lo], w_slot(slot)[:, k, m * P:m * P + P], act_in[:, k, lo:hi],
                             start=k == 0, stop=k == KT - 1)
                last.then_inc(done, 1)
                return last

            with pe.Fori(0, HEADS) as h:
                for s in range(2):
                    slab_ready(s, h, HEAD_SLABS)
                    for m in range(MT):
                        project(s, m, hT, 2 * s + m, q_mm)
                    pe.drain().then_inc(w_used, 1)
                pe.wait_ge(gkw_in, h * 32 + 32)
                for u in range(4):
                    M(ps[4 + u][:], gkw[:, u // 2, (u % 2) * P:(u % 2) * P + P], glow[:, u // 2, :],
                      start=True, stop=True).then_inc(z_mm, 1)
                pe.wait_ge(q_ev, h * 4 + 4)
                for first, bank0, done in ((2, 0, v_mm), (4, 4, og_mm)):
                    if bank0:
                        pe.wait_ge(z_dif, h * 4 + 4)
                    for s in range(2):
                        slab_ready(first + s, h, HEAD_SLABS)
                        for k in range(KT // 2):
                            kk = s * (KT // 2) + k
                            for b in range(NB):
                                last = M(ps[bank0 + b][:], hT[:, kk, b * P:b * P + P], w_slot_half(s)[:, k, :],
                                         start=kk == 0, stop=kk == KT - 1)
                                if kk == KT - 1:
                                    last.then_inc(done, 1)
                        pe.drain().then_inc(w_used, 1)
                pe.wait_ge(z_qk, h * 4 + 4)
                pe.wait_ge(v_ev, h * 4 + 4)
                for u in range(4):
                    for c in range(NB):
                        last = nc.tensor.transpose(ps[u][:, c * P:c * P + P],
                                                   km[:, u // 2, u % 2, c * P:c * P + P], ident[:])
                    last.then_inc(kt_tr, 1)
                pe.wait_ge(kt_ev, h * 4 + 4)
                for j, c in enumerate((3, 2, 1)):
                    if j == 2:
                        pe.wait_ge(ub_done, h * 6 + 2)
                    for m in range(MT):
                        M(ps[2 * (j % 2) + m][:], kmT[:, c, 1, m * P:m * P + P], v_tok[:, c, :],
                          start=True, stop=True).then_inc(ub_mm, 1)

                def scores(c):
                    if c >= 2:
                        pe.wait_ge(sc_done, h * 4 + (c - 1))
                    for d in range(2):
                        for m in range(MT):
                            last = M(ps[4 + c % 2][:, d * P:d * P + P], km[:, d, m, c * P:c * P + P],
                                     qm[:, d, m, c * P:c * P + P], start=m == 0, stop=m == MT - 1)
                    last.then_inc(sc_mm, 1)

                def heads_out(c):
                    pe.wait_ge(o_norm, h * 4 + (c + 1))
                    if c >= 2:
                        pe.wait_ge(ot_ev, h * 4 + (c - 1))
                    for q in range(4):
                        last = nc.tensor.transpose(ps[2 + c % 2][:, q * P:q * P + P],
                                                   on[:, c % 2, q * P:q * P + P], ident[:])
                    last.then_inc(ot_tr, 1)

                pe.wait_ge(og_ev, h * 4 + 4)
                scores(0)
                pe.wait_ge(ub_done, h * 6 + 6)
                for c in range(NB):
                    if c < NB - 1:
                        scores(c + 1)
                        if c:
                            pe.wait_ge(uf_done, h * 6 + 2 * c)
                        for m in range(MT):
                            M(ps[m][:], kmT[:, c, 0, m * P:m * P + P], v_tok[:, c, :],
                              start=True, stop=True).then_inc(uf_mm, 1)
                    terms = []
                    if c < NB - 1:
                        terms += [(qm[:, 1, m, c * P:c * P + P], st_b[:, c, m, :]) for m in range(MT)]
                    if c > 0:
                        terms += [(qm[:, 0, m, c * P:c * P + P], st_f[:, c % 2, m, :]) for m in range(MT)]
                    terms.append((p_t[:, c % 2, :], v_tok[:, c, :]))
                    if c:
                        pe.wait_ge(uf_done, h * 6 + 2 * c)
                    if c >= 2:
                        pe.wait_ge(o_norm, h * 4 + (c - 1))
                    pe.wait_ge(sc_done, h * 4 + (c + 1))
                    for n, (lhs, rhs) in enumerate(terms):
                        last = M(ps[6 + c % 2][:], lhs, rhs, start=n == 0, stop=n == len(terms) - 1)
                    last.then_inc(o_mm, 1)
                    if c:
                        heads_out(c - 1)
                heads_out(NB - 1)
                pe.wait_ge(ot_ev, h * 4 + 4)

            def pairs(name, first, val_in, lo):
                p = pair[name]
                with pe.Fori(0, KT // 2) as i:
                    slab_ready(first, i, 2)
                    for m in range(2):
                        pe.wait_ge(p["use"], i * 2 + (m + 1))
                        project(0, m, hT, m, p["gate"], lo)
                    pe.drain().then_inc(w_used, 1)
                    slab_ready(first + 1, i, 2)
                    for m in range(2):
                        project(1, m, val_in, 2 + m, p["val"], lo)
                    pe.drain().then_inc(w_used, 1)

            def pairs1(name, first, start, end, val_in):
                p = pair[name]
                with pe.Fori(start, end) as g:
                    pe.wait_ge(p["use"], g + 1)
                    for j, (src, done) in enumerate(((hT, p["gate"]), (val_in, p["val"]))):
                        for s in range(2):
                            slab_ready(first + 2 * j + s, g, 4)
                            for k in range(KT // 2):
                                kk = s * (KT // 2) + k
                                last = M(ps[j][:], src[:, kk, 0:TA], w_slot_half(s)[:, k, :],
                                         start=kk == 0, stop=kk == KT - 1)
                            if s:
                                last.then_inc(done, 1)
                            pe.drain().then_inc(w_used, 1)

            pairs("cv", SB_CONV, hT, 0)
            pe.wait_ge(pair["cv"]["use"], KT + 2)
            pairs1("ma1", SB_MA1, 0, 2, oT)
            pe.wait_ge(cv_done, KT)
            for t in range(KT):
                last = M(ps[4][:], ones_d[:], cv[:, t, :], start=t == 0, stop=t == KT - 1)
            last.then_inc(ln_sum, 1)
            pairs1("ma1", SB_MA1, 2, 4, oT)
            for t in range(KT):
                pe.wait_ge(ln_sq, t + 1)
                last = M(ps[5][:], ones_d[:], sqr[:, t % 2, :], start=t == 0, stop=t == KT - 1)
                last.then_inc(ln_varu, 1)
            pe.wait_ge(pair["ma1"]["use"], 4 + 1)
            pe.wait_ge(ln_act, KT)
            pairs1("mb1", SB_MB1, 0, 4, cv)

            pe.wait_ge(mb1_done, 4)
            pe.wait_ge(ln_ms, 1)
            transposes(2, 4, lambda t: mgA[:, t * P:t * P + P], mt_tr, lambda g: None)
            pe.wait_ge(keys_in, 16)
            transposes(6, 4, lambda t: keys_nA[:, t, :], keys_tr, lambda g: None)
            pe.wait_ge(mt_ev, 4)
            pe.wait_ge(keys_ev, 4)

            def project_out(i, first, lhs, nb, done, free):
                for g in range(2):
                    for s in range(2):
                        slab_ready(first + 2 * g + s, i, 4)
                        for k in range(KT // 2):
                            kk = s * (KT // 2) + k
                            for b in range(nb):
                                if kk == 0:
                                    pe.wait_ge(free, i * (2 * nb) + (g * nb + b + 1))
                                last = M(ps[g * nb + b][:], lhs(kk, b), w_slot_half(s)[:, k, :],
                                         start=kk == 0, stop=kk == KT - 1)
                                if kk == KT - 1:
                                    last.then_inc(done, 1)
                        pe.drain().then_inc(w_used, 1)

            with pe.Fori(0, 2) as i:
                project_out(i, SB_OUT1, lambda kk, b: mgTA[:, kk, :], 1, out1_mm, out1_free)

            def norm2_turn(blocks):
                for b in blocks:
                    pe.wait_ge(n2_h, b + 1)

                    def ready(g):
                        if b * 4 + g >= 8:
                            pe.wait_ge(n2_ev, b * 4 + g - 7)

                    transposes(b * 4, 4, lambda t: h2[:, t, b * P:b * P + P], n2_tr, ready)

            def query(hg, first, i, per, m, lo, nb):
                slab_ready(first, i, per)
                for c in range(2):
                    project(m, c, h2T, 4 * m + c, pq_mm, lo, lo + nb * P)
                pe.drain().then_inc(w_used, 1)
                for c in range(2):
                    pe.wait_ge(pq_ev, hg * 2 + (c + 1))
                    key = keysT[:, bass.ds((hg % PH) * 2 + c, 1), :].rearrange("p a n -> p (a n)")
                    for b in range(nb):
                        last = M(ps[4 * m + 2 + c][:, b * NK:b * NK + NK], qh[:, c, b * P:b * P + P], key,
                                 start=True, stop=True)
                    last.then_inc(s_mm, 1)

            norm2_turn([0])
            pe.wait_ge(n2_ev, 4)
            with pe.Fori(0, PH // 2) as i:
                for m in range(2):
                    query(i * 2 + m, SB_WQ1 + m, i, 2, m, 0, 1)

            pe.wait_ge(s_ev, 2 * PH)
            pairs("ma", SB_MA, oT, TA)
            pe.wait_ge(pair["ma"]["use"], KT + 2)
            pairs("mb", SB_MB, cv, TA)
            pe.wait_ge(mb_done, KT)

            def merged(kk, b):
                return mgT1[:, kk, :] if b == 0 else mgT23[:, kk, (b - 1) * P:b * P]

            with pe.Fori(0, 2) as i:
                project_out(i, SB_OUT, merged, NBB, out_mm, out_free)
            norm2_turn(range(1, NB))
            pe.wait_ge(keys_in, 32)
            pe.wait_ge(n2_ev, 16)
            transposes(0, 4, lambda t: keys_n[:, t, :], keys_tr, lambda g: None)
            pe.wait_ge(keys_ev, 8)
            with pe.Fori(0, PH // 2) as i:
                for m in range(2):
                    query(i * 2 + (PH + m), SB_WQ + m, i, 2, m, TA, NBB)

            with pe.Fori(0, (UNITS - PH) // 2) as i:
                for n in range(2 * TOP):
                    m, k = n // TOP, n % TOP
                    s = n % SLOTS
                    if k == 0:
                        pe.wait_ge(mix_free, i * 2 + (m + 1))
                    pe.wait_ge(v2_ready[s], i * (32 * TOP // SLOTS) + 16 * (n // SLOTS + 1))
                    pe.wait_ge(diag_ready, i * 2 * TOP + (n + 1))
                    for q in range(4):
                        last = M(ps[4 * m + q][:], diag[:, s, :], v2_row[s][:, q * 512:q * 512 + 512],
                                 start=k == 0, stop=k == TOP - 1)
                    last.then_inc(v2_used, 1)


_INS = ["x", "norm1_g", "w_in", "gla_gk_fwd_w", "gla_gk_fwd_b", "gla_gk_bwd_w", "gla_gk_bwd_b", "gla_onorm_g",
        "gla_w_o", "conv_w", "conv_b", "conv_ln_g", "conv_ln_b", "conv_w_pw2", "w_out", "norm2_g", "peer_w_q",
        "peer_keys", "peer_u", "peer_v", "final_norm_g"]


def kernel(**inputs):
    import numpy as np
    import concourse.bacc as bacc
    from concourse import mybir as mb
    from concourse.bass_utils import run_bass_kernel_spmd

    nc = bacc.Bacc("TRN2", target_bir_lowering=False, num_devices=1)
    arrays, args = {}, []
    for name in _INS:
        a = np.ascontiguousarray(inputs[name])
        arrays["in_" + name] = a
        args.append(nc.dram_tensor("in_" + name, a.shape, mb.dt.from_np(a.dtype), kind="ExternalInput").ap())
    out = nc.dram_tensor("out_0", (1, T, D), mb.dt.float32, kind="ExternalOutput").ap()
    hybrid_block(nc, *args, out)
    r = run_bass_kernel_spmd(nc, [arrays], core_ids=[0])
    return r.results[0]["out_0"]
```

```python
import concourse.bass as bass
from concourse import mybir
from contextlib import ExitStack
import numpy as np

P = 128
F32 = mybir.dt.float32
U32 = mybir.dt.uint32
I32 = mybir.dt.int32
ALU = mybir.AluOpType
ACT = mybir.ActivationFunctionType
AX = mybir.AxisListType

D = 2048
T = 512
KT = D // P
NB = T // P
HEADS = 4
DK = 256
DV = 512
MT = DK // P
RANK = 16
TAPS = 31
PAD = TAPS // 2
EPS = 1e-6
PH = 8
NK = 128
TOP = 16
REF = P // 2
CLAMP = 16.0 * 80.0
LOW = -3.0e38

OQ, OK_, OV, OG = 0, 1024, 2048, 4096
OGK = 6144
OGLU = 6176
OGATE = OGLU + 2048
OGA = OGLU + 4096
OGB = OGA + 2048

R_N1, R_CB, R_LG, R_LB, R_CW = 0, 1, 2, 3, 4
R_GK = R_CW + TAPS
ROWS = R_GK + 1

TA = P
TB = T - TA
NBB = NB - 1

HEAD_SLABS = 6
SB_CONV = HEADS * HEAD_SLABS
SB_MA1 = SB_CONV + KT
SB_MB1 = SB_MA1 + 16
SB_OUT1 = SB_MB1 + 16
SB_WQ1 = SB_OUT1 + 8
SB_MA = SB_WQ1 + PH
SB_MB = SB_MA + KT
SB_OUT = SB_MB + KT
SB_WQ = SB_OUT + 8
SLAB = 4096
UNITS = NB * PH
SIDE = 2 * PH
US, VS = 2, 4
SLOTS = 4

PLAN_FIRST = ((0, 3, 8, 13), (0, 4, 9, 14))
PLAN_3 = ((2, 7, 12), (4, 9, 14))
PLAN_LAST = ((), (4,))
COPY_AT = 11
EXP_AT = 11
GATE_OUT_AT = 12
SCORES_AT = 13
QUERY_FROM, QUERY_STEP = 4, 4


class Chain:

    def __init__(self, eng, sem):
        self.eng, self.sem, self.n = eng, sem, 0

    def enter(self):
        self.start = self.n

    def leave(self):
        self.wait()
        self.eng.sem_inc(self.sem, self.start - self.n)
        self.n = self.start

    def mark(self, ins):
        self.n += 1
        ins.then_inc(self.sem, 1)

    def wait(self, but=0):
        self.eng.wait_ge(self.sem, self.n - but)

    def step(self, ins):
        self.mark(ins)
        self.wait()


def hold(eng, sem, value, passed):
    eng.wait_ge(sem, value)
    eng.sem_inc(passed, 1)


def hybrid_block(nc, x, norm1_g, w_in, gk_f_w, gk_f_b, gk_b_w, gk_b_b, onorm_g, w_o, conv_w, conv_b,
                 ln_g, ln_b, w_pw2, w_out, norm2_g, w_q, keys, u_tab, v_tab, final_g, out):
    def slabs(w, half):
        w2 = w[0]
        if half:
            return w2.rearrange("(s k p) n -> s p k n", p=P, s=2)
        return w2.rearrange("(k p) n -> p k n", p=P)

    ctx = ExitStack()
    with ctx:
        def sb(name, shape, dt=F32):
            return ctx.enter_context(nc.sbuf_tensor(name, shape, dt))

        def sem(name):
            return ctx.enter_context(nc.semaphore(name))

        def view(t, off, *shape):
            n = 1
            for s in shape:
                n *= s
            a = t[:, off:off + n]
            if len(shape) == 2:
                a = a.rearrange("p (a b) -> p a b", b=shape[1])
            elif len(shape) == 3:
                a = a.rearrange("p (a b c) -> p a b c", b=shape[1], c=shape[2])
            return a

        arena_h = sb("arena_h", [P, KT * T])
        arena_o = sb("arena_o", [P, KT * T])
        YB = KT * T
        arena_c = sb("arena_c", [P, YB + 17664])
        wring = sb("wring", [P, 2 * SLAB])
        ident = sb("ident", [P, P])
        ones_d = sb("ones_d", [P, P])
        iota_i = sb("iota_i", [P, TOP], I32)
        iota16 = sb("iota16", [P, TOP])
        cols = sb("cols", [P, KT, ROWS])
        small = sb("small", [P, 64])
        idx_all = sb("idx_all", [P, UNITS + 1, TOP], U32)
        gate_all = sb("gate_all", [P, UNITS, TOP])

        hT = view(arena_h, 0, KT, T)
        h2T = view(arena_h, 0, KT, T)
        mgT1 = view(arena_h, 0, KT, T)[:, :, 0:P]
        oT = view(arena_o, 0, KT, T)
        x2 = view(arena_o, 0, KT, T)
        cv = view(arena_c, 0, KT, T)
        h2 = view(arena_c, 0, KT, T)

        xb = view(arena_c, 0, NB, D)
        sq_x = view(arena_c, 8192, D)
        rows = arena_c[0:ROWS, 10240:10240 + D]
        wgk = view(arena_c, 12800, KT, 32 + RANK)
        o_ = [0]

        def take(*shape):
            n = 1
            for d in shape:
                n *= d
            a = view(arena_c, o_[0], *shape)
            o_[0] += n
            return a

        qT = take(MT, T)
        kT = take(MT, T)
        v_tok = take(NB, DV)
        og_s = take(NB, DV)
        qm = take(2, MT, T)
        km = take(2, MT, T)
        kmT = take(NB, 2, DK)
        st_b = take(3, MT, DV)
        st_f = take(2, MT, DV)
        t_abs = take(T)
        t_l = take(T)
        t_b = take(T)
        t_d = take(T)
        t_e = take(T)
        on = take(2, DV)
        p_t = take(2, P)
        dec = take(4, 4)
        dif = take(4)
        causal = take(P)
        reset = take(T)
        gbc_o = take(D)
        gkw = take(DK)
        glow = take(T)
        assert o_[0] <= YB + 17664, o_[0]
        upad = view(arena_c, YB, 2, T + 2 * PAD)
        sig_c = view(arena_c, YB + 1088, 2, T)
        RU, RV, MG, SG = YB, YB + US * D, YB + (US + VS) * D, YB + (US + VS) * D + 4096
        RX = RU + SLOTS * D
        mgA = view(arena_c, RU, D)
        mgTA = view(arena_c, RU + 2048, KT, P)
        sigA = view(arena_c, RU + 4096, 512)
        tmpA = view(arena_c, RU + 4608, 512)
        sq_a = view(arena_c, RU + 6144, KT, P)
        sqr = view(arena_c, RX, 2, T)
        rstd_ln = view(arena_c, RX + 1024, T)
        root_ln = view(arena_c, RX + 1536, T)
        ln_acc = view(arena_c, RX + 2048, 2, T)
        keys_nA = view(arena_c, RX, 2 * PH, NK)

        s_a = view(arena_c, RU, 2, PH, NK)

        def scoresB(c):
            return h2T[:, 4 * c:4 * c + NBB, 0:NK]

        u_row = [view(arena_c, RU + s * D, D) for s in range(US)]
        v_row = [view(arena_c, RV + s * D, D) for s in range(VS)]
        mgT23 = view(arena_c, MG, KT, 2 * P)
        sig = view(arena_c, SG, 2, TB)
        mtmp = view(arena_c, SG + 768, TB)
        act_u = view(arena_c, SG + 1152, TOP)
        act_g = view(arena_c, SG + 1168, TOP)
        act_w = view(arena_c, SG + 1184, TOP)
        idx_cur = view(arena_c, SG + 1200, 2, TOP).bitcast(U32)
        sq_b = view(arena_c, MG + 2048, KT, P)
        gbc2 = view(arena_c, MG, D)
        keys_n = view(arena_c, MG, 2 * PH, NK)
        keysT = view(arena_c, MG + 2048, 2 * PH, NK)
        qh = view(arena_c, MG, 2, TB)
        cand = view(arena_c, MG + 768, TOP * TOP)
        cand2 = view(arena_c, MG + 1024, TOP * TOP)
        onehot = view(arena_c, MG + 1280, NBB, TOP, TOP)

        def topk_work(at, n, more):
            w, o = {}, at
            for name, shape, kind in (
                    ("vals", (2 * n, TOP), F32), ("s_rep", (NK,), F32), ("best", (n, TOP), F32),
                    ("pa", (n, TOP), F32), ("pb", (n, TOP), F32), ("ia", (n, TOP), F32), ("ib", (n, TOP), F32),
                    ("idxf", (2 * n, TOP), F32), ("ee", (n, TOP), F32), ("es", (n,), F32),
                    ("idx_u", (2 * n, TOP), U32), ("pos_u", (n, TOP), U32), ("pos_a", (n, TOP), U32),
                    ("pos_b", (n, TOP), U32)):
                w[name] = view(arena_c, o, *shape)
                if kind == U32:
                    w[name] = w[name].bitcast(U32)
                o += int(np.prod(shape))
            w["s_rep"] = (w["s_rep"], view(arena_c, more, NK))
            return w, o

        work_b, end = topk_work(SG, NBB, SG + 1000)
        assert end <= SG + 1000
        work_b["onehot"] = onehot
        work_a, end = topk_work(RU + 2048, PH, RU + 8192 - NK)
        assert end <= RU + 5888
        work_a["onehot"] = view(arena_c, RU + 5888, PH, TOP, TOP)
        diag1 = h2T[:, 8:8 + VS, 0:P]
        u2_row = [view(arena_h, s * D, D) for s in range(SLOTS)]
        v2_row = [view(arena_c, RU + s * D, D) for s in range(SLOTS)]
        diag = view(arena_c, RX, SLOTS, P)
        act_u2 = view(arena_c, RX + 512, 2, TOP)
        act_g2 = view(arena_c, RX + 544, 2, TOP)
        act_w2 = view(arena_c, RX + 576, 2, TOP)
        idx_cur2 = view(arena_c, SG + 1232, 2, TOP).bitcast(U32)
        gbc_f = view(arena_c, MG, D)
        sq_f = view(arena_c, MG + 2048, KT, P)
        y_out = view(arena_h, 0, NB, D)

        ps = [ctx.enter_context(nc.psum_tensor(f"bank{n}", [P, 512], F32)) for n in range(8)]

        const_step = sem("const_step")
        consts = sem("consts")
        x_in = [sem(f"x_in{b}") for b in range(NB)]
        rows_in = sem("rows_in")
        cols_tr = sem("cols_tr")
        cols_done = sem("cols_done")
        small_in = sem("small_in")
        gkw_in = sem("gkw_in")
        gbc_in = sem("gbc_in")
        wgk_in = sem("wgk_in")
        wgk_gap = sem("wgk_gap")
        w_in_slot = [sem("w_slot0"), sem("w_slot1")]
        w_used = sem("w_used")
        dve_chain = sem("dve_chain")
        sp_passed = sem("sp_passed")
        pool_passed = sem("pool_passed")
        dve_passed = sem("dve_passed")
        n1_sum = sem("n1_sum")
        n1_ms = sem("n1_ms")
        n1_root = sem("n1_root")
        n1_xn = sem("n1_xn")
        n1_tr = sem("n1_tr")
        n1_done = sem("n1_done")
        glow_mm = sem("glow_mm")
        glow_done = sem("glow_done")
        q_mm = sem("q_mm")
        q_ev = sem("q_ev")
        z_mm = sem("z_mm")
        z_exp = sem("z_exp")
        z_ln = sem("z_ln")
        z_dif = sem("z_dif")
        z_dec = sem("z_dec")
        z_qk = sem("z_qk")
        v_mm = sem("v_mm")
        v_ev = sem("v_ev")
        og_mm = sem("og_mm")
        og_ev = sem("og_ev")
        og_scaled = sem("og_scaled")
        kt_tr = sem("kt_tr")
        kt_ev = sem("kt_ev")
        ub_mm = sem("ub_mm")
        ub_done = sem("ub_done")
        uf_mm = sem("uf_mm")
        uf_done = sem("uf_done")
        sc_mm = sem("sc_mm")
        sc_done = sem("sc_done")
        o_mm = sem("o_mm")
        o_sum = sem("o_sum")
        o_ms = sem("o_ms")
        o_root = sem("o_root")
        o_norm = sem("o_norm")
        ot_tr = sem("ot_tr")
        ot_ev = sem("ot_ev")
        pair = {}
        for name in ("cv", "ma1", "mb1", "ma", "mb"):
            pair[name] = dict(gate=sem(name + "_gate"), sig=sem(name + "_sig"), val=sem(name + "_val"),
                              use=sem(name + "_use"))
        cv_done = sem("cv_done")
        ln_added = sem("ln_added")
        ln_sum = sem("ln_sum")
        ln_xc = sem("ln_xc")
        ln_sq = sem("ln_sq")
        ln_varu = sem("ln_varu")
        ln_ms = sem("ln_ms")
        ln_root = sem("ln_root")
        ln_scaled = sem("ln_scaled")
        ln_act = sem("ln_act")
        mb1_done = sem("mb1_done")
        mb_done = sem("mb_done")
        mt_tr = sem("mt_tr")
        mt_ev = sem("mt_ev")
        out1_mm = sem("out1_mm")
        out1_free = sem("out1_free")
        res_in = sem("res_in")
        out_mm = sem("out_mm")
        out_free = sem("out_free")
        n2_sum = sem("n2_sum")
        n2_ms = sem("n2_ms")
        n2_root = sem("n2_root")
        n2_h = sem("n2_h")
        n2_tr = sem("n2_tr")
        n2_ev = sem("n2_ev")
        keys_in = sem("keys_in")
        keys_tr = sem("keys_tr")
        keys_ev = sem("keys_ev")
        pq_mm = sem("pq_mm")
        pq_ev = sem("pq_ev")
        s_mm = sem("s_mm")
        s_ev = sem("s_ev")
        sm_in = sem("sm_in")
        sm_exp = sem("sm_exp")
        s_free = sem("s_free")
        idx_ready = sem("idx_ready")
        u_ready = [sem(f"u_ready{s}") for s in range(US)]
        v_ready = [sem(f"v_ready{s}") for s in range(VS)]
        u_used = sem("u_used")
        v_used = sem("v_used")
        act_done = sem("act_done")
        w_ready = sem("w_ready")
        diag1_ready = sem("diag1_ready")
        mix1_free = sem("mix1_free")
        idx2_ready = sem("idx2_ready")
        u2_ready = [sem(f"u2_ready{s}") for s in range(SLOTS)]
        v2_ready = [sem(f"v2_ready{s}") for s in range(SLOTS)]
        u2_used = sem("u2_used")
        v2_used = sem("v2_used")
        act2_done = sem("act2_done")
        diag_ready = sem("diag_ready")
        mix_free = sem("mix_free")
        fin_sum = sem("fin_sum")
        fin_ms = sem("fin_ms")
        fin_root = sem("fin_root")
        fin_y = sem("fin_y")
        out_done = sem("out_done")

        block = ctx.enter_context(nc.Block())
        x_d = x[0].rearrange("(b p) d -> b p d", p=P)
        out_d = out[0].rearrange("(b p) d -> b p d", p=P)

        def block_of(a, b):
            return a[:, :, bass.ds(b * P, P)]

        def by_tile(a):
            return a.rearrange("p (k j) -> p k j", j=P)

        def w_slot(n):
            return view(wring, (n % 2) * SLAB, KT, 256)

        def w_slot_half(n):
            return view(wring, (n % 2) * SLAB, KT // 2, 512)

        @block.sync
        def _(sp):
            for b in range(NB):
                sp.dma_start(xb[:, b, :], x_d[b]).then_inc(x_in[b], 16)
            for d in range(2):
                sp.dma_start(wgk[:, :, 32 * d:32 * d + RANK],
                             slabs(w_in, False)[:, :, OGK + d * RANK:OGK + (d + 1) * RANK]).then_inc(wgk_in, 16)

            def load(n, i, per, dst, src):
                hold(sp, w_used, i * per + (n + 1), sp_passed)
                sp.dma_start(dst, src).then_inc(w_in_slot[n % 2], 16)

            full, half = slabs(w_in, False), slabs(w_in, True)
            with sp.Fori(0, HEADS) as h:
                load(0, h, HEAD_SLABS, w_slot(0), full[:, :, bass.ds(h * DK + OQ, DK)])
                load(1, h, HEAD_SLABS, w_slot(1), full[:, :, bass.ds(h * DK + OK_, DK)])
                for s in range(2):
                    load(2 + s, h, HEAD_SLABS, w_slot_half(s), half[s][:, :, bass.ds(h * DV + OV, DV)])
                for s in range(2):
                    load(4 + s, h, HEAD_SLABS, w_slot_half(s), half[s][:, :, bass.ds(h * DV + OG, DV)])

            def pair_loads(first, w_gate, o_gate, w_val, o_val):
                with sp.Fori(0, KT // 2) as i:
                    load(first, i, 2, w_slot(0), slabs(w_gate, False)[:, :, bass.ds(i * 256 + o_gate, 256)])
                    load(first + 1, i, 2, w_slot(1), slabs(w_val, False)[:, :, bass.ds(i * 256 + o_val, 256)])

            pair_loads(SB_CONV, w_in, OGATE, w_in, OGLU)

            def group_loads(first, w_gate, o_gate, w_val):
                with sp.Fori(0, 4) as g:
                    for j, (w, o) in enumerate(((w_gate, o_gate), (w_val, 0))):
                        for s in range(2):
                            load(first + 2 * j + s, g, 4, w_slot_half(s), slabs(w, True)[s][:, :, bass.ds(g * 512 + o, 512)])

            def out_loads(first):
                with sp.Fori(0, 4) as g:
                    for s in range(2):
                        load(first + s, g, 2, w_slot_half(s), slabs(w_out, True)[s][:, :, bass.ds(g * 512, 512)])

            def query_loads(first):
                with sp.Fori(0, PH // 2) as i:
                    for s in range(2):
                        load(first + s, i, 2, w_slot(s), slabs(w_q, False)[:, :, bass.ds(i * 512 + s * 256, 256)])

            group_loads(SB_MA1, w_in, OGA, w_o)
            group_loads(SB_MB1, w_in, OGB, w_pw2)
            out_loads(SB_OUT1)
            query_loads(SB_WQ1)
            pair_loads(SB_MA, w_in, OGA, w_o, 0)
            pair_loads(SB_MB, w_in, OGB, w_pw2, 0)
            out_loads(SB_OUT)
            query_loads(SB_WQ)
            for b in range(NB):
                sp.wait_ge(fin_y, b + 1)
                sp.dma_start(out_d[b], y_out[:, b, :]).then_inc(out_done, 16)
            sp.wait_ge(out_done, 16 * NB)

        @block.gpsimd
        def _(pool):
            G = nc.gpsimd
            G.memset(ident[:], 0.0).then_inc(const_step, 1)
            pool.wait_ge(const_step, 1)
            G.affine_select(out=ident[:], in_=ident[:], compare_op=ALU.not_equal, fill=1.0, base=0,
                            pattern=[[-1, P]], channel_multiplier=1).then_inc(consts, 1)
            G.memset(ones_d[:], 1.0 / D).then_inc(consts, 1)
            G.memset(wgk[:, :, RANK:32], 0.0).then_inc(wgk_gap, 1)
            G.memset(causal, 1.0).then_inc(const_step, 1)
            pool.wait_ge(const_step, 2)
            G.affine_select(out=causal, in_=causal, compare_op=ALU.is_ge, fill=0.0, base=0,
                            pattern=[[1, P]], channel_multiplier=-1).then_inc(consts, 1)
            G.memset(reset, 1.0).then_inc(const_step, 1)
            pool.wait_ge(const_step, 3)
            G.memset(reset.rearrange("p (c t) -> p c t", t=P)[:, :, 0:1], 0.0).then_inc(consts, 1)
            G.iota(iota_i[:], pattern=[[1, TOP]], base=0, channel_multiplier=0).then_inc(const_step, 1)
            pool.wait_ge(const_step, 4)
            G.tensor_copy(iota16[:], iota_i[:]).then_inc(consts, 1)

            for t in range(KT):
                pool.wait_ge(cv_done, t + 1)
                if t == 0:
                    G.tensor_copy(ln_acc[:, 0, :], cv[:, 0, :]).then_inc(ln_added, 1)
                else:
                    pool.wait_ge(ln_added, t)
                    G.tensor_tensor(ln_acc[:, 0, :], ln_acc[:, 0, :], cv[:, t, :], ALU.add).then_inc(ln_added, 1)
            for t in range(KT):
                pool.wait_ge(ln_sq, t + 1)
                if t == 0:
                    G.tensor_copy(ln_acc[:, 1, :], sqr[:, 0, :]).then_inc(ln_added, 1)
                else:
                    pool.wait_ge(ln_added, KT + t)
                    G.tensor_tensor(ln_acc[:, 1, :], ln_acc[:, 1, :], sqr[:, t % 2, :], ALU.add)\
                        .then_inc(ln_added, 1)

            def gathers(turns, idx_sem, idx, u_rows, u_sems, u_free, v_rows, v_sems, v_free):
                with pool.Fori(0, turns) as i:
                    for m in range(2):
                        hold(pool, idx_sem, i * 2 + (m + 1), pool_passed)
                        for k in range(TOP):
                            n = m * TOP + k
                            at = bass.IndirectOffsetOnAxis(ap=idx[:, m, k:k + 1], axis=0)
                            hold(pool, u_free, i * 2 * TOP + (n + 1), pool_passed)
                            s = n % len(u_rows)
                            pool.indirect_dma_start(out=u_rows[s], out_offset=None, in_=u_tab[0], in_offset=at)\
                                .then_inc(u_sems[s], 16)
                            hold(pool, v_free, i * 2 * TOP + (n + 1), pool_passed)
                            s = n % len(v_rows)
                            pool.indirect_dma_start(out=v_rows[s], out_offset=None, in_=v_tab[0], in_offset=at)\
                                .then_inc(v_sems[s], 16)

            gathers(SIDE // 2, idx_ready, idx_cur, u_row, u_ready, u_used, v_row, v_ready, v_used)
            gathers((UNITS - SIDE) // 2, idx2_ready, idx_cur2, u2_row, u2_ready, u2_used, v2_row, v2_ready, v2_used)

        @block.scalar
        def _(act):
            A = nc.scalar.activation
            for src, r in ((norm1_g, R_N1), (conv_b, R_CB), (ln_g, R_LG), (ln_b, R_LB)):
                act.dma_start(rows[r:r + 1, :], src).then_inc(rows_in, 16)
            act.dma_start(rows[R_CW:R_CW + TAPS, :], conv_w[0]).then_inc(rows_in, 16)
            act.dma_start(rows[R_GK:R_GK + 1, 0:1024], gk_f_b).then_inc(rows_in, 16)
            act.dma_start(rows[R_GK:R_GK + 1, 1024:2048], gk_b_b).then_inc(rows_in, 16)
            for b in range(NB):
                act.wait_ge(x_in[b], 16)
                A(sq_x, xb[:, b, :], ACT.Square, accum_out=small[:, b:b + 1]).then_inc(n1_sum, 1)
                act.wait_ge(n1_sum, b + 1)
            for b in range(NB):
                act.wait_ge(n1_ms, b + 1)
                A(small[:, 8 + b:9 + b], small[:, 4 + b:5 + b], ACT.Sqrt).then_inc(n1_root, 1)

            act.dma_start(gbc_o, onorm_g.rearrange("a h e -> a (h e)").broadcast_to([P, D])).then_inc(gbc_in, 16)

            for d in range(2):
                rank = slice(32 * d, 32 * d + RANK)
                act.wait_ge(glow_mm, 1)
                A(glow[rank, :], ps[0][rank, :], ACT.Copy).then_inc(glow_done, 1)

            with act.Fori(0, HEADS) as h:
                act.dma_start(gkw[0:RANK, :], gk_f_w[0][:, bass.ds(h * DK, DK)]).then_inc(gkw_in, 16)
                act.dma_start(gkw[32:32 + RANK, :], gk_b_w[0][:, bass.ds(h * DK, DK)]).then_inc(gkw_in, 16)
                for n in range(4):
                    act.wait_ge(q_mm, h * 4 + (n + 1))
                    dst = qT[:, n, :] if n < 2 else kT[:, n - 2, :]
                    A(dst, ps[n][:], ACT.Copy, scale=DK ** -0.5 if n < 2 else 1.0).then_inc(q_ev, 1)
                for u in range(4):
                    fwd = u < 2
                    act.wait_ge(z_mm, h * 4 + (u + 1))
                    bias = cols[:, bass.ds(h * MT + (8 * (u // 2) + u % 2), 1), R_GK]
                    A(t_abs, ps[4 + u][:], ACT.Abs, bias=bias).then_inc(z_exp, 1)
                    act.wait_ge(z_exp, h * 8 + (2 * u + 1))
                    A(t_abs, t_abs, ACT.Exp, scale=-1.0).then_inc(z_exp, 1)
                    act.wait_ge(z_exp, h * 8 + (2 * u + 2))
                    A(t_abs, t_abs, ACT.Ln, bias=1.0).then_inc(z_ln, 1)
                    act.wait_ge(z_dif, h * 4 + (u + 1))
                    A(t_e, t_d, ACT.Exp, scale=1.0 / 16 if fwd else -1.0 / 16).then_inc(z_dec, 1)
                    A(dec[:, u, 0:3], dif[:, 0:3], ACT.Exp, scale=1.0 / 16).then_inc(z_dec, 1)
                    act.wait_ge(z_dec, h * 12 + (3 * u + 2))
                    A(t_d, t_d, ACT.Exp, scale=-1.0 / 16 if fwd else 1.0 / 16).then_inc(z_dec, 1)
                    act.wait_ge(z_qk, h * 4 + (u + 1))
                for b in range(NB):
                    act.wait_ge(v_mm, h * 4 + (b + 1))
                    A(v_tok[:, b, :], ps[b][:], ACT.Copy).then_inc(v_ev, 1)
                for b in range(NB):
                    act.wait_ge(og_mm, h * 4 + (b + 1))
                    A(og_s[:, b, :], ps[4 + b][:], ACT.Silu).then_inc(og_ev, 1)
                for n in range(4):
                    act.wait_ge(kt_tr, h * 4 + (n + 1))
                    A(kmT[:, :, n // 2, (n % 2) * P:(n % 2) * P + P],
                      ps[n][:].rearrange("p (c f) -> p c f", f=P), ACT.Copy).then_inc(kt_ev, 1)

                def ot_out(c):
                    act.wait_ge(ot_tr, h * 4 + (c + 1))
                    A(oT[:, bass.ds(h * 4, 4), c * P:c * P + P],
                      ps[2 + c % 2][:].rearrange("p (m t) -> p m t", t=P), ACT.Copy).then_inc(ot_ev, 1)

                for c in range(NB):
                    act.wait_ge(o_mm, h * 4 + (c + 1))
                    if c:
                        act.wait_ge(o_sum, h * 4 + c)
                    A(t_abs, ps[6 + c % 2][:], ACT.Square, accum_out=small[:, 16 + c:17 + c]).then_inc(o_sum, 1)
                    act.wait_ge(o_ms, h * 4 + (c + 1))
                    A(small[:, 24 + c:25 + c], small[:, 20 + c:21 + c], ACT.Sqrt).then_inc(o_root, 1)
                    if c:
                        ot_out(c - 1)
                ot_out(NB - 1)

            def gates(name, i, dst, nt):
                p = pair[name]
                for m in range(2):
                    act.wait_ge(p["gate"], i * 2 + (m + 1))
                    act.wait_ge(p["use"], i * 2 + (m + 1))
                    A(dst[:, m, :], ps[m][:, 0:nt], ACT.Sigmoid).then_inc(p["sig"], 1)

            def gates1(name, start, end):
                p = pair[name]
                with act.Fori(start, end) as g:
                    act.wait_ge(p["gate"], g + 1)
                    act.wait_ge(p["use"], g + 1)
                    A(sigA, ps[0][:], ACT.Sigmoid).then_inc(p["sig"], 1)

            with act.Fori(0, KT // 2) as i:
                gates("cv", i, sig_c, T)
            act.dma_start(gbc2, norm2_g.broadcast_to([P, D])).then_inc(gbc_in, 16)
            gates1("ma1", 0, 2)
            for t in range(KT):
                act.wait_ge(ln_xc, t + 1)
                if t >= 2:
                    act.wait_ge(ln_added, KT + t - 1)
                A(sqr[:, t % 2, :], cv[:, t, :], ACT.Square).then_inc(ln_sq, 1)
            gates1("ma1", 2, 3)
            act.wait_ge(ln_ms, 1)
            A(root_ln, rstd_ln, ACT.Sqrt).then_inc(ln_root, 1)

            def ln_out(n, lo, hi):
                for t in range(KT):
                    act.wait_ge(ln_scaled, n * KT + t + 1)
                    A(cv[:, t, lo:hi], cv[:, t, lo:hi], ACT.Silu, bias=cols[:, t, R_LB:R_LB + 1],
                      scale=cols[:, t, R_LG:R_LG + 1]).then_inc(ln_act, 1)

            ln_out(0, 0, TA)
            gates1("ma1", 3, 4)
            act.wait_ge(pair["ma1"]["use"], 4 + 1)
            act.dma_start(block_of(x2, 0), by_tile(x_d[0])).then_inc(res_in, 16)
            gates1("mb1", 0, 4)
            ln_out(1, TA, T)

            def keys_load(dst):
                act.dma_start(dst, keys[0].rearrange("h c n d -> n (h c) d")).then_inc(keys_in, 16)

            def keys_out(n, bank):
                for g in range(4):
                    act.wait_ge(keys_tr, 4 * n + g + 1)
                    A(keysT[:, 4 * g:4 * g + 4, :], ps[(bank + g) % 8][:].rearrange("p (k t) -> p k t", t=P),
                      ACT.Copy).then_inc(keys_ev, 1)

            def norm2_sums(blocks, sq):
                for b in blocks:
                    A(sq, block_of(x2, b), ACT.Square, accum_out=small[:, 32 + b:33 + b]).then_inc(n2_sum, 1)
                    act.wait_ge(n2_sum, b + 1)

            def norm2_roots(blocks):
                for b in blocks:
                    act.wait_ge(n2_ms, b + 1)
                    A(small[:, 40 + b:41 + b], small[:, 36 + b:37 + b], ACT.Sqrt).then_inc(n2_root, 1)

            def norm2_out(blocks):
                for b in blocks:
                    for g in range(4):
                        n = b * 4 + g
                        act.wait_ge(n2_tr, n + 1)
                        A(h2T[:, 4 * g:4 * g + 4, b * P:b * P + P],
                          ps[n % 8][:].rearrange("p (k t) -> p k t", t=P), ACT.Copy).then_inc(n2_ev, 1)

            def queries_out(hg, m, nb):
                for c in range(2):
                    act.wait_ge(pq_mm, hg * 2 + (c + 1))
                    A(qh[:, c, 0:nb * P], ps[4 * m + c][:, 0:nb * P], ACT.Copy).then_inc(pq_ev, 1)

            def queries(hg, m, nb, scores):
                queries_out(hg, m, nb)
                scores_out(hg, m, nb, scores)

            def scores_out(hg, m, nb, scores):
                if nb > 1:
                    act.wait_ge(s_free, hg)
                for c in range(2):
                    act.wait_ge(s_mm, hg * 2 + (c + 1))
                    A(scores(c), ps[4 * m + 2 + c][:, 0:nb * NK].rearrange("p (b n) -> p b n", n=NK),
                      ACT.Copy).then_inc(s_ev, 1)

            def exponentials(first, count, w):
                act.wait_ge(sm_in, first + count)
                A(w["ee"], w["ee"], ACT.Exp).then_inc(sm_exp, count)

            keys_load(keys_nA)
            for g in range(4):
                act.wait_ge(mt_tr, g + 1)
                A(mgTA[:, 4 * g:4 * g + 4, :], ps[2 + g][:].rearrange("p (k t) -> p k t", t=P),
                  ACT.Copy).then_inc(mt_ev, 1)
            act.wait_ge(out1_free, 2 + 4)
            norm2_sums([0], sq_a)
            norm2_roots([0])
            keys_out(0, 4)
            norm2_out([0])
            with act.Fori(0, PH // 2) as i:
                for m in range(2):
                    queries(i * 2 + m, m, 1, lambda c: s_a[:, c, bass.ds(i * 2 + m, 1), :])
            exponentials(0, PH, work_a)

            def expert(U, k):
                one = slice(k, k + 1)
                act.wait_ge(u_used, U * TOP + (k + 1 + US))
                A(act_g[:, one], act_u[:, one], ACT.Gelu).then_inc(act_done, 1)
                act.wait_ge(act_done, U * TOP + (k + 1))
                A(act_w[:, one], act_g[:, one], ACT.Copy, scale=gate_all[:, bass.ds(U, 1), k]).then_inc(w_ready, 1)

            def unit(U, after):
                for k in range(TOP):
                    expert(U, k)
                    after(k)

            def gates_after(plan, *steps):
                def after(k):
                    if k in plan[0]:
                        gates(*steps[plan[0].index(k)], sig, TB)
                return after

            unit(0, gates_after(PLAN_FIRST, *(("ma", i) for i in range(4))))
            unit(1, gates_after(PLAN_3, *(("ma", i) for i in range(4, 7))))
            unit(2, gates_after(PLAN_3, ("ma", 7), ("mb", 0), ("mb", 1)))
            act.wait_ge(pair["ma"]["use"], KT + 2)
            for b in range(1, NB):
                act.dma_start(block_of(x2, b), by_tile(x_d[b])).then_inc(res_in, 16)
            with act.Fori(3, 5) as U:
                unit(U, gates_after(PLAN_3, *(("mb", U * 3 + (j - 7)) for j in range(3))))
            unit(5, lambda k: None)

            def second_norm(k):
                if k == 6:
                    act.wait_ge(out_free, 6 + 4 * NBB)
                    act.dma_start(gbc2, norm2_g.broadcast_to([P, D])).then_inc(gbc_in, 16)
                    norm2_sums(range(1, NB), sq_b)
                if k == 8:
                    norm2_roots(range(1, NB))
                if 10 <= k < 10 + NBB:
                    norm2_out([k - 9])
                if k == 13:
                    keys_load(keys_n)
                if k == 15:
                    keys_out(1, 0)

            unit(6, second_norm)

            def first_head(k):
                if k == 0:
                    queries(PH, 0, NBB, scoresB)
                if k == EXP_AT:
                    exponentials(PH, 1, work_b)
                if k == SCORES_AT:
                    queries(PH + 1, 0, NBB, scoresB)

            unit(7, first_head)
            def unit_on_diag(U, after):
                for k in range(TOP):
                    expert(U, k)
                    act.wait_ge(w_ready, U * TOP + (k + 1))
                    act.wait_ge(v_used, U * TOP + (k + 1))
                    A(diag1[:, k % VS, :], ident[:], ACT.Copy, scale=act_w[:, k:k + 1]).then_inc(diag1_ready, 1)
                    after(k)

            with act.Fori(8, 14) as U:

                def head_beside(k):
                    if k == EXP_AT:
                        exponentials(U + 1, 1, work_b)
                    if k == SCORES_AT - 1:
                        queries_out(U + 2, 0, NBB)
                    if k == SCORES_AT:
                        scores_out(U + 2, 0, NBB, scoresB)

                unit_on_diag(U, head_beside)
            unit_on_diag(14, lambda k: exponentials(2 * PH - 1, 1, work_b) if k == EXP_AT else None)
            unit_on_diag(15, lambda k: None)

            act.wait_ge(idx2_ready, 1)
            act.dma_start(gbc_f, final_g.rearrange("(a d) -> a d", a=1).broadcast_to([P, D])).then_inc(gbc_in, 16)
            with act.Fori(0, (UNITS - SIDE) // 2) as i:
                for n in range(2 * TOP):
                    m, k = n // TOP, n % TOP
                    one = slice(k, k + 1)
                    act.wait_ge(u2_used, i * 2 * TOP + (n + 1 + SLOTS))
                    A(act_g2[:, m, one], act_u2[:, m, one], ACT.Gelu).then_inc(act2_done, 1)
                    act.wait_ge(act2_done, i * 4 * TOP + (2 * n + 1))
                    A(act_w2[:, m, one], act_g2[:, m, one], ACT.Copy,
                      scale=gate_all[:, bass.ds(i * 2 + (SIDE + m), 1), k]).then_inc(act2_done, 1)
                    act.wait_ge(act2_done, i * 4 * TOP + (2 * n + 2))
                    act.wait_ge(v2_used, i * 2 * TOP + (n + 1))
                    A(diag[:, n % SLOTS, :], ident[:], ACT.Copy, scale=act_w2[:, m, one]).then_inc(diag_ready, 1)

            act.wait_ge(mix_free, UNITS - SIDE + 2)
            for b in range(NB):
                A(sq_f, block_of(x2, b), ACT.Square, accum_out=small[:, 48 + b:49 + b]).then_inc(fin_sum, 1)
                act.wait_ge(fin_sum, b + 1)
            for b in range(NB):
                act.wait_ge(fin_ms, b + 1)
                A(small[:, 56 + b:57 + b], small[:, 52 + b:53 + b], ACT.Sqrt).then_inc(fin_root, 1)

        @block.vector
        def _(dve):
            V = nc.vector
            chain = Chain(dve, dve_chain)

            def mean_square(dst, src, n):
                return V.tensor_scalar(small[:, dst:dst + 1], small[:, src:src + 1], 1.0 / n, EPS, ALU.mult, ALU.add)

            def inverse(dst, src):
                return V.reciprocal(small[:, dst:dst + 1], small[:, src:src + 1])

            for name, p in pair.items():
                dve.sem_inc(p["use"], 1 if name[-1] == "1" else 2)
                if name[-1] == "1":
                    dve.sem_inc(p["sig"], 1)
            dve.sem_inc(out1_free, 2)
            dve.sem_inc(out_free, 6)
            dve.sem_inc(u_used, US)
            dve.sem_inc(v_used, VS)
            dve.sem_inc(u2_used, SLOTS)
            dve.sem_inc(mix_free, 2)

            for g in range(2):
                dve.wait_ge(cols_tr, g + 1)
                V.tensor_copy(cols[:, 8 * g:8 * g + 8, :],
                              ps[g][:].rearrange("p (k r) -> p k r", r=64)[:, :, 0:ROWS]).then_inc(cols_done, 1)
            for b in range(NB):
                dve.wait_ge(n1_sum, b + 1)
                mean_square(4 + b, b, D).then_inc(n1_ms, 1)
            for b in range(NB):
                dve.wait_ge(n1_root, b + 1)
                chain.step(inverse(12 + b, 8 + b))
                V.tensor_scalar(xb[:, b, :], xb[:, b, :], small[:, 12 + b:13 + b], None, ALU.mult)\
                    .then_inc(n1_xn, 1)
            dve.wait_ge(cols_done, 2)
            for b in range(NB):
                for g in range(4):
                    n = b * 4 + g
                    dve.wait_ge(n1_tr, n + 1)
                    gain = cols[:, 4 * g:4 * g + 4, R_N1:R_N1 + 1].broadcast_to([P, 4, P])
                    V.tensor_tensor(hT[:, 4 * g:4 * g + 4, b * P:b * P + P],
                                    ps[n % 8][:].rearrange("p (k t) -> p k t", t=P), gain, ALU.mult)\
                        .then_inc(n1_done, 1)
            dve.wait_ge(consts, 5)
            dve.wait_ge(gbc_in, 16)

            with dve.Fori(0, HEADS) as h:
                chain.enter()
                for u in range(4):
                    d, m = u // 2, u % 2
                    bias = cols[:, bass.ds(h * MT + (8 * d + m), 1), R_GK]
                    dve.wait_ge(z_exp, h * 8 + (2 * u + 1))
                    chain.step(V.tensor_scalar(t_l, ps[4 + u][:], bias, 0.0, ALU.add, ALU.min))
                    dve.wait_ge(z_ln, h * 4 + (u + 1))
                    chain.step(V.tensor_tensor(t_l, t_l, t_abs, ALU.subtract))
                    chain.step(V.tensor_tensor_scan(t_b, reset, t_l, 0.0, ALU.mult, ALU.add))
                    b3 = t_b.rearrange("p (c t) -> p c t", t=P)
                    src = b3
                    if d:
                        chain.step(V.tensor_tensor(t_l, t_b, t_l, ALU.subtract))
                        src = t_l.rearrange("p (c t) -> p c t", t=P)
                    ref = src[:, :, REF]
                    chain.mark(V.tensor_tensor(t_d.rearrange("p (c t) -> p c t", t=P), src,
                                               src[:, :, REF:REF + 1].broadcast_to([P, NB, P]), ALU.subtract))
                    chain.step(V.tensor_tensor(dif, b3[:, :, P - 1], ref, ALU.subtract))
                    chain.step(V.tensor_tensor(dif[:, 0:3], dif[:, 0:3], src[:, 1:4, REF], ALU.add))
                    V.tensor_scalar(t_d, t_d, CLAMP, -CLAMP, ALU.min, ALU.max).then_inc(z_dif, 1)
                    dve.wait_ge(z_dec, h * 12 + (3 * u + 3))
                    dve.wait_ge(q_ev, h * 4 + 4)
                    chain.mark(V.tensor_tensor(qm[:, d, m, :], qT[:, m, :], t_e, ALU.mult))
                    chain.wait()
                    V.tensor_tensor(km[:, d, m, :], kT[:, m, :], t_d, ALU.mult).then_inc(z_qk, 1)
                for b in range(NB):
                    dve.wait_ge(og_ev, h * 4 + (b + 1))
                    V.tensor_tensor(og_s[:, b, :], og_s[:, b, :], gbc_o[:, bass.ds(h * DV, DV)], ALU.mult)\
                        .then_inc(og_scaled, 1)
                for j, c in enumerate((3, 2, 1)):
                    for m in range(MT):
                        dve.wait_ge(ub_mm, h * 6 + (2 * j + m + 1))
                        bank = ps[2 * (j % 2) + m][:]
                        if c < 3:
                            dve.wait_ge(ub_done, h * 6 + (2 * j - 1 + m))
                            chain.step(V.tensor_tensor(st_b[:, c - 1, m, :], bank, st_b[:, c, m, :], ALU.add))
                            bank = st_b[:, c - 1, m, :]
                        V.tensor_scalar(st_b[:, c - 1, m, :], bank, dec[:, 2 + m, c - 1:c], None, ALU.mult)\
                            .then_inc(ub_done, 1)

                def merge_scores(c):
                    dve.wait_ge(sc_mm, h * 4 + (c + 1))
                    if c >= 2:
                        dve.wait_ge(o_mm, h * 4 + (c - 1))
                    bank = ps[4 + c % 2]
                    chain.step(V.tensor_copy(p_t[:, c % 2, :], bank[:, P:2 * P]))
                    V.copy_predicated(p_t[:, c % 2, :], causal.bitcast(U32), bank[:, 0:P]).then_inc(sc_done, 1)

                merge_scores(0)
                for c in range(NB):
                    if c < NB - 1:
                        merge_scores(c + 1)
                        for m in range(MT):
                            dve.wait_ge(uf_mm, h * 6 + (2 * c + m + 1))
                            new = st_f[:, (c + 1) % 2, m, :]
                            bank = ps[m][:]
                            if c >= 1:
                                dve.wait_ge(uf_done, h * 6 + (2 * c - 1 + m))
                                if c >= 2:
                                    dve.wait_ge(o_mm, h * 4 + c)
                                chain.step(V.tensor_tensor(new, bank, st_f[:, c % 2, m, :], ALU.add))
                                bank = new
                            V.tensor_scalar(new, bank, dec[:, m, c:c + 1], None, ALU.mult).then_inc(uf_done, 1)
                    dve.wait_ge(o_sum, h * 4 + (c + 1))
                    mean_square(20 + c, 16 + c, DV).then_inc(o_ms, 1)
                    dve.wait_ge(o_root, h * 4 + (c + 1))
                    chain.step(inverse(28 + c, 24 + c))
                    if c >= 2:
                        dve.wait_ge(ot_tr, h * 4 + (c - 1))
                    V.scalar_tensor_tensor(on[:, c % 2, :], ps[6 + c % 2][:], small[:, 28 + c:29 + c],
                                           og_s[:, c, :], ALU.mult, ALU.mult).then_inc(o_norm, 1)
                chain.leave()

            chain.step(V.memset(upad, 0.0))
            with dve.Fori(0, KT // 2) as i:
                chain.enter()
                p = pair["cv"]
                for m in range(2):
                    dve.wait_ge(p["val"], i * 2 + (m + 1))
                    dve.wait_ge(p["sig"], i * 2 + (m + 1))
                    V.tensor_tensor(upad[:, m, PAD:PAD + T], ps[2 + m][:], sig_c[:, m, :], ALU.mult)\
                        .then_inc(p["use"], 1)
                dve.wait_ge(p["use"], i * 2 + 4)

                for r in range(TAPS):
                    for m in range(2):
                        dst = cv[:, bass.ds(i * 2 + m, 1), :].rearrange("p a t -> p (a t)")
                        tap = cols[:, bass.ds(i * 2 + m, 1), R_CW + r]
                        if r == 0:
                            bias = cols[:, bass.ds(i * 2 + m, 1), R_CB]
                            ins = V.tensor_scalar(dst, upad[:, m, 0:T], tap, bias, ALU.mult, ALU.add)
                        else:
                            chain.wait(but=1)
                            ins = V.scalar_tensor_tensor(dst, upad[:, m, r:r + T], tap, dst, ALU.mult, ALU.add)
                        if r < TAPS - 1:
                            chain.mark(ins)
                        else:
                            ins.then_inc(cv_done, 1)
                            chain.wait()
                dve.wait_ge(cv_done, i * 2 + 2)
                chain.leave()
            dve.wait_ge(cv_done, KT)

            def merge1(name, start, end):
                p = pair[name]
                with dve.Fori(start, end) as g:
                    dst = mgA[:, bass.ds(g * 512, 512)]
                    dve.wait_ge(p["val"], g + 1)
                    dve.wait_ge(p["sig"], g + 2)
                    V.tensor_tensor(dst if name == "ma1" else tmpA, ps[1][:], sigA, ALU.mult).then_inc(p["use"], 1)
                    dve.wait_ge(p["use"], g + 2)
                    if name == "mb1":
                        V.tensor_tensor(dst, tmpA, dst, ALU.add).then_inc(mb1_done, 1)
                        dve.wait_ge(mb1_done, g + 1)

            merge1("ma1", 0, 2)
            dve.wait_ge(ln_sum, 1)
            for t in range(KT):
                V.tensor_tensor(cv[:, t, :], cv[:, t, :], ps[4][:], ALU.subtract).then_inc(ln_xc, 1)
            merge1("ma1", 2, 3)
            dve.wait_ge(ln_varu, 1)
            V.tensor_scalar(rstd_ln, ps[5][:], EPS, None, ALU.add).then_inc(ln_ms, 1)
            dve.wait_ge(ln_root, 1)
            chain.step(V.reciprocal(rstd_ln, root_ln))
            for lo, hi in ((0, TA), (TA, T)):
                for t in range(KT):
                    V.tensor_tensor(cv[:, t, lo:hi], cv[:, t, lo:hi], rstd_ln[:, lo:hi], ALU.mult)\
                        .then_inc(ln_scaled, 1)
                if lo == 0:
                    merge1("ma1", 3, 4)
            merge1("mb1", 0, 4)

            dve.wait_ge(res_in, 16)
            with dve.Fori(0, 2) as i:
                for g in range(2):
                    dve.wait_ge(out1_mm, i * 2 + (g + 1))
                    dst = x2[:, bass.ds(i * 8 + g * 4, 4), 0:P]
                    V.tensor_tensor(dst, by_tile(ps[g][:]), dst, ALU.add).then_inc(out1_free, 1)

            def norm2_means(blocks):
                for b in blocks:
                    dve.wait_ge(n2_sum, b + 1)
                    mean_square(36 + b, 32 + b, D).then_inc(n2_ms, 1)

            def norm2(blocks):
                for b in blocks:
                    dve.wait_ge(n2_root, b + 1)
                    chain.step(inverse(44 + b, 40 + b))
                    V.scalar_tensor_tensor(block_of(h2, b), block_of(x2, b), small[:, 44 + b:45 + b],
                                           by_tile(gbc2), ALU.mult, ALU.mult).then_inc(n2_h, 1)

            norm2_means([0])
            dve.wait_ge(gbc_in, 32)
            norm2([0])
            chain.step(V.memset(idx_all[:, UNITS, :], 0))

            idx4 = idx_all[:, 0:UNITS, :].rearrange("p (b h) k -> p b h k", h=PH)
            gate4 = gate_all[:, 0:UNITS, :].rearrange("p (b h) k -> p b h k", h=PH)

            def top16(rows):
                for stage in range(5):
                    for values, v16, i16, rep in rows:
                        if stage == 0:
                            ins = V.max(v16[:, 0:8], values)
                        elif stage == 1:
                            ins = V.max_index(i16[:, 0:8], v16[:, 0:8], values)
                        elif stage == 2:
                            ins = V.match_replace(rep, v16[:, 0:8], values, LOW)
                        elif stage == 3:
                            ins = V.max(v16[:, 8:16], rep)
                        else:
                            ins = V.max_index(i16[:, 8:16], v16[:, 8:16], rep)
                        chain.mark(ins)
                    chain.wait()

            def topk_parts(first, count, nb, scores, w, place_in):
                vals, best, ee, es, idxf = w["vals"], w["best"], w["ee"], w["es"], w["idxf"]

                def halves(b):
                    if count > 1 or b == 0:
                        hold(dve, s_ev, first * 2 + 2 * (b + 1), dve_passed)
                    top16([(scores(c, b), vals[:, c * nb + b, :], w["idx_u"][:, c * nb + b, :], w["s_rep"][c])
                           for c in range(2)])
                    if b == nb - 1:
                        V.tensor_copy(idxf, w["idx_u"]).then_inc(s_free, count)
                        dve.wait_ge(s_free, first + count)

                def pairs_of(b):
                    c3 = cand.rearrange("p (a b) -> p a b", b=TOP)
                    chain.step(V.tensor_tensor(
                        c3, vals[:, b, :].unsqueeze(2).broadcast_to([P, TOP, TOP]),
                        vals[:, nb + b, :].unsqueeze(1).broadcast_to([P, TOP, TOP]), ALU.add))
                    top16([(cand, best[:, b, :], w["pos_u"][:, b, :], cand2)])

                def places():
                    V.tensor_tensor(ee, best, best[:, :, 0:1].broadcast_to([P, nb, TOP]),
                                    ALU.subtract).then_inc(sm_in, count)
                    chain.mark(V.tensor_scalar(w["pos_a"], w["pos_u"], 4, None, ALU.logical_shift_right))
                    chain.step(V.tensor_scalar(w["pos_b"], w["pos_u"], TOP - 1, None, ALU.bitwise_and))
                    chain.mark(V.tensor_copy(w["pa"], w["pos_a"]))
                    chain.step(V.tensor_copy(w["pb"], w["pos_b"]))

                def keys_at(c):
                    place, got = ((w["pa"], w["ia"]), (w["pb"], w["ib"]))[c]
                    shape, hot = [P, nb, TOP, TOP], w["onehot"]
                    chain.step(V.tensor_tensor(
                        hot, iota16[:].unsqueeze(1).unsqueeze(1).broadcast_to(shape),
                        place.unsqueeze(3).broadcast_to(shape), ALU.is_equal))
                    chain.step(V.tensor_tensor(
                        hot, hot, idxf[:, c * nb:c * nb + nb, :].unsqueeze(2).broadcast_to(shape), ALU.mult))
                    chain.step(V.tensor_reduce(got, hot, AX.X, ALU.add))

                def experts():
                    chain.step(V.scalar_tensor_tensor(place_in(idx_all), w["ia"], float(NK), w["ib"],
                                                      ALU.mult, ALU.add))

                def softmax():
                    dve.wait_ge(sm_exp, first + count)
                    chain.step(V.tensor_reduce(es, ee, AX.X, ALU.add))
                    chain.step(V.reciprocal(es, es))
                    chain.step(V.tensor_tensor(place_in(gate_all), ee,
                                               es.unsqueeze(2).broadcast_to([P, nb, TOP]), ALU.mult))

                def part(f, *a):
                    return lambda: f(*a)

                return ([part(f, b) for b in range(nb) for f in (halves, pairs_of)]
                        + [places, part(keys_at, 0), part(keys_at, 1), experts]), softmax

            def all_of(find):
                for part in find:
                    part()

            find, softmax = topk_parts(0, PH, PH, lambda c, b: s_a[:, c, b, :], work_a, lambda a: a[:, 0:PH, :])
            all_of(find)
            softmax()

            def topk_beside(head):
                def place_in(a):
                    return a[:, 0:UNITS, :].rearrange("p (b h) k -> p b h k", h=PH)[
                        :, 1:NB, bass.ds(head, 1), :].rearrange("p b h k -> p b (h k)")

                return topk_parts(head + PH, 1, NBB, lambda c, b: scoresB(c)[:, b, :], work_b, place_in)

            def dot(U, b, k):
                s = k % US
                dve.wait_ge(u_ready[s], U * (16 * TOP // US) + 16 * (k // US + 1))
                row = by_tile(u_row[s])
                V.scalar_tensor_tensor(row, row, 1.0, block_of(h2, b), ALU.mult, ALU.mult,
                                       accum_out=act_u[:, k:k + 1]).then_inc(u_used, 1)

            def add_row(U, b, k):
                s = k % VS
                dve.wait_ge(w_ready, U * TOP + (k + 1))
                dve.wait_ge(v_ready[s], U * (16 * TOP // VS) + 16 * (k // VS + 1))
                dve.wait_ge(v_used, U * TOP + (k + VS))
                V.scalar_tensor_tensor(block_of(x2, b), by_tile(v_row[s]), act_w[:, k:k + 1], block_of(x2, b),
                                       ALU.mult, ALU.add).then_inc(v_used, 1)

            def unit(U, b, after):
                for k in range(TOP):
                    if b == 0 and k:
                        add_row(U, b, k - 1)
                    dot(U, b, k)
                    after(k)
                    if k == COPY_AT:
                        nxt = U + 1
                        V.tensor_copy(idx_cur[:, bass.ds(nxt % 2, 1), :], idx_all[:, bass.ds(nxt, 1), :])\
                            .then_inc(idx_ready, 1)
                if b == 0:
                    add_row(U, b, TOP - 1)
                else:
                    dve.wait_ge(v_used, U * TOP + (TOP + VS))
                    for q in range(4):
                        dst = x2[:, 4 * q:4 * q + 4, b * P:b * P + P]
                        ins = V.tensor_tensor(dst, by_tile(ps[4 + q][:]), dst, ALU.add)
                    ins.then_inc(mix1_free, 1)
                    dve.wait_ge(mix1_free, U + (2 - PH))

            def merge(name, i):
                p = pair[name]
                for m in range(2):
                    d1 = mgT1[:, bass.ds(i * 2 + m, 1), :].rearrange("p a t -> p (a t)")
                    d23 = mgT23[:, bass.ds(i * 2 + m, 1), :].rearrange("p a t -> p (a t)")
                    dve.wait_ge(p["val"], i * 2 + (m + 1))
                    dve.wait_ge(p["sig"], i * 2 + (m + 1))
                    if name == "ma":
                        V.tensor_tensor(d1, ps[2 + m][:, 0:P], sig[:, m, 0:P], ALU.mult)
                        V.tensor_tensor(d23, ps[2 + m][:, P:TB], sig[:, m, P:TB], ALU.mult)\
                            .then_inc(p["use"], 1)
                        dve.wait_ge(p["use"], i * 2 + (m + 3))
                    else:
                        V.tensor_tensor(mtmp, ps[2 + m][:, 0:TB], sig[:, m, :], ALU.mult)\
                            .then_inc(p["use"], 1)
                        dve.wait_ge(p["use"], i * 2 + (m + 3))
                        V.tensor_tensor(d1, mtmp[:, 0:P], d1, ALU.add)
                        V.tensor_tensor(d23, mtmp[:, P:TB], d23, ALU.add).then_inc(mb_done, 1)
                        dve.wait_ge(mb_done, i * 2 + (m + 1))

            def residual(i, g):
                for b in range(NBB):
                    dve.wait_ge(out_mm, i * (2 * NBB) + (g * NBB + b + 1))
                    dst = x2[:, i * 8 + g * 4:i * 8 + g * 4 + 4, (b + 1) * P:(b + 2) * P]
                    V.tensor_tensor(dst, by_tile(ps[g * NBB + b][:]), dst, ALU.add).then_inc(out_free, 1)

            def steps_after(plan, *steps):
                def after(k):
                    if k in plan[1]:
                        name, *at = steps[plan[1].index(k)]
                        if name == "out":
                            residual(*at)
                        else:
                            merge(name, *at)
                return after

            V.tensor_copy(idx_cur[:, 0, :], idx_all[:, 0, :]).then_inc(idx_ready, 1)
            unit(0, 0, steps_after(PLAN_FIRST, *(("ma", i) for i in range(4))))
            unit(1, 0, steps_after(PLAN_3, *(("ma", i) for i in range(4, 7))))
            unit(2, 0, steps_after(PLAN_3, ("ma", 7), ("mb", 0), ("mb", 1)))
            with dve.Fori(3, 5) as U:
                unit(U, 0, steps_after(PLAN_3, *(("mb", U * 3 + (j - 7)) for j in range(3))))
            dve.wait_ge(res_in, 16 * NB)
            unit(5, 0, steps_after(PLAN_3, ("out", 0, 0), ("out", 0, 1), ("out", 1, 0)))
            last_step = steps_after(PLAN_LAST, ("out", 1, 1))

            def second_norm(k):
                last_step(k)
                if k == 7:
                    norm2_means(range(1, NB))
                if k == 9:
                    dve.wait_ge(gbc_in, 48)
                    norm2(range(1, NB))

            unit(6, 0, second_norm)

            def parts_beside(head, start):
                find, softmax = topk_beside(head)

                def after(k):
                    if start <= k < start + len(find):
                        find[k - start]()
                    if k == GATE_OUT_AT:
                        softmax()
                return after

            unit(7, 0, parts_beside(0, 1))
            dve.wait_ge(v_used, PH * TOP + VS)
            dve.sem_inc(mix1_free, 1)
            with dve.Fori(8, 15) as U:
                chain.enter()
                unit(U, 1, parts_beside(U - (PH - 1), 0))
                chain.leave()

            def hand_over(k):
                if k == COPY_AT:
                    V.tensor_copy(idx_cur2[:, 0, :], idx_all[:, SIDE, :]).then_inc(idx2_ready, 1)

            unit(SIDE - 1, 1, hand_over)
            dve.wait_ge(u_used, SIDE * TOP + US)
            dve.sem_inc(v2_used, SLOTS)
            with dve.Fori(SIDE // PH, NB) as b:
                with dve.Fori(0, PH // 2) as j:
                    lu = b * PH + j * 2 - SIDE
                    for n in range(2 * TOP):
                        m, k = n // TOP, n % TOP
                        s = n % SLOTS
                        dve.wait_ge(u2_ready[s], lu * (16 * TOP // SLOTS) + 16 * (n // SLOTS + 1))
                        row = by_tile(u2_row[s])
                        V.scalar_tensor_tensor(row, row, 1.0, block_of(h2, b), ALU.mult, ALU.mult,
                                               accum_out=act_u2[:, m, k:k + 1]).then_inc(u2_used, 1)
                        if k == TOP // 2:
                            dve.wait_ge(v2_used, lu * TOP + (m * TOP + SLOTS))
                            V.tensor_copy(idx_cur2[:, 1 - m, :], idx_all[:, bass.ds(lu + (SIDE + m + 1), 1), :]
                                          .rearrange("p a k -> p (a k)")).then_inc(idx2_ready, 1)
                        if k == TOP - 1:
                            dve.wait_ge(v2_used, lu * TOP + ((m + 1) * TOP + SLOTS))
                            for q in range(4):
                                dst = x2[:, 4 * q:4 * q + 4, bass.ds(b * P, P)]
                                ins = V.tensor_tensor(dst, by_tile(ps[4 * m + q][:]), dst, ALU.add)
                            ins.then_inc(mix_free, 1)
                            dve.wait_ge(mix_free, lu + (m + 3))

            for b in range(NB):
                dve.wait_ge(fin_sum, b + 1)
                mean_square(52 + b, 48 + b, D).then_inc(fin_ms, 1)
            dve.wait_ge(gbc_in, 64)
            for b in range(NB):
                dve.wait_ge(fin_root, b + 1)
                chain.step(inverse(60 + b, 56 + b))
                V.scalar_tensor_tensor(by_tile(y_out[:, b, :]), block_of(x2, b), small[:, 60 + b:61 + b],
                                       by_tile(gbc_f), ALU.mult, ALU.mult).then_inc(fin_y, 1)

        @block.tensor
        def _(pe):
            M = nc.tensor.matmul

            def transposes(banks_first, n_banks, src, done, ready):
                for g in range(n_banks):
                    ready(g)
                    for q in range(4):
                        last = nc.tensor.transpose(ps[(banks_first + g) % 8][:, q * P:q * P + P],
                                                   src(4 * g + q), ident[:])
                    last.then_inc(done, 1)

            def slab_ready(n, i=None, per=0):
                if i is None:
                    pe.wait_ge(w_in_slot[n % 2], 16 * (n // 2 + 1))
                else:
                    pe.wait_ge(w_in_slot[n % 2], i * (8 * per) + 16 * (n // 2 + 1))

            pe.sem_inc(w_used, 2)

            pe.wait_ge(consts, 2)
            pe.wait_ge(rows_in, 16 * 7)
            for g in range(2):
                for q in range(8):
                    last = nc.tensor.transpose(ps[g][:, 64 * q:64 * q + ROWS],
                                               rows[:, (8 * g + q) * P:(8 * g + q + 1) * P], ident[0:ROWS, 0:ROWS])
                last.then_inc(cols_tr, 1)
            pe.wait_ge(cols_done, 2)
            for b in range(NB):
                pe.wait_ge(n1_xn, b + 1)

                def ready(g):
                    if b * 4 + g >= 8:
                        pe.wait_ge(n1_done, b * 4 + g - 7)

                transposes(b * 4, 4, lambda t: xb[:, b, t * P:t * P + P], n1_tr, ready)
            pe.wait_ge(n1_done, 16)
            pe.wait_ge(wgk_in, 32)
            pe.wait_ge(wgk_gap, 1)
            for k in range(KT):
                last = M(ps[0][0:32 + RANK, :], wgk[:, k, :], hT[:, k, :], start=k == 0, stop=k == KT - 1)
            last.then_inc(glow_mm, 1)
            pe.wait_ge(glow_done, 2)

            def project(slot, m, act_in, bank, done, lo=0, hi=T):
                for k in range(KT):
                    last = M(ps[bank][:, 0:hi - lo], w_slot(slot)[:, k, m * P:m * P + P], act_in[:, k, lo:hi],
                             start=k == 0, stop=k == KT - 1)
                last.then_inc(done, 1)
                return last

            with pe.Fori(0, HEADS) as h:
                for s in range(2):
                    slab_ready(s, h, HEAD_SLABS)
                    for m in range(MT):
                        project(s, m, hT, 2 * s + m, q_mm)
                    pe.drain().then_inc(w_used, 1)
                pe.wait_ge(gkw_in, h * 32 + 32)
                for u in range(4):
                    rank = slice(32 * (u // 2), 32 * (u // 2) + RANK)
                    M(ps[4 + u][:], gkw[rank, (u % 2) * P:(u % 2) * P + P], glow[rank, :],
                      start=True, stop=True).then_inc(z_mm, 1)
                pe.wait_ge(q_ev, h * 4 + 4)
                for first, bank0, done in ((2, 0, v_mm), (4, 4, og_mm)):
                    if bank0:
                        pe.wait_ge(z_dif, h * 4 + 4)
                    for s in range(2):
                        slab_ready(first + s, h, HEAD_SLABS)
                        for k in range(KT // 2):
                            kk = s * (KT // 2) + k
                            for b in range(NB):
                                last = M(ps[bank0 + b][:], hT[:, kk, b * P:b * P + P], w_slot_half(s)[:, k, :],
                                         start=kk == 0, stop=kk == KT - 1)
                                if kk == KT - 1:
                                    last.then_inc(done, 1)
                        pe.drain().then_inc(w_used, 1)
                pe.wait_ge(z_qk, h * 4 + 4)
                pe.wait_ge(v_ev, h * 4 + 4)
                for u in range(4):
                    for c in range(NB):
                        last = nc.tensor.transpose(ps[u][:, c * P:c * P + P],
                                                   km[:, u // 2, u % 2, c * P:c * P + P], ident[:])
                    last.then_inc(kt_tr, 1)
                pe.wait_ge(kt_ev, h * 4 + 4)
                for j, c in enumerate((3, 2, 1)):
                    if j == 2:
                        pe.wait_ge(ub_done, h * 6 + 2)
                    for m in range(MT):
                        M(ps[2 * (j % 2) + m][:], kmT[:, c, 1, m * P:m * P + P], v_tok[:, c, :],
                          start=True, stop=True).then_inc(ub_mm, 1)

                def scores(c):
                    if c >= 2:
                        pe.wait_ge(sc_done, h * 4 + (c - 1))
                    for d in range(2):
                        for m in range(MT):
                            last = M(ps[4 + c % 2][:, d * P:d * P + P], km[:, d, m, c * P:c * P + P],
                                     qm[:, d, m, c * P:c * P + P], start=m == 0, stop=m == MT - 1)
                    last.then_inc(sc_mm, 1)

                def heads_out(c):
                    pe.wait_ge(o_norm, h * 4 + (c + 1))
                    if c >= 2:
                        pe.wait_ge(ot_ev, h * 4 + (c - 1))
                    for q in range(4):
                        last = nc.tensor.transpose(ps[2 + c % 2][:, q * P:q * P + P],
                                                   on[:, c % 2, q * P:q * P + P], ident[:])
                    last.then_inc(ot_tr, 1)

                pe.wait_ge(og_ev, h * 4 + 4)
                scores(0)
                pe.wait_ge(ub_done, h * 6 + 6)
                for c in range(NB):
                    if c < NB - 1:
                        scores(c + 1)
                        if c:
                            pe.wait_ge(uf_done, h * 6 + 2 * c)
                        for m in range(MT):
                            M(ps[m][:], kmT[:, c, 0, m * P:m * P + P], v_tok[:, c, :],
                              start=True, stop=True).then_inc(uf_mm, 1)
                    terms = []
                    if c < NB - 1:
                        terms += [(qm[:, 1, m, c * P:c * P + P], st_b[:, c, m, :]) for m in range(MT)]
                    if c > 0:
                        terms += [(qm[:, 0, m, c * P:c * P + P], st_f[:, c % 2, m, :]) for m in range(MT)]
                    terms.append((p_t[:, c % 2, :], v_tok[:, c, :]))
                    if c:
                        pe.wait_ge(uf_done, h * 6 + 2 * c)
                    if c >= 2:
                        pe.wait_ge(o_norm, h * 4 + (c - 1))
                    pe.wait_ge(sc_done, h * 4 + (c + 1))
                    for n, (lhs, rhs) in enumerate(terms):
                        last = M(ps[6 + c % 2][:], lhs, rhs, start=n == 0, stop=n == len(terms) - 1)
                    last.then_inc(o_mm, 1)
                    if c:
                        heads_out(c - 1)
                heads_out(NB - 1)
                pe.wait_ge(ot_ev, h * 4 + 4)

            def pairs(name, first, val_in, lo):
                p = pair[name]
                with pe.Fori(0, KT // 2) as i:
                    slab_ready(first, i, 2)
                    for m in range(2):
                        pe.wait_ge(p["use"], i * 2 + (m + 1))
                        project(0, m, hT, m, p["gate"], lo)
                    pe.drain().then_inc(w_used, 1)
                    slab_ready(first + 1, i, 2)
                    for m in range(2):
                        project(1, m, val_in, 2 + m, p["val"], lo)
                    pe.drain().then_inc(w_used, 1)

            def pairs1(name, first, start, end, val_in):
                p = pair[name]
                with pe.Fori(start, end) as g:
                    for j, (src, done) in enumerate(((hT, p["gate"]), (val_in, p["val"]))):
                        pe.wait_ge(p["use"] if j else p["sig"], g + 1)
                        if name == "mb1" and j:
                            pe.wait_ge(ln_act, KT)
                            pe.wait_ge(pair["ma1"]["use"], 4 + 1)
                        for s in range(2):
                            slab_ready(first + 2 * j + s, g, 4)
                            for k in range(KT // 2):
                                kk = s * (KT // 2) + k
                                last = M(ps[j][:], src[:, kk, 0:TA], w_slot_half(s)[:, k, :],
                                         start=kk == 0, stop=kk == KT - 1)
                            if s:
                                last.then_inc(done, 1)
                            pe.drain().then_inc(w_used, 1)

            pairs("cv", SB_CONV, hT, 0)
            pe.wait_ge(pair["cv"]["sig"], KT)
            pairs1("ma1", SB_MA1, 0, 2, oT)
            pe.wait_ge(ln_added, KT)
            M(ps[4][:], ones_d[:], ln_acc[:, 0, :], start=True, stop=True).then_inc(ln_sum, 1)
            pairs1("ma1", SB_MA1, 2, 3, oT)
            pe.wait_ge(ln_added, 2 * KT)
            M(ps[5][:], ones_d[:], ln_acc[:, 1, :], start=True, stop=True).then_inc(ln_varu, 1)
            pairs1("ma1", SB_MA1, 3, 4, oT)
            pe.wait_ge(pair["ma1"]["sig"], 4 + 1)
            pairs1("mb1", SB_MB1, 0, 4, cv)

            pe.wait_ge(mb1_done, 4)
            pe.wait_ge(ln_ms, 1)
            transposes(2, 4, lambda t: mgA[:, t * P:t * P + P], mt_tr, lambda g: None)
            pe.wait_ge(mt_ev, 4)

            def project_out(i, first, lhs, nb, done, free):
                for g in range(2):
                    for s in range(2):
                        slab_ready(first + 2 * g + s, i, 4)
                        for k in range(KT // 2):
                            kk = s * (KT // 2) + k
                            for b in range(nb):
                                if kk == 0:
                                    pe.wait_ge(free, i * (2 * nb) + (g * nb + b + 1))
                                last = M(ps[g * nb + b][:], lhs(kk, b), w_slot_half(s)[:, k, :],
                                         start=kk == 0, stop=kk == KT - 1)
                                if kk == KT - 1:
                                    last.then_inc(done, 1)
                        pe.drain().then_inc(w_used, 1)

            with pe.Fori(0, 2) as i:
                project_out(i, SB_OUT1, lambda kk, b: mgTA[:, kk, :], 1, out1_mm, out1_free)

            def norm2_turn(blocks):
                for b in blocks:
                    pe.wait_ge(n2_h, b + 1)

                    def ready(g):
                        if b * 4 + g >= 8:
                            pe.wait_ge(n2_ev, b * 4 + g - 7)

                    transposes(b * 4, 4, lambda t: h2[:, t, b * P:b * P + P], n2_tr, ready)

            def query(hg, first, i, per, slot, m, lo, nb):
                slab_ready(first, i, per)
                for c in range(2):
                    project(slot, c, h2T, 4 * m + c, pq_mm, lo, lo + nb * P)
                pe.drain().then_inc(w_used, 1)
                head_scores(hg, m, nb)

            def head_scores(hg, m, nb):
                for c in range(2):
                    pe.wait_ge(pq_ev, hg * 2 + (c + 1))
                    key = keysT[:, bass.ds((hg % PH) * 2 + c, 1), :].rearrange("p a n -> p (a n)")
                    for b in range(nb):
                        last = M(ps[4 * m + 2 + c][:, b * NK:b * NK + NK], qh[:, c, b * P:b * P + P], key,
                                 start=True, stop=True)
                    last.then_inc(s_mm, 1)

            pe.wait_ge(keys_in, 16)
            transposes(4, 4, lambda t: keys_nA[:, t, :], keys_tr, lambda g: None)
            norm2_turn([0])
            pe.wait_ge(n2_ev, 4)
            pe.wait_ge(keys_ev, 4)
            with pe.Fori(0, PH // 2) as i:
                for m in range(2):
                    query(i * 2 + m, SB_WQ1 + m, i, 2, m, m, 0, 1)

            pe.wait_ge(s_ev, 2 * PH)
            pairs("ma", SB_MA, oT, TA)
            pe.wait_ge(pair["ma"]["use"], KT + 2)
            pairs("mb", SB_MB, cv, TA)
            pe.wait_ge(mb_done, KT)

            def merged(kk, b):
                return mgT1[:, kk, :] if b == 0 else mgT23[:, kk, (b - 1) * P:b * P]

            with pe.Fori(0, 2) as i:
                project_out(i, SB_OUT, merged, NBB, out_mm, out_free)
            norm2_turn(range(1, NB))
            pe.wait_ge(keys_in, 32)
            pe.wait_ge(n2_ev, 16)
            transposes(0, 4, lambda t: keys_n[:, t, :], keys_tr, lambda g: None)
            pe.wait_ge(keys_ev, 8)
            for s in range(2):
                query(PH + s, SB_WQ + s, 0, 2, s, 0, TA, NBB)

            def products(i, heads):
                for m in range(2):
                    for k in range(TOP):
                        n = m * TOP + k
                        if k == 0:
                            pe.wait_ge(mix1_free, i * 2 + (m + 1))
                        pe.wait_ge(v_ready[k % VS], (i * 2 + (PH + m)) * (16 * TOP // VS) + 16 * (k // VS + 1))
                        pe.wait_ge(diag1_ready, i * 2 * TOP + (n + 1))
                        for q in range(4):
                            last = M(ps[4 + q][:], diag1[:, k % VS, :], v_row[k % VS][:, q * 512:q * 512 + 512],
                                     start=k == 0, stop=k == TOP - 1)
                        last.then_inc(v_used, 1)
                        if not heads:
                            continue
                        first = (k - QUERY_FROM) * QUERY_STEP
                        if first == 0:
                            slab_ready(SB_WQ + 2 + m, i, 2)
                        if 0 <= first < 2 * KT:
                            for step in range(first, first + QUERY_STEP):
                                c, kk = step // KT, step % KT
                                last = M(ps[c][:, 0:TB], w_slot(m)[:, kk, c * P:c * P + P], h2T[:, kk, TA:T],
                                         start=kk == 0, stop=kk == KT - 1)
                                if kk == KT - 1:
                                    last.then_inc(pq_mm, 1)
                        if k == SCORES_AT - 1:
                            pe.drain().then_inc(w_used, 1)
                            head_scores(i * 2 + (PH + 2 + m), 0, NBB)

            with pe.Fori(0, (PH - 2) // 2) as i:
                products(i, True)
            products((PH - 2) // 2, False)
            pe.wait_ge(mix1_free, PH + 1)

            with pe.Fori(0, (UNITS - SIDE) // 2) as i:
                for n in range(2 * TOP):
                    m, k = n // TOP, n % TOP
                    s = n % SLOTS
                    if k == 0:
                        pe.wait_ge(mix_free, i * 2 + (m + 1))
                    pe.wait_ge(v2_ready[s], i * (32 * TOP // SLOTS) + 16 * (n // SLOTS + 1))
                    pe.wait_ge(diag_ready, i * 2 * TOP + (n + 1))
                    for q in range(4):
                        last = M(ps[4 * m + q][:], diag[:, s, :], v2_row[s][:, q * 512:q * 512 + 512],
                                 start=k == 0, stop=k == TOP - 1)
                    last.then_inc(v2_used, 1)


_INS = ["x", "norm1_g", "w_in", "gla_gk_fwd_w", "gla_gk_fwd_b", "gla_gk_bwd_w", "gla_gk_bwd_b", "gla_onorm_g",
        "gla_w_o", "conv_w", "conv_b", "conv_ln_g", "conv_ln_b", "conv_w_pw2", "w_out", "norm2_g", "peer_w_q",
        "peer_keys", "peer_u", "peer_v", "final_norm_g"]


def kernel(**inputs):
    import numpy as np
    import concourse.bacc as bacc
    from concourse import mybir as mb
    from concourse.bass_utils import run_bass_kernel_spmd

    nc = bacc.Bacc("TRN2", target_bir_lowering=False, num_devices=1)
    arrays, args = {}, []
    for name in _INS:
        a = np.ascontiguousarray(inputs[name])
        arrays["in_" + name] = a
        args.append(nc.dram_tensor("in_" + name, a.shape, mb.dt.from_np(a.dtype), kind="ExternalInput").ap())
    out = nc.dram_tensor("out_0", (1, T, D), mb.dt.float32, kind="ExternalOutput").ap()
    hybrid_block(nc, *args, out)
    r = run_bass_kernel_spmd(nc, [arrays], core_ids=[0])
    return r.results[0]["out_0"]
```
